# Optimizing a Trainium2 kernel written in Bass

```python
import jax, jax.numpy as jnp
from jax import lax
import numpy as np

D_MODEL = 2048
BATCH = 1
SEQ = 256
DEPTH = 2
DEC_BATCH = 1
DEC_SEQ = 32
PAST_LEN = 256

CHUNK = 64
N_MIXERS = 2
N_LRU_LAYERS = (DEPTH + 1) // 2
N_POOL_LAYERS = DEPTH // 2
D_RNN = D_MODEL
LRU_HEADS = 8
LRU_BLOCK = D_RNN // LRU_HEADS
CONV_WIDTH = 4
LRU_C = 8.0
POOL_WINDOWS = (2, 4, 8, 16)
POOL_GROUPS = 4
POOL_GROUP_DIM = D_MODEL // POOL_GROUPS
POOL_STATE = max(POOL_WINDOWS) - 1
MOE_GROUPS = 4
MOE_EXPERTS_PER_GROUP = 4
N_EXPERTS = MOE_GROUPS * MOE_EXPERTS_PER_GROUP
MOE_TOP_K = 2
D_EXPERT = 512
DEEPNORM_ALPHA = (2.0 * DEPTH) ** 0.25
DEEPNORM_BETA = (8.0 * DEPTH) ** -0.25
LN_EPS = 1e-5

kernel_name = "hawk_pool_hmoe_stream_step"

F32 = jnp.float32

def layer_norm(x, g, b):
    xf = x.astype(F32)
    mu = jnp.mean(xf, axis=-1, keepdims=True)
    var = jnp.mean(jnp.square(xf - mu), axis=-1, keepdims=True)
    y = (xf - mu) * lax.rsqrt(var + LN_EPS) * g.astype(F32) + b.astype(F32)
    return y.astype(x.dtype)

def causal_depthwise_conv(u, prefix, w, b):
    s = u.shape[1]
    ext = jnp.concatenate([prefix.astype(u.dtype), u], axis=1)
    y = b
    for k in range(CONV_WIDTH):
        y = y + ext[:, k:k + s] * w[k]
    return y, ext[:, -(CONV_WIDTH - 1):]

def _lin_combine(left, right):
    a1, b1 = left
    a2, b2 = right
    return a1 * a2, a2 * b1 + b2

def rg_lru_block(x, h0, conv0, w_in, conv_w, conv_b, w_a, b_a, w_x, b_x, lam, w_out):
    bsz, s, _ = x.shape
    proj = jnp.einsum('bsd,de->bse', x, w_in)
    gate_br, u = jnp.split(proj, 2, axis=-1)
    uc, conv_new = causal_depthwise_conv(u, conv0, conv_w, conv_b)
    uh = uc.reshape(bsz, s, LRU_HEADS, LRU_BLOCK)
    r = jax.nn.sigmoid((jnp.einsum('bshi,hij->bshj', uh, w_a) + b_a).astype(F32)).reshape(bsz, s, D_RNN)
    ig = jax.nn.sigmoid((jnp.einsum('bshi,hij->bshj', uh, w_x) + b_x).astype(F32)).reshape(bsz, s, D_RNN)
    log_a = -LRU_C * r * jax.nn.softplus(-lam.astype(F32))
    a = jnp.exp(log_a)
    mult = jnp.sqrt(-jnp.expm1(2.0 * log_a))
    bterm = mult * ig * uc.astype(F32)
    bterm = bterm.at[:, 0].add(a[:, 0] * h0.astype(F32))
    _, h = lax.associative_scan(_lin_combine, (a, bterm), axis=1)
    y = h.astype(x.dtype) * jax.nn.gelu(gate_br)
    out = jnp.einsum('bse,ed->bsd', y, w_out)
    return out, h[:, -1].astype(h0.dtype), conv_new

def pool_mixer(x, prefix, pos0, w_map, scale):
    s = x.shape[1]
    ext = jnp.concatenate([prefix.astype(x.dtype), x], axis=1)
    cs = jnp.pad(jnp.cumsum(ext.astype(F32), axis=1), ((0, 0), (1, 0), (0, 0)))
    pos = pos0 + jnp.arange(s, dtype=F32)
    upper = cs[:, POOL_STATE + 1:]
    outs = []
    for g, w in enumerate(POOL_WINDOWS):
        lo, hi = g * POOL_GROUP_DIM, (g + 1) * POOL_GROUP_DIM
        lower = cs[:, POOL_STATE + 1 - w:POOL_STATE + 1 - w + s, lo:hi]
        count = jnp.minimum(float(w), pos + 1.0)[None, :, None]
        mean = (upper[..., lo:hi] - lower) / count
        diff = (mean - x[..., lo:hi].astype(F32)).astype(x.dtype)
        outs.append(jnp.einsum('bsi,ij->bsj', diff, w_map[g]))
    y = jnp.concatenate(outs, axis=-1) * scale
    return y, ext[:, -POOL_STATE:]

def hier_moe(x, wg, bg, we, be, w_gate_up, w_down):
    bsz, s, d = x.shape
    xt = x.reshape(-1, d)
    t = xt.shape[0]
    lg = (xt @ wg + bg).astype(F32)
    pg = jax.nn.softmax(lg, axis=-1)
    gsel = jnp.argmax(lg, axis=-1)
    p_sel = jnp.max(pg, axis=-1, keepdims=True)
    le = (xt @ we + be).astype(F32).reshape(t, MOE_GROUPS, MOE_EXPERTS_PER_GROUP)
    le_sel = le[jnp.arange(t), gsel]
    topv, topi = lax.top_k(le_sel, MOE_TOP_K)
    wt = jax.nn.softmax(topv, axis=-1) * p_sel
    eidx = gsel[:, None] * MOE_EXPERTS_PER_GROUP + topi
    gates = jnp.sum(jax.nn.one_hot(eidx, N_EXPERTS, dtype=F32) * wt[..., None], axis=1)
    hu = jnp.einsum('td,edf->tef', xt, w_gate_up)
    hg, hv = jnp.split(hu, 2, axis=-1)
    act = jax.nn.silu(hg) * hv * gates[..., None].astype(x.dtype)
    out = jnp.einsum('tef,efd->td', act, w_down)
    return out.reshape(bsz, s, d)

def run_trunk(x, lru_h0, lru_conv0, pool0, pos0,
              lru_w_in, lru_conv_w, lru_conv_b, lru_w_a, lru_b_a, lru_w_x, lru_b_x, lru_lambda, lru_w_out,
              pool_w, pool_scale, ln_g, ln_b,
              moe_router_g_w, moe_router_g_b, moe_router_e_w, moe_router_e_b, moe_w_gate_up, moe_w_down):
    new_h, new_conv, new_pool = [], [], []
    for i in range(DEPTH):
        j = i // N_MIXERS
        if i % N_MIXERS == 0:
            mix, h, c = rg_lru_block(x, lru_h0[j], lru_conv0[j], lru_w_in[j], lru_conv_w[j], lru_conv_b[j],
                                     lru_w_a[j], lru_b_a[j], lru_w_x[j], lru_b_x[j], lru_lambda[j], lru_w_out[j])
            new_h.append(h)
            new_conv.append(c)
        else:
            mix, p = pool_mixer(x, pool0[j], pos0, pool_w[j], pool_scale[j])
            new_pool.append(p)
        x = layer_norm(DEEPNORM_ALPHA * x + mix, ln_g[i, 0], ln_b[i, 0])
        ffn = hier_moe(x, moe_router_g_w[i], moe_router_g_b[i], moe_router_e_w[i], moe_router_e_b[i],
                       moe_w_gate_up[i], moe_w_down[i])
        x = layer_norm(DEEPNORM_ALPHA * x + ffn, ln_g[i, 1], ln_b[i, 1])
    return x, jnp.stack(new_h), jnp.stack(new_conv), jnp.stack(new_pool)

def setup_inputs(seed: int = 0) -> dict:
    key = jax.random.key(seed)
    ks = jax.random.split(key, 24)
    nrm = jax.random.normal
    s_lam = jax.random.uniform(ks[10], (N_LRU_LAYERS, D_RNN), minval=0.9, maxval=0.999)
    return {
        "x_prompt": nrm(ks[0], (BATCH, SEQ, D_MODEL), F32),
        "x_sample": nrm(ks[1], (DEC_BATCH, DEC_SEQ, D_MODEL), F32),
        "state_lru_h": 0.3 * nrm(ks[2], (N_LRU_LAYERS, DEC_BATCH, D_RNN), F32),
        "state_lru_conv": nrm(ks[3], (N_LRU_LAYERS, DEC_BATCH, CONV_WIDTH - 1, D_RNN), F32),
        "state_pool": nrm(ks[4], (N_POOL_LAYERS, DEC_BATCH, POOL_STATE, D_MODEL), F32),
        "lru_w_in": nrm(ks[5], (N_LRU_LAYERS, D_MODEL, 2 * D_RNN), F32) * D_MODEL ** -0.5,
        "lru_conv_w": nrm(ks[6], (N_LRU_LAYERS, CONV_WIDTH, D_RNN), F32) * CONV_WIDTH ** -0.5,
        "lru_conv_b": 0.02 * nrm(ks[7], (N_LRU_LAYERS, D_RNN), F32),
        "lru_w_a": nrm(ks[8], (N_LRU_LAYERS, LRU_HEADS, LRU_BLOCK, LRU_BLOCK), F32) * LRU_BLOCK ** -0.5,
        "lru_b_a": 0.02 * nrm(ks[9], (N_LRU_LAYERS, LRU_HEADS, LRU_BLOCK), F32),
        "lru_w_x": nrm(ks[11], (N_LRU_LAYERS, LRU_HEADS, LRU_BLOCK, LRU_BLOCK), F32) * LRU_BLOCK ** -0.5,
        "lru_b_x": 0.02 * nrm(ks[12], (N_LRU_LAYERS, LRU_HEADS, LRU_BLOCK), F32),
        "lru_lambda": jnp.log(s_lam) - jnp.log1p(-s_lam),
        "lru_w_out": nrm(ks[13], (N_LRU_LAYERS, D_RNN, D_MODEL), F32) * (D_RNN ** -0.5 * DEEPNORM_BETA),
        "pool_w": nrm(ks[14], (N_POOL_LAYERS, POOL_GROUPS, POOL_GROUP_DIM, POOL_GROUP_DIM), F32) * (POOL_GROUP_DIM ** -0.5 * DEEPNORM_BETA),
        "pool_scale": 1.0 + 0.02 * nrm(ks[15], (N_POOL_LAYERS, D_MODEL), F32),
        "ln_g": 1.0 + 0.02 * nrm(ks[16], (DEPTH, 2, D_MODEL), F32),
        "ln_b": 0.02 * nrm(ks[17], (DEPTH, 2, D_MODEL), F32),
        "moe_router_g_w": nrm(ks[18], (DEPTH, D_MODEL, MOE_GROUPS), F32) * D_MODEL ** -0.5,
        "moe_router_g_b": 0.01 * nrm(ks[19], (DEPTH, MOE_GROUPS), F32),
        "moe_router_e_w": nrm(ks[20], (DEPTH, D_MODEL, N_EXPERTS), F32) * D_MODEL ** -0.5,
        "moe_router_e_b": 0.01 * nrm(ks[21], (DEPTH, N_EXPERTS), F32),
        "moe_w_gate_up": nrm(ks[22], (DEPTH, N_EXPERTS, D_MODEL, 2 * D_EXPERT), F32) * D_MODEL ** -0.5,
        "moe_w_down": nrm(ks[23], (DEPTH, N_EXPERTS, D_EXPERT, D_MODEL), F32) * (D_EXPERT ** -0.5 * DEEPNORM_BETA),
    }

def reference(x_prompt, x_sample, state_lru_h, state_lru_conv, state_pool,
              lru_w_in, lru_conv_w, lru_conv_b, lru_w_a, lru_b_a, lru_w_x, lru_b_x, lru_lambda, lru_w_out,
              pool_w, pool_scale, ln_g, ln_b,
              moe_router_g_w, moe_router_g_b, moe_router_e_w, moe_router_e_b, moe_w_gate_up, moe_w_down):
    bp = x_prompt.shape[0]
    dt = x_prompt.dtype
    h0_p = jnp.zeros((N_LRU_LAYERS, bp, D_RNN), dt)
    conv0_p = jnp.zeros((N_LRU_LAYERS, bp, CONV_WIDTH - 1, D_RNN), dt)
    pool0_p = jnp.zeros((N_POOL_LAYERS, bp, POOL_STATE, D_MODEL), dt)
    y_prompt, lru_h_prompt, lru_conv_prompt, pool_prompt = run_trunk(
        x_prompt, h0_p, conv0_p, pool0_p, 0,
        lru_w_in, lru_conv_w, lru_conv_b, lru_w_a, lru_b_a, lru_w_x, lru_b_x, lru_lambda, lru_w_out,
        pool_w, pool_scale, ln_g, ln_b,
        moe_router_g_w, moe_router_g_b, moe_router_e_w, moe_router_e_b, moe_w_gate_up, moe_w_down)
    y_sample, lru_h_sample, lru_conv_sample, pool_sample = run_trunk(
        x_sample, state_lru_h, state_lru_conv, state_pool, PAST_LEN,
        lru_w_in, lru_conv_w, lru_conv_b, lru_w_a, lru_b_a, lru_w_x, lru_b_x, lru_lambda, lru_w_out,
        pool_w, pool_scale, ln_g, ln_b,
        moe_router_g_w, moe_router_g_b, moe_router_e_w, moe_router_e_b, moe_w_gate_up, moe_w_down)
    return (y_prompt, y_sample, lru_h_prompt, lru_conv_prompt, pool_prompt,
            lru_h_sample, lru_conv_sample, pool_sample)


_drawn_inputs = setup_inputs


def setup_inputs(seed=0):
    import zlib

    import numpy as np

    out = dict(_drawn_inputs(seed))
    spreads = {}
    factors = {'lru_b_a': 8.0,
     'lru_b_x': 7.097,
     'pool_scale': 17.885,
     'moe_router_g_b': 8.0,
     'moe_router_e_b': 35.934}
    for name, (base, spread) in spreads.items():
        noise = np.random.default_rng([zlib.crc32(name.encode()), seed]).standard_normal(out[name].shape)
        drawn = base * np.exp(spread * noise) if base else spread * noise
        out[name] = __import__('jax').numpy.asarray(drawn.astype(out[name].dtype))
    for name, factor in factors.items():
        out[name] = (out[name] * factor).astype(out[name].dtype)
    return out
```

```python
import numpy as np
import concourse.bass as bass
from concourse import mybir
from contextlib import ExitStack

F32 = mybir.dt.float32
I32 = mybir.dt.int32
ALU = mybir.AluOpType
ACT = mybir.ActivationFunctionType
AX = mybir.AxisListType

D = 2048
KD = D // 128
TP, TS = 256, 32
T = TP + TS
TILES = [(0, 128), (128, 128), (256, 32)]
HEADS = 8
CW = 4
TG = TP + TS + CW - 1
SEAM = TP + CW - 2
UX = TG + CW - 1
NG, NE = 4, 4
FE = 512
KF = FE // 128
W = 96
MORE = T // (W + 1)
PW = 15
ALPHA = 4.0 ** 0.25
EPS = 1e-5
NSLOT, SLOT = 6, 4096
SLOT0 = 4
C_OUT = 3 * HEADS
N_OUT = 8
C_MOE0 = C_OUT + N_OUT
PER_WIN = 24
C_POOL = C_MOE0 + NG * PER_WIN
C_MOE1 = C_POOL + NG
GU_DONE = [4, 8, 14, 20]
DN_DONE = [10, 16, 22, 24]
WINDOW_ORDER = [("gu", 0), ("gu", 1), ("dn", 0), ("gu", 2), ("dn", 1), ("gu", 3), ("dn", 2), ("dn", 3)]
V_CW, V_CB, V_BA, V_BX, V_LAM, V_LNG, V_LNB, V_SCALE, V_H0, V_CONV0 = 0, 4, 5, 6, 7, 8, 12, 16, 17, 18


def slot_of(n):
    return (n + SLOT0) % NSLOT


def dmas_of(n):
    return 2 if n < C_OUT and n % 3 == 2 else 1


def ready_at(n):
    return 16 * sum(dmas_of(m) for m in range(n % NSLOT, n + 1, NSLOT))


LRU_LINKS = 28
MOE_LINKS = 5


class SelfOrder:

    def __init__(self, eng, sem):
        self.eng, self.sem, self.n, self.i, self.per = eng, sem, 0, None, 0

    def start(self, i, per):
        self.i, self.per, self.n = i, per, 0

    def __call__(self, ins):
        self.n += 1
        ins.then_inc(self.sem, 1)
        self.eng.wait_ge(self.sem, self.n if self.i is None else self.i * self.per + self.n)

    def check(self):
        assert self.n == self.per, (self.n, self.per)


def encoder_step(nc, A, O):
    ctx = ExitStack()
    with ctx:
        def sb(name, shape, dt=F32):
            return ctx.enter_context(nc.sbuf_tensor(name, shape, dt))

        def sem(name):
            return ctx.enter_context(nc.semaphore(name))

        ring = sb("ring", [128, NSLOT, SLOT])
        xT = sb("xT", [128, KD, T])
        z = sb("z", [128, KD, T])
        xtok = sb("xtok", [128, 3, D])
        arena = sb("arena", [128, 7616])
        prmT = sb("prmT", [128, 24 * KD])
        wrT = sb("wrT", [128, 2, 20, KD])
        brow = sb("brow", [1, 2, 20])
        ident = sb("ident", [128, 128])
        ones = sb("ones", [128, 128])
        onesd = sb("onesd", [128, 128])
        before = sb("before", [128, 128])
        iota_i = sb("iota_i", [128, 128], I32)
        iota_f = sb("iota_f", [128, 128])
        valid = sb("valid", [128, 3, 1])
        rcount = sb("rcount", [128, 16])
        poolpre = sb("poolpre", [128, KD, PW])
        cst = sb("cst", [128, KD, 8])
        cstT = sb("cstT", [128, 128])
        half_ba = sb("half_ba", [128, KD])
        half_bx = sb("half_bx", [128, KD])
        c_lam = sb("c_lam", [128, KD])
        sp = [sb(f"sp{i}", [128, KD]) for i in range(4)]
        tiny = sb("tiny", [128, 1])
        mark = sb("mark", [1, 32])
        uext = sb("uext", [128, 2, UX])
        sq = sb("sq", [128, 2, T])
        mean = sb("mean", [128, T])
        rstd = sb("rstd", [128, T])
        nmr = sb("nmr", [128, T])
        zsum = sb("zsum", [128, T])
        logit = sb("logit", [128, 3, 20])
        r4 = [sb(f"r4_{i}", [128, 3, 4]) for i in range(4)]
        Gh = sb("Gh", [128, 3, 4])
        E1 = sb("E1", [128, 3, 4])
        gate4 = sb("gate4", [128, 3, 4])
        les = sb("les", [128, 3, 4])
        lprod = sb("lprod", [128, 3, 16])
        r1 = [sb(f"r1_{i}", [128, 3, 1]) for i in range(8)]
        gidx = sb("gidx", [128, 4])
        firstw = sb("firstw", [128, 4])
        n_g = sb("n_g", [128, 4])
        more = sb("more", [128, 4])
        mbase = sb("mbase", [128, 4])
        t4 = sb("t4", [128, 4])
        slotno = sb("slotno", [128, 3, 1])
        route_f = sb("route_f", [128, 8])
        route_i = sb("route_i", [1, 2, 8], I32)
        ps = ctx.enter_context(nc.psum_tensor("ps", [128, 8, 512], F32))

        def carve(tensor, at, *shape):
            n = int(np.prod(shape))
            v = tensor[:, at:at + n]
            names = " ".join("abc"[:len(shape)])
            kw = {"abc"[i]: s for i, s in enumerate(shape[1:], 1)}
            return v.rearrange(f"p ({names}) -> p {names}", **kw) if len(shape) > 1 else v

        xg = carve(arena, 0, KD, W)
        osb = carve(arena, 1536, D)
        act = [carve(arena, 3584 + 384 * i, KF, W) for i in range(2)]
        th = carve(arena, 4352, KF * W)
        P = carve(arena, 5120, 3, W)
        S = carve(arena, 5408, T)
        gbc = carve(arena, 5696, NE, W)
        grep = arena[:, 6080:7616].rearrange("p (i e c) -> p i e c", i=3, e=NE)
        prow = carve(sq[:, :, :].rearrange("p a t -> p (a t)"), 0, 3, 128)
        wrow = [(arena[0:16, l * 2560:l * 2560 + 512].rearrange("k (p g) -> k p g", g=4),
                 arena[0:16, l * 2560 + 512:(l + 1) * 2560].rearrange("k (p g) -> k p g", g=16)) for l in range(2)]
        pstrow = arena[0:PW, 5120:5120 + D]
        prow_out = arena[0:PW, 0:2 * D].rearrange("r (s d) -> r s d", s=2)
        zf = z[:, :, :].rearrange("p k t -> p (k t)")
        UC, GG, GS, TR, TX, AA, TL = [carve(zf, i * 2 * TG, 2, TG) for i in range(7)]
        xtf = xtok[:, :, :].rearrange("p i d -> p (i d)")
        yT = carve(xtf, 0, KD, T)
        PX = PW + TP + PW + TS
        pext, pa, pb = [carve(xtf, i * 4 * PX, 4, PX) for i in range(3)]
        pdiff = [carve(xtf, 12 * PX + i * 4 * T, 4, T) for i in range(2)]

        x_in = [sem(f"x_in{i}") for i in range(3)]
        prm_in, wr_in, pst_in = sem("prm_in"), sem("wr_in"), sem("pst_in")
        consts = sem("consts")
        ring_ready = [sem(f"ring_ready{i}") for i in range(NSLOT)]
        chunks_done = sem("chunks_done")
        init_tr = sem("init_tr")
        init_cp = sem("init_cp")
        derived = sem("derived")
        lam_exp = sem("lam_exp")
        vself = sem("vself")
        tr_full = [sem(f"tr_full{i}") for i in range(4)]
        tr_act = [sem(f"tr_act{i}") for i in range(4)]
        tr_dve = [sem(f"tr_dve{i}") for i in range(4)]
        u_copied, uext_free, uc_ready = sem("u_copied"), sem("uext_free"), sem("uc_ready")
        gsq_ready, gin_ready, gtanh_ready, gelu_done = sem("gsq"), sem("gin"), sem("gtanh"), sem("gelu_done")
        ri_read, decay_ready, q_ready, mult_ready = sem("ri_read"), sem("decay_ready"), sem("q_ready"), sem("mult")
        head_done = sem("head_done")
        vlru = sem("vlru")
        z_ready = [sem(f"z_ready{i}") for i in range(4)]
        zall = [sem(f"zall{i}") for i in range(4)]
        sq_ready = [sem(f"sq_ready{i}") for i in range(4)]
        sq_used = [sem(f"sq_used{i}") for i in range(4)]
        zsum_ready = [sem(f"zsum_ready{i}") for i in range(4)]
        stat_done = [sem(f"stat_done{i}") for i in range(4)]
        var_ready = [sem(f"var_ready{i}") for i in range(4)]
        std_ready = [sem(f"std_ready{i}") for i in range(4)]
        norm_q = [sem(f"norm_q{i}") for i in range(4)]
        x_ready = [sem(f"x_ready{i}") for i in range(4)]
        ax_ready = [sem(f"ax_ready{i}") for i in range(3)]
        two = range(2)
        lg_done = [sem(f"lg_done{i}") for i in two]
        ex_in = [sem(f"ex_in{i}") for i in two]
        ex_out = [sem(f"ex_out{i}") for i in two]
        oh_ready = [sem(f"oh_ready{i}") for i in two]
        cnt_done = [sem(f"cnt_done{i}") for i in two]
        route_ready = [sem(f"route_ready{i}") for i in two]
        grep_ready = [sem(f"grep_ready{i}") for i in two]
        P_ready = [sem(f"P_ready{i}") for i in two]
        aux_full = [sem(f"aux_full{i}") for i in two]
        aux_act = [sem(f"aux_act{i}") for i in two]
        aux_dve = [sem(f"aux_dve{i}") for i in two]
        th_ready = [sem(f"th_ready{i}") for i in two]
        gu_free = [sem(f"gu_free{i}") for i in two]
        act_ready = [sem(f"act_ready{i}") for i in two]
        o_act = [sem(f"o_act{i}") for i in two]
        o_dve = [sem(f"o_dve{i}") for i in two]
        vmoe = [sem(f"vmoe{i}") for i in two]
        cst_done, cstT_full, cstT_ready = sem("cst_done"), sem("cstT_full"), sem("cstT_ready")
        pst_full, pst_copied = sem("pst_full"), sem("pst_copied")
        pext_ready, pool_diff = sem("pext_ready"), sem("pool_diff")
        out_st, out_y = sem("out_st"), sem("out_y")

        w_in = A["lru_w_in"][0].rearrange("(k p) e -> p k e", p=128)
        w_a = A["lru_w_a"].rearrange("l h i j -> (l h i j)")
        w_x = A["lru_w_x"].rearrange("l h i j -> (l h i j)")
        w_out = A["lru_w_out"][0].rearrange("(k p) e -> p k e", p=128)
        pool_w = A["pool_w"][0].rearrange("g (k p) j -> g p k j", p=128)
        gu_w = [A["moe_w_gate_up"][l].rearrange("e d f -> (e d f)") for l in two]
        dn_w = [A["moe_w_down"][l].rearrange("e f d -> (e f d)") for l in two]

        def ring_at(n):
            return ring[:, slot_of(n), :]

        block = ctx.enter_context(nc.Block())

        @block.sync
        def _(eng):
            xp, xs = A["x_prompt"][0], A["x_sample"][0]
            for i, (t0, m) in enumerate(TILES):
                src = xp[t0:t0 + m, :] if t0 < TP else xs
                eng.dma_start(xtok[0:m, i, :], src).then_inc(x_in[i], 16)

            def lru_head(h, hh, it):
                for j in range(3):
                    n = 3 * hh + j
                    dst = ring_at(n)
                    if j < 2:
                        col = h * 256 + (D if j == 0 else 0)
                        if it is not None:
                            need = eng.snap(it * 6 + (n - NSLOT + 1))
                            eng.wait_ge(chunks_done, need)
                            col = h * 256 + D if j == 0 else it * 512 + hh * 256
                        eng.dma_start(dst.rearrange("p (k c) -> p k c", c=256), w_in[:, :, bass.ds(col, 256)])\
                           .then_inc(ring_ready[slot_of(n)], 16)
                    else:
                        if it is not None:
                            need = eng.snap(it * 6 + (n - NSLOT + 1))
                            eng.wait_ge(chunks_done, need)
                        for a, w in enumerate((w_a, w_x)):
                            src = w[bass.ds(h * (256 * 256), 256 * 256)]\
                                .rearrange("(k p j) -> p k j", k=2, p=128)
                            eng.dma_start(dst[:, a * 512:(a + 1) * 512].rearrange("p (k j) -> p k j", k=2), src)\
                               .then_inc(ring_ready[slot_of(n)], 16)

            for hh in range(2):
                lru_head(hh, hh, None)
            with eng.Fori(2, HEADS // 2 + 1) as after:
                it = after - 1
                for hh in range(2):
                    lru_head(eng.snap(it * 2 + hh), hh, it)
            for i in range(N_OUT):
                n = C_OUT + i
                eng.wait_ge(chunks_done, n - NSLOT + 1)
                eng.dma_start(ring_at(n).rearrange("p (k c) -> p k c", c=256), w_out[:, :, i * 256:(i + 1) * 256])\
                   .then_inc(ring_ready[slot_of(n)], 16)

            def window_loads(l, group, seq, base):
                n = base
                for kind, e in WINDOW_ORDER:
                    for c in range(4 if kind == "gu" else 2):
                        w, per_expert, k = (gu_w[l], D * 2 * FE, 4) if kind == "gu" else (dn_w[l], FE * D, 2)
                        at = eng.snap(group * (NE * per_expert) + (e * per_expert + c * 128 * SLOT))
                        need = eng.snap(seq * PER_WIN + (n - NSLOT + 1))
                        eng.wait_ge(chunks_done, need)
                        src = w[bass.ds(at, 128 * SLOT)].rearrange("(k p f) -> p k f", k=k, p=128)
                        dst = ring_at(n).rearrange("p (k f) -> p k f", k=k)
                        eng.dma_start(dst, src).then_inc(ring_ready[slot_of(n)], 16)
                        n += 1

            extra = 0
            for l, base in enumerate((C_MOE0, C_MOE1)):
                if l == 1:
                    for g in range(NG):
                        n = C_POOL + g
                        need = eng.snap(extra * PER_WIN + (n - NSLOT + 1))
                        eng.wait_ge(chunks_done, need)
                        eng.dma_start(ring_at(n)[:, 0:2048].rearrange("p (k j) -> p k j", k=4), pool_w[g])\
                           .then_inc(ring_ready[slot_of(n)], 16)
                with eng.Fori(0, NG) as w:
                    window_loads(l, eng.snap(w + 0), eng.snap(w + extra), base)
                eng.wait_ge(route_ready[l], 1)
                n_win = eng.value_load(route_i[0:1, l, 0:1], min_val=NG, max_val=NG + MORE)
                with eng.If(n_win > NG):
                    with eng.Fori(NG, n_win) as w:
                        g = eng.value_load(route_i[0:1, l, bass.ds(w - (NG - 1), 1)], min_val=0, max_val=NG - 1)
                        window_loads(l, g, eng.snap(w + extra), base)
                with eng.Else():
                    eng.nop()
                if l == 0:
                    extra = eng.snap(n_win - NG)
            eng.wait_ge(tr_act[3], 6)
            eng.wait_ge(tr_dve[3], 6)
            for i, (t0, m) in enumerate(TILES):
                dst = O["y_prompt"][0, t0:t0 + m, :] if t0 < TP else O["y_sample"][0]
                eng.dma_start(dst, xtok[0:m, i, :]).then_inc(out_y, 16)
            eng.wait_ge(out_y, 48)

        @block.gpsimd
        def _(eng):
            eng.memset(ident[:, :], 0.0).then_inc(consts, 1)
            eng.memset(before[:, :], 1.0).then_inc(consts, 1)
            eng.memset(ones[:, :], 1.0).then_inc(consts, 1)
            eng.memset(onesd[:, :], 1.0 / D).then_inc(consts, 1)
            eng.wait_ge(consts, 4)
            eng.affine_select(out=ident[:, :], in_=ident[:, :], compare_op=ALU.not_equal, fill=1.0, base=0,
                              pattern=[[-1, 128]], channel_multiplier=1).then_inc(consts, 1)
            eng.affine_select(out=before[:, :], in_=before[:, :], compare_op=ALU.is_gt, fill=0.0, base=0,
                              pattern=[[1, 128]], channel_multiplier=-1).then_inc(consts, 1)
            eng.iota(iota_i[:, :], pattern=[[1, 128]], base=0, channel_multiplier=0).then_inc(consts, 1)
            for n in range(3):
                for k in range(KD):
                    eng.wait_ge(x_ready[n], k + 1)
                    eng.tensor_scalar(z[:, k, :], xT[:, k, :], ALPHA, None, ALU.mult).then_inc(ax_ready[n], 1)

        @block.scalar
        def _(eng):
            def rows(v, src):
                r0, q = (v % 8) * KD, v // 8
                eng.dma_start(prow[r0:r0 + src.shape[0], q, :], src).then_inc(prm_in, 16)
            rows(V_CW, A["lru_conv_w"].rearrange("l w (b p) -> (l w b) p", p=128))
            rows(V_CB, A["lru_conv_b"].rearrange("l (b p) -> (l b) p", p=128))
            rows(V_BA, A["lru_b_a"].rearrange("l h (b p) -> (l h b) p", p=128))
            rows(V_BX, A["lru_b_x"].rearrange("l h (b p) -> (l h b) p", p=128))
            rows(V_LAM, A["lru_lambda"].rearrange("l (b p) -> (l b) p", p=128))
            rows(V_LNG, A["ln_g"].rearrange("l j (b p) -> (l j b) p", p=128))
            rows(V_LNB, A["ln_b"].rearrange("l j (b p) -> (l j b) p", p=128))
            rows(V_SCALE, A["pool_scale"].rearrange("l (b p) -> (l b) p", p=128))
            rows(V_H0, A["state_lru_h"].rearrange("l n (b p) -> (l n b) p", p=128))
            rows(V_CONV0, A["state_lru_conv"].rearrange("l n w (b p) -> (l n w b) p", p=128))
            for l in two:
                eng.dma_start(arena[0:16, l * 2560:l * 2560 + 512],
                              A["moe_router_g_w"][l].rearrange("(k p) g -> k (p g)", p=128)).then_inc(wr_in, 16)
                eng.dma_start(arena[0:16, l * 2560 + 512:(l + 1) * 2560],
                              A["moe_router_e_w"][l].rearrange("(k p) g -> k (p g)", p=128)).then_inc(wr_in, 16)
                eng.dma_start(brow[0:1, l, 0:4], A["moe_router_g_b"][l:l + 1, :]).then_inc(wr_in, 16)
                eng.dma_start(brow[0:1, l, 4:20], A["moe_router_e_b"][l:l + 1, :]).then_inc(wr_in, 16)
            eng.dma_start(pstrow, A["state_pool"][0, 0]).then_inc(pst_in, 16)

            def evacuate_x(which, to_feature, part):
                for n in part:
                    if n % 2 and which in (0, 3):
                        continue
                    i, q = n // 4, n % 4
                    t0, m = TILES[i]
                    eng.wait_ge(tr_full[which], n + 1)
                    if to_feature:
                        o = xT[:, 4 * q:4 * q + 4, t0:t0 + m]
                        s = ps[:, 4 + n % 4, :].rearrange("p (k c) -> p k c", k=4)[:, :, 0:m]
                    else:
                        o = xtok[0:m, i, q * 512:(q + 1) * 512]
                        s = ps[0:m, 4 + n % 4, :]
                    eng.activation(o, s, ACT.Copy).then_inc(tr_act[which], 1)

            eng.wait_ge(init_tr, 1)
            eng.activation(prmT[:, 0:336], ps[:, 0, 0:336], ACT.Copy).then_inc(init_cp, 1)
            evacuate_x(0, True, range(12))
            for l in two:
                eng.wait_ge(init_tr, 2 + l)
                eng.activation(wrT[:, l, :, :].rearrange("p j k -> p (j k)"), ps[:, 1 + l, 0:320], ACT.Copy)\
                   .then_inc(init_cp, 1)
            eng.wait_ge(init_tr, 4)
            eng.activation(poolpre[:, :, :].rearrange("p k r -> p (k r)"), ps[:, 3, 0:KD * PW], ACT.Copy)\
               .then_inc(init_cp, 1)
            eng.wait_ge(derived, 1)
            eng.activation(sp[1][:, :], sp[0][:, :], ACT.Exp, scale=-1.0).then_inc(lam_exp, 1)
            eng.activation(mark[0:1, 30:31], tiny[0:1, 0:1], ACT.Copy).then_inc(u_copied, 2)
            eng.activation(mark[0:1, 31:32], tiny[0:1, 0:1], ACT.Copy).then_inc(ri_read, 1)

            with eng.Fori(0, HEADS // 2) as it:
                for hh in range(2):
                    h = it * 2 + hh
                    eng.wait_ge(chunks_done, it * 6 + (3 * hh + 1))
                    eng.wait_ge(uext_free, it * 2 + (hh + 1))
                    for b in range(2):
                        eng.activation(uext[:, b, CW - 1:CW - 1 + TP], ps[:, b, 0:TP], ACT.Copy)
                        eng.activation(uext[:, b, TP + 2 * (CW - 1):UX], ps[:, b, TP:T], ACT.Copy)\
                           .then_inc(u_copied, 1)
                    eng.wait_ge(chunks_done, it * 6 + (3 * hh + 2))
                    eng.wait_ge(head_done, it * 2 + (hh + 1))
                    eng.activation(GS[:, :, 0:T], ps[:, 2:4, 0:T], ACT.Square).then_inc(gsq_ready, 1)
                    eng.wait_ge(gin_ready, it * 2 + (hh + 1))
                    eng.activation(GG[:, :, 0:T], GS[:, :, 0:T], ACT.Tanh, scale=0.7978845608028654)\
                       .then_inc(gtanh_ready, 1)
                    eng.wait_ge(chunks_done, it * 6 + (3 * hh + 3))
                    for b in range(2):
                        blk = h * 2 + b
                        eng.activation(TR[:, b, :], ps[:, 4 + b, 0:TG], ACT.Tanh, scale=0.5,
                                       bias=half_ba[:, bass.ds(blk, 1)])
                        last = eng.activation(TX[:, b, :], ps[:, 6 + b, 0:TG], ACT.Tanh, scale=0.5,
                                              bias=half_bx[:, bass.ds(blk, 1)])
                    last.then_inc(ri_read, 1)
                    eng.wait_ge(ri_read, it * 2 + (hh + 2))
                    for b in range(2):
                        blk = h * 2 + b
                        c = c_lam[:, bass.ds(blk, 1)]
                        eng.activation(AA[:, b, :], TR[:, b, :], ACT.Exp, scale=c, bias=c)
                        last = eng.activation(TL[:, b, :], TR[:, b, :], ACT.Tanh, scale=c, bias=c)
                    last.then_inc(decay_ready, 1)
                    eng.wait_ge(q_ready, it * 2 + (hh + 1))
                    eng.activation(TL[:, :, :], TL[:, :, :], ACT.Sqrt, scale=-1.0, bias=tiny[:, 0:1])\
                       .then_inc(mult_ready, 1)

            def layer_norm(n, vec):
                for k in range(KD):
                    if n in (0, 2):
                        eng.wait_ge(z_ready[n], k + 1)
                    elif k == 0:
                        eng.wait_ge(zall[n], 1)
                    if k >= 2:
                        eng.wait_ge(sq_used[n], k - 1)
                    eng.activation(sq[:, k % 2, :], z[:, k, :], ACT.Square).then_inc(sq_ready[n], 1)
                eng.wait_ge(var_ready[n], 1)
                eng.activation(rstd[:, :], rstd[:, :], ACT.Sqrt).then_inc(std_ready[n], 1)
                for k in range(KD):
                    if k % 4 == 0:
                        eng.wait_ge(norm_q[n], k // 4 + 1)
                    g, b = (V_LNG + vec) * KD + k, (V_LNB + vec) * KD + k
                    eng.activation(xT[:, k, :], z[:, k, :], ACT.Identity, scale=prmT[:, g:g + 1],
                                   bias=prmT[:, b:b + 1]).then_inc(x_ready[n], 1)

            def moe(l):
                evacuate_x(1 + l, False, range(0, 4))
                eng.wait_ge(ex_in[l], 1)
                eng.activation(r4[1][:, :, :], r4[0][:, :, :], ACT.Exp).then_inc(ex_out[l], 1)
                eng.wait_ge(ex_in[l], 2)
                eng.activation(r1[3][:, :, :], r1[2][:, :, :], ACT.Exp).then_inc(ex_out[l], 1)
                evacuate_x(1 + l, False, range(4, 12))
                if l == 0:
                    eng.wait_ge(cstT_full, 1)
                    eng.activation(cstT[:, :], ps[:, 2, 0:128], ACT.Copy).then_inc(cstT_ready, 1)
                    eng.wait_ge(cstT_ready, 1)
                    dst = [O["lru_conv_prompt"][0, 0, k] for k in range(3)] + [O["lru_conv_sample"][0, 0, k] for k in range(3)]
                    dst += [O["lru_h_prompt"][0, 0], O["lru_h_sample"][0, 0]]
                    for j, o in enumerate(dst):
                        eng.dma_start(o.rearrange("(b p) -> b p", p=128), cstT[j:128:8, :]).then_inc(out_st, 16)
                eng.wait_ge(route_ready[l], 1)
                n_win = eng.value_load(route_i[0:1, l, 0:1], min_val=NG, max_val=NG + MORE)
                base = C_MOE0 if l == 0 else C_MOE1
                with eng.Fori(0, n_win) as w:
                    seq = w if l == 0 else w + act_extra[0]
                    eng.wait_ge(aux_full[l], w * 22 + 1)
                    eng.activation(S[0:W, :], ps[0:W, 6, 0:T], ACT.Copy).then_inc(aux_act[l], 1)
                    eng.wait_ge(aux_full[l], w * 22 + 2)
                    eng.activation(gbc[:, :, :], ps[:, 7, 0:NE * W].rearrange("p (e w) -> p e w", e=NE), ACT.Copy,
                                   scale=0.5).then_inc(aux_act[l], 1)
                    for q in range(4):
                        eng.wait_ge(aux_full[l], w * 22 + (3 + q))
                        eng.activation(xg[:, 4 * q:4 * q + 4, :],
                                       ps[:, 6 + q % 2, 0:4 * W].rearrange("p (k w) -> p k w", k=4), ACT.Copy)\
                           .then_inc(aux_act[l], 1)
                    for e in range(NE):
                        eng.wait_ge(chunks_done, seq * PER_WIN + (base + GU_DONE[e]))
                        eng.activation(th[:, :], ps[:, 0, 0:KF * W], ACT.Tanh, scale=0.5).then_inc(th_ready[l], 1)
                    eng.wait_ge(chunks_done, seq * PER_WIN + (base + DN_DONE[3]))
                    for b in range(2):
                        last = eng.activation(osb[0:W, b * 512:(b + 1) * 512], ps[0:W, 2 + b, :], ACT.Copy)
                    last.then_inc(o_act[l], 1)
                if l == 0:
                    act_extra.append(eng.snap(n_win - NG))

            act_extra = []
            layer_norm(0, 0)
            moe(0)
            layer_norm(1, 1)
            for n in range(8):
                s, q = n // 4, n % 4
                eng.wait_ge(pst_full, n + 1)
                eng.activation(prow_out[:, s, q * 512:(q + 1) * 512], ps[0:PW, 4 + n % 4, :], ACT.Copy)\
                   .then_inc(pst_copied, 1)
            eng.wait_ge(pst_copied, 8)
            eng.dma_start(O["pool_prompt"][0, 0], prow_out[:, 0, :]).then_inc(out_st, 16)
            eng.dma_start(O["pool_sample"][0, 0], prow_out[:, 1, :]).then_inc(out_st, 16)
            layer_norm(2, 2)
            eng.wait_ge(out_st, 160)
            moe(1)
            layer_norm(3, 3)
            evacuate_x(3, False, range(12))
            eng.wait_ge(out_st, 160)

        @block.tensor
        def _(eng):
            mm = nc.tensor.matmul
            eng.wait_ge(consts, 7)
            eng.wait_ge(prm_in, 160)
            for q in range(3):
                r = 128 if q < 2 else 80
                last = nc.tensor.transpose(ps[:, 0, q * 128:q * 128 + r], prow[0:r, q, :], ident[0:r, 0:r])
            last.then_inc(init_tr, 1)

            def transpose_x(which, to_feature, part=range(12)):
                for n in part:
                    i, q = n // 4, n % 4
                    t0, m = TILES[i]
                    if to_feature and q == 0:
                        eng.wait_ge(x_in[i], 16)
                    if n >= 4 and which in (0, 3):
                        eng.wait_ge((tr_act if n % 2 == 0 else tr_dve)[which], (n - 4) // 2 + 1)
                    elif n >= 4:
                        eng.wait_ge(tr_act[which], n - 3)
                    for b in range(4):
                        k = 4 * q + b
                        if to_feature:
                            last = nc.tensor.transpose(ps[:, 4 + n % 4, b * 128:b * 128 + m],
                                                       xtok[0:m, i, k * 128:(k + 1) * 128], ident[0:m, 0:m])
                        else:
                            last = nc.tensor.transpose(ps[0:m, 4 + n % 4, b * 128:(b + 1) * 128],
                                                       xT[:, k, t0:t0 + m], ident[:, :])
                    last.then_inc(tr_full[which], 1)

            transpose_x(0, True)
            eng.wait_ge(wr_in, 128)
            for l in two:
                for j in range(20):
                    src = wrow[l][0][:, :, j] if j < 4 else wrow[l][1][:, :, j - 4]
                    last = nc.tensor.transpose(ps[:, 1 + l, j * 16:(j + 1) * 16], src, ident[0:16, 0:16])
                last.then_inc(init_tr, 1)
            eng.wait_ge(pst_in, 16)
            for k in range(KD):
                last = nc.tensor.transpose(ps[:, 3, k * PW:(k + 1) * PW], pstrow[:, k * 128:(k + 1) * 128],
                                           ident[0:PW, 0:PW])
            last.then_inc(init_tr, 1)

            eng.wait_ge(tr_act[0], 6)
            eng.wait_ge(tr_dve[0], 6)
            eng.wait_ge(init_cp, 4)
            with eng.Fori(0, HEADS // 2) as it:
                for hh in range(2):
                    for j in range(2):
                        n = 3 * hh + j
                        eng.wait_ge(ring_ready[slot_of(n)], it * (16 * dmas_of(n)) + ready_at(n))
                        if j == 1:
                            eng.wait_ge(gelu_done, it * 2 + (hh + 1))
                        wv = ring_at(n).rearrange("p (k c) -> p k c", c=256)
                        for b in range(2):
                            if j == 0:
                                eng.wait_ge(u_copied, it * 4 + (2 * hh + b + 1))
                            for k in range(KD):
                                last = mm(ps[:, 2 * j + b, 0:T], wv[:, k, b * 128:(b + 1) * 128], xT[:, k, :],
                                          start=(k == 0), stop=(k == KD - 1))
                        last.then_inc(chunks_done, 1)
                    n = 3 * hh + 2
                    eng.wait_ge(ring_ready[slot_of(n)], it * (16 * dmas_of(n)) + ready_at(n))
                    eng.wait_ge(uc_ready, it * 2 + (hh + 1))
                    eng.wait_ge(ri_read, it * 2 + (hh + 1))
                    wv = ring_at(n)[:, 0:1024].rearrange("p (a k j) -> p a k j", a=2, k=2)
                    for a in range(2):
                        for b in range(2):
                            for k in range(2):
                                last = mm(ps[:, 4 + 2 * a + b, 0:TG], wv[:, a, k, b * 128:(b + 1) * 128], UC[:, k, :],
                                          start=(k == 0), stop=(k == 1))
                    last.then_inc(chunks_done, 1)
            eng.wait_ge(head_done, HEADS + 1)
            for i in range(N_OUT):
                n = C_OUT + i
                eng.wait_ge(ring_ready[slot_of(n)], ready_at(n))
                if i >= 3:
                    eng.wait_ge(z_ready[0], 2 * (i - 2))
                wv = ring_at(n).rearrange("p (k c) -> p k c", c=256)
                for b in range(2):
                    for k in range(KD):
                        last = mm(ps[:, (2 * i + b) % 6, 0:T], wv[:, k, b * 128:(b + 1) * 128], yT[:, k, :],
                                  start=(k == 0), stop=(k == KD - 1))
                last.then_inc(chunks_done, 1)

            def layer_norm(n):
                for k in range(KD):
                    eng.wait_ge(sq_ready[n], k + 1)
                    mm(ps[:, 6, 0:T], onesd[:, :], sq[:, k % 2, :], start=(k == 0), stop=(k == KD - 1))\
                        .then_inc(sq_used[n], 1)
                eng.wait_ge(zsum_ready[n], 1)
                mm(ps[:, 7, 0:T], onesd[:, :], zsum[:, :], start=True, stop=True).then_inc(stat_done[n], 1)

            def moe(l):
                for i, (t0, m) in enumerate(TILES):
                    o = ps[0:m, 0, i * 32:i * 32 + 20]
                    mm(o, ones[0:1, 0:m], brow[0:1, l, :], start=True, stop=False)
                    for k in range(KD):
                        if i == 0:
                            eng.wait_ge(x_ready[2 * l], k + 1)
                        last = mm(o, xT[:, k, t0:t0 + m], wrT[:, l, :, k], start=False, stop=(k == KD - 1))
                last.then_inc(lg_done[l], 1)
                transpose_x(1 + l, False, range(4))
                eng.wait_ge(oh_ready[l], 1)
                for i in range(3):
                    for j in range(i + 1):
                        mm(ps[:, 1, i * 4:i * 4 + 4], (before if j == i else ones)[:, :], Gh[:, j, :],
                           start=(j == 0), stop=(j == i))
                for j in range(3):
                    last = mm(ps[:, 1, 16:20], ones[:, :], Gh[:, j, :], start=(j == 0), stop=(j == 2))
                last.then_inc(cnt_done[l], 1)
                transpose_x(1 + l, False, range(4, 12))
                if l == 0:
                    eng.wait_ge(cst_done, 1)
                    nc.tensor.transpose(ps[:, 2, 0:128], cst[:, :, :].rearrange("p b j -> p (b j)"), ident[:, :])\
                        .then_inc(cstT_full, 1)

                base = C_MOE0 if l == 0 else C_MOE1
                eng.wait_ge(grep_ready[l], 1)
                eng.wait_ge(tr_act[1 + l], 12)
                eng.wait_ge(route_ready[l], 1)
                n_win = eng.value_load(route_i[0:1, l, 0:1], min_val=NG, max_val=NG + MORE)
                with eng.Fori(0, n_win) as w:
                    seq = w if l == 0 else w + pe_extra[0]
                    eng.wait_ge(P_ready[l], w + 1)
                    eng.wait_ge(aux_dve[l], w * 16 + 1)
                    for i, (t0, m) in enumerate(TILES):
                        last = nc.tensor.transpose(ps[0:W, 6, t0:t0 + m], P[0:m, i, :], ident[0:m, 0:m])
                    last.then_inc(aux_full[l], 1)
                    eng.wait_ge(aux_dve[l], w * 16 + 2)
                    for e in range(NE):
                        for i in range(3):
                            last = mm(ps[:, 7, e * W:(e + 1) * W], grep[:, i, e, :], P[:, i, :],
                                      start=(i == 0), stop=(i == 2))
                    last.then_inc(aux_full[l], 1)
                    for q in range(4):
                        eng.wait_ge(aux_act[l], w * 6 + (1 + q))
                        for b in range(4):
                            k = 4 * q + b
                            for i in range(3):
                                last = mm(ps[:, 6 + q % 2, b * W:(b + 1) * W], xtok[:, i, k * 128:(k + 1) * 128],
                                          P[:, i, :], start=(i == 0), stop=(i == 2))
                        last.then_inc(aux_full[l], 1)
                    n = base
                    for kind, e in WINDOW_ORDER:
                        if kind == "gu":
                            eng.wait_ge(gu_free[l], w * 4 + (e + 1))
                            for c in range(4):
                                if e == 0:
                                    eng.wait_ge(aux_act[l], w * 6 + (3 + c))
                                eng.wait_ge(ring_ready[slot_of(n)], seq * 64 + ready_at(n))
                                wv = ring_at(n).rearrange("p (k f) -> p k f", k=4)
                                for f in range(8):
                                    for kk in range(4):
                                        last = mm(ps[:, f // 4, (f % 4) * W:(f % 4 + 1) * W],
                                                  wv[:, kk, f * 128:(f + 1) * 128], xg[:, 4 * c + kk, :],
                                                  start=(c == 0 and kk == 0 and f % 4 == 0),
                                                  stop=(c == 3 and kk == 3), skip_group_check=True)
                                last.then_inc(chunks_done, 1)
                                n += 1
                        else:
                            eng.wait_ge(act_ready[l], w * 4 + (e + 1))
                            if e == 0:
                                eng.wait_ge(o_act[l], w + 1)
                                eng.wait_ge(o_dve[l], w + 1)
                            for c in range(2):
                                eng.wait_ge(ring_ready[slot_of(n)], seq * 64 + ready_at(n))
                                wv = ring_at(n).rearrange("p (k f) -> p k f", k=2)
                                for kk in range(2):
                                    for j in range(4):
                                        last = mm(ps[0:W, 2 + j, :], act[e % 2][:, 2 * c + kk, :],
                                                  wv[:, kk, j * 512:(j + 1) * 512],
                                                  start=(e == 0 and c == 0 and kk == 0),
                                                  stop=(e == 3 and c == 1 and kk == 1))
                                last.then_inc(chunks_done, 1)
                                n += 1
                    eng.wait_ge(o_act[l], w + 2)
                    eng.wait_ge(o_dve[l], w + 2)
                    for j in range(KD):
                        if j < 2:
                            eng.wait_ge(aux_act[l], w * 6 + (5 + j))
                        else:
                            eng.wait_ge(aux_dve[l], w * 16 + (j + 1))
                        mm(ps[:, 6 + j % 2, 0:T], osb[0:W, j * 128:(j + 1) * 128], S[0:W, :], start=True, stop=True)\
                            .then_inc(aux_full[l], 1)
                if l == 0:
                    pe_extra.append(eng.snap(n_win - NG))

            pe_extra = []
            layer_norm(0)
            moe(0)
            layer_norm(1)
            eng.wait_ge(x_ready[1], KD)
            for n in range(8):
                s, q = n // 4, n % 4
                t0 = (TP if s == 0 else T) - PW
                if n >= 4:
                    eng.wait_ge(pst_copied, n - 3)
                for b in range(4):
                    last = nc.tensor.transpose(ps[0:PW, 4 + n % 4, b * 128:(b + 1) * 128],
                                               xT[:, 4 * q + b, t0:t0 + PW], ident[:, :])
                last.then_inc(pst_full, 1)
            for g in range(NG):
                n = C_POOL + g
                eng.wait_ge(pool_diff, g + 1)
                eng.wait_ge(ring_ready[slot_of(n)], pe_extra[0] * 64 + ready_at(n))
                wv = ring_at(n)[:, 0:2048].rearrange("p (k j) -> p k j", k=4)
                if g >= 1:
                    eng.wait_ge(z_ready[2], 4 * g)
                for b in range(4):
                    for k in range(4):
                        last = mm(ps[:, b, 0:T], wv[:, k, b * 128:(b + 1) * 128], pdiff[g % 2][:, k, :],
                                  start=(k == 0), stop=(k == 3))
                last.then_inc(chunks_done, 1)
            eng.wait_ge(pst_copied, 8)
            layer_norm(2)
            moe(1)
            layer_norm(3)
            eng.wait_ge(x_ready[3], KD)
            transpose_x(3, False)

        @block.vector
        def _(eng):
            V = nc.vector
            link = SelfOrder(eng, vself)
            TS_, TT_, STT = V.tensor_scalar, V.tensor_tensor, V.scalar_tensor_tensor

            def evacuate_x(which, to_feature, part=range(12)):
                for n in part:
                    if n % 2 == 0:
                        continue
                    i, q = n // 4, n % 4
                    t0, m = TILES[i]
                    eng.wait_ge(tr_full[which], n + 1)
                    if to_feature:
                        o = xT[:, 4 * q:4 * q + 4, t0:t0 + m]
                        s = ps[:, 4 + n % 4, :].rearrange("p (k c) -> p k c", k=4)[:, :, 0:m]
                    else:
                        o = xtok[0:m, i, q * 512:(q + 1) * 512]
                        s = ps[0:m, 4 + n % 4, :]
                    V.tensor_copy(o, s).then_inc(tr_dve[which], 1)

            marks = []

            def signal(s, n=1):
                marks.append(0)
                c = len(marks)
                V.memset(mark[0:1, c:c + 1], 0.0).then_inc(s, n)

            V.memset(tiny[:, :], 1e-30)
            V.memset(uext[:, :, :], 0.0)
            V.memset(valid[:, 0:2, :], 1.0)
            link(V.memset(valid[:, 2, :], 0.0))
            link(V.memset(valid[0:32, 2, :], 1.0))
            eng.wait_ge(consts, 7)
            link(V.tensor_copy(iota_f[:, :], iota_i[:, :]))
            V.tensor_copy(gidx[:, :], iota_f[:, 0:4])
            TS_(firstw[:, :], iota_f[:, 0:4], -1.0, 4.0, ALU.mult, ALU.add)
            link(TS_(rcount[:, :], iota_f[:, 0:16], 1.0, None, ALU.add))
            link(V.reciprocal(rcount[:, :], rcount[:, :]))
            signal(uext_free, 1)
            signal(gelu_done, 1)
            signal(head_done, 1)
            for l in two:
                signal(aux_dve[l], 2)
                signal(gu_free[l], 1)
                signal(o_act[l], 1)
                signal(o_dve[l], 1)
            eng.wait_ge(init_cp, 1)
            lam = prmT[:, V_LAM * KD:(V_LAM + 1) * KD]
            STT(sp[0][:, :], lam, -1.0, lam, ALU.mult, ALU.max).then_inc(derived, 1)
            TS_(half_ba[:, :], prmT[:, V_BA * KD:(V_BA + 1) * KD], 0.5, None, ALU.mult)
            TS_(half_bx[:, :], prmT[:, V_BX * KD:(V_BX + 1) * KD], 0.5, None, ALU.mult)
            evacuate_x(0, True)
            eng.wait_ge(lam_exp, 1)
            link(TS_(sp[2][:, :], sp[1][:, :], 2.0, None, ALU.add))
            link(V.reciprocal(sp[2][:, :], sp[2][:, :]))
            link(TT_(sp[1][:, :], sp[1][:, :], sp[2][:, :], ALU.mult))
            link(TT_(sp[2][:, :], sp[1][:, :], sp[1][:, :], ALU.mult))
            link(TS_(sp[3][:, :], sp[2][:, :], 1.0 / 15, None, ALU.mult))
            for q in (13, 11, 9, 7, 5, 3):
                link(STT(sp[3][:, :], sp[3][:, :], 1.0 / q, sp[2][:, :], ALU.add, ALU.mult))
            link(STT(sp[3][:, :], sp[3][:, :], 1.0, sp[1][:, :], ALU.add, ALU.mult))
            link(TS_(sp[2][:, :], lam, -1.0, 0.0, ALU.mult, ALU.max))
            link(STT(sp[3][:, :], sp[3][:, :], 2.0, sp[2][:, :], ALU.mult, ALU.add))
            TS_(c_lam[:, :], sp[3][:, :], -4.0, None, ALU.mult).then_inc(derived, 1)
            eng.wait_ge(derived, 2)

            with eng.Fori(0, HEADS // 2) as it:
                lk = SelfOrder(eng, vlru)
                lk.start(it, LRU_LINKS)
                for hh in range(2):
                    h = it * 2 + hh

                    def prm(v, b):
                        return prmT[:, bass.ds(h * 2 + (b + v * KD), 1)]
                    eng.wait_ge(u_copied, it * 4 + (2 * hh + 4))
                    pre = prmT[:, V_CONV0 * KD:(V_CONV0 + 3) * KD].rearrange("p (w k) -> p k w", w=3)
                    lk(V.tensor_copy(uext[:, :, TP + CW - 1:TP + 2 * (CW - 1)], pre[:, bass.ds(h * 2, 2), :]))
                    for b in range(2):
                        lk(TS_(UC[:, b, :], uext[:, b, 0:TG], prm(V_CW, b), prm(V_CB, b), ALU.mult, ALU.add))
                        for k in range(1, CW):
                            i = STT(UC[:, b, :], uext[:, b, k:k + TG], prm(V_CW + k, b), UC[:, b, :], ALU.mult, ALU.add)
                            if k == CW - 1 and b == 1:
                                i.then_inc(uc_ready, 1)
                            else:
                                lk(i)
                    eng.wait_ge(uc_ready, it * 2 + (hh + 1))
                    V.tensor_copy(cst[:, bass.ds(h * 2, 2), 0:3], uext[:, :, TP:TP + 3])
                    V.tensor_copy(cst[:, bass.ds(h * 2, 2), 3:6], uext[:, :, UX - 3:UX]).then_inc(uext_free, 1)
                    eng.wait_ge(gsq_ready, it * 2 + (hh + 1))
                    lk(TS_(GS[:, :, 0:T], GS[:, :, 0:T], 0.044715, 1.0, ALU.mult, ALU.add))
                    TT_(GS[:, :, 0:T], GS[:, :, 0:T], ps[:, 2:4, 0:T], ALU.mult).then_inc(gin_ready, 1)
                    eng.wait_ge(gtanh_ready, it * 2 + (hh + 1))
                    STT(GG[:, :, 0:T], GG[:, :, 0:T], 1.0, ps[:, 2:4, 0:T], ALU.add, ALU.mult).then_inc(gelu_done, 1)
                    eng.wait_ge(decay_ready, it * 2 + (hh + 1))
                    lk(TT_(GS[:, :, :], AA[:, :, :], AA[:, :, :], ALU.mult))
                    STT(TL[:, :, :], GS[:, :, :], 1.0, TL[:, :, :], ALU.add, ALU.mult).then_inc(q_ready, 1)
                    lk(STT(TX[:, :, :], TX[:, :, :], 1.0, UC[:, :, :], ALU.add, ALU.mult))
                    eng.wait_ge(mult_ready, it * 2 + (hh + 1))
                    lk(STT(TX[:, :, :], TX[:, :, :], 0.5, TL[:, :, :], ALU.mult, ALU.mult))
                    V.memset(AA[:, :, SEAM:SEAM + 1], 0.0)
                    lk(V.tensor_copy(TX[:, :, SEAM:SEAM + 1],
                                     prmT[:, bass.ds(h * 2 + V_H0 * KD, 2)].rearrange("p (b o) -> p b o", o=1)))
                    for b in range(2):
                        i = V.tensor_tensor_scan(TR[:, b, :], AA[:, b, :], TX[:, b, :], 0.0, ALU.mult, ALU.add)
                    lk(i)
                    V.tensor_copy(cst[:, bass.ds(h * 2, 2), 6:7], TR[:, :, TP - 1:TP])
                    V.tensor_copy(cst[:, bass.ds(h * 2, 2), 7:8], TR[:, :, TG - 1:TG])
                    STT(yT[:, bass.ds(h * 2, 2), 0:TP], GG[:, :, 0:TP], 0.5, TR[:, :, 0:TP], ALU.mult, ALU.mult)
                    STT(yT[:, bass.ds(h * 2, 2), TP:T], GG[:, :, TP:T], 0.5, TR[:, :, TG - TS:TG], ALU.mult, ALU.mult)\
                        .then_inc(head_done, 1)
                lk.check()
            signal(cst_done, 1)
            for i in range(N_OUT):
                eng.wait_ge(chunks_done, C_OUT + i + 1)
                for b in range(2):
                    k = 2 * i + b
                    STT(z[:, k, :], xT[:, k, :], ALPHA, ps[:, k % 6, 0:T], ALU.mult, ALU.add).then_inc(z_ready[0], 1)
            eng.wait_ge(z_ready[0], KD)
            eng.wait_ge(chunks_done, C_MOE0)

            def layer_norm(n):
                V.tensor_reduce(zsum[:, :], z[:, :, :].rearrange("p k t -> p t k"), AX.X, ALU.add)\
                    .then_inc(zsum_ready[n], 1)
                eng.wait_ge(stat_done[n], 1)
                link(V.tensor_copy(mean[:, :], ps[:, 7, 0:T]))
                link(TT_(nmr[:, :], mean[:, :], mean[:, :], ALU.mult))
                link(STT(nmr[:, :], ps[:, 6, 0:T], EPS, nmr[:, :], ALU.add, ALU.subtract))
                TS_(rstd[:, :], nmr[:, :], EPS * 0.5, None, ALU.max).then_inc(var_ready[n], 1)
                eng.wait_ge(std_ready[n], 1)
                link(V.reciprocal(rstd[:, :], rstd[:, :]))
                link(STT(nmr[:, :], mean[:, :], -1.0, rstd[:, :], ALU.mult, ALU.mult))
                for q in range(4):
                    zq = z[:, 4 * q:4 * q + 4, :]
                    link(TT_(zq, zq, rstd[:, :].unsqueeze(1).to_broadcast([128, 4, T]), ALU.mult))
                    TT_(zq, zq, nmr[:, :].unsqueeze(1).to_broadcast([128, 4, T]), ALU.add).then_inc(norm_q[n], 1)

            def bc(v, n):
                return v.to_broadcast([128, 3, n])

            def first_max(out, v, m, tmp, tmp1):
                link(V.tensor_reduce(m[:, :, 0], v[:, :, :], AX.X, ALU.max))
                link(TT_(tmp[:, :, :], v[:, :, :], bc(m[:, :, :], 4), ALU.is_equal))
                fw = firstw[:, :].unsqueeze(1).to_broadcast([128, 3, 4])
                link(TT_(tmp[:, :, :], tmp[:, :, :], fw, ALU.mult))
                link(V.tensor_reduce(tmp1[:, :, 0], tmp[:, :, :], AX.X, ALU.max))
                link(TT_(out[:, :, :], tmp[:, :, :], bc(tmp1[:, :, :], 4), ALU.is_equal))

            def moe(l):
                link(V.memset(logit[:, :, :], 0.0))
                eng.wait_ge(lg_done[l], 1)
                V.tensor_copy(logit[:, 0:2, :], ps[:, 0, 0:64].rearrange("p (i j) -> p i j", i=2)[:, :, 0:20])
                link(V.tensor_copy(logit[0:32, 2, :], ps[0:32, 0, 64:84]))
                lg = logit[:, :, 0:4]
                link(V.tensor_reduce(r1[0][:, :, 0], lg, AX.X, ALU.max))
                TT_(r4[0][:, :, :], lg, bc(r1[0][:, :, :], 4), ALU.subtract).then_inc(ex_in[l], 1)
                link(TT_(r4[2][:, :, :], lg, bc(r1[0][:, :, :], 4), ALU.is_equal))
                fw = firstw[:, :].unsqueeze(1).to_broadcast([128, 3, 4])
                link(TT_(r4[2][:, :, :], r4[2][:, :, :], fw, ALU.mult))
                link(V.tensor_reduce(r1[1][:, :, 0], r4[2][:, :, :], AX.X, ALU.max))
                link(TT_(Gh[:, :, :], r4[2][:, :, :], bc(r1[1][:, :, :], 4), ALU.is_equal))
                TT_(Gh[:, :, :], Gh[:, :, :], bc(valid[:, :, :], 4), ALU.mult).then_inc(oh_ready[l], 1)
                eng.wait_ge(oh_ready[l], 1)
                for i in range(3):
                    o = lprod[:, i, :].rearrange("p (g j) -> p g j", g=4)
                    ins = TT_(o, logit[:, i, 4:20].rearrange("p (g j) -> p g j", g=4),
                              Gh[:, i, :].unsqueeze(2).to_broadcast([128, 4, 4]), ALU.mult)
                link(ins)
                link(V.tensor_reduce(les[:, :, :], lprod[:, :, :].rearrange("p i (g j) -> p i j g", g=4), AX.X, ALU.add))
                first_max(E1, les, r1[0], r4[2], r1[1])
                link(STT(les[:, :, :], E1[:, :, :], -1e30, les[:, :, :], ALU.mult, ALU.add))
                first_max(gate4, les, r1[4], r4[2], r1[1])
                TT_(r1[2][:, :, :], r1[4][:, :, :], r1[0][:, :, :], ALU.subtract).then_inc(ex_in[l], 1)
                eng.wait_ge(ex_out[l], 1)
                link(V.tensor_reduce(r1[5][:, :, 0], r4[1][:, :, :], AX.X, ALU.add))
                eng.wait_ge(ex_out[l], 2)
                link(STT(r1[6][:, :, :], r1[3][:, :, :], 1.0, r1[5][:, :, :], ALU.add, ALU.mult))
                link(V.reciprocal(r1[6][:, :, :], r1[6][:, :, :]))
                link(TT_(r1[7][:, :, :], r1[6][:, :, :], r1[3][:, :, :], ALU.mult))
                link(TT_(gate4[:, :, :], gate4[:, :, :], bc(r1[7][:, :, :], 4), ALU.mult))
                link(TT_(E1[:, :, :], E1[:, :, :], bc(r1[6][:, :, :], 4), ALU.mult))
                link(TT_(gate4[:, :, :], gate4[:, :, :], E1[:, :, :], ALU.add))
                eng.wait_ge(cnt_done[l], 1)
                link(V.tensor_copy(n_g[:, :], ps[:, 1, 16:20]))
                link(TT_(r4[2][:, :, :], Gh[:, :, :], ps[:, 1, 0:12].rearrange("p (i g) -> p i g", i=3), ALU.mult))
                pos, k_w, first, tmp = r1[0], r1[1], r1[2], r1[4]
                link(V.tensor_reduce(pos[:, :, 0], r4[2][:, :, :], AX.X, ALU.add))
                link(TS_(k_w[:, :, :], pos[:, :, :], float(W), None, ALU.is_ge))
                link(TS_(more[:, :], n_g[:, :], float(W), None, ALU.is_gt))
                for m in range(2, -(-T // W)):
                    link(STT(k_w[:, :, :], pos[:, :, :], float(m * W), k_w[:, :, :], ALU.is_ge, ALU.add))
                    link(STT(more[:, :], n_g[:, :], float(m * W), more[:, :], ALU.is_gt, ALU.add))
                link(STT(pos[:, :, :], k_w[:, :, :], -float(W), pos[:, :, :], ALU.mult, ALU.add))
                link(V.memset(mbase[:, :], 0.0))
                for g in range(1, NG):
                    link(TT_(mbase[:, g:g + 1], mbase[:, g - 1:g], more[:, g - 1:g], ALU.add))
                g_w, m_w = r4[0], r4[3]
                link(TT_(g_w[:, :, :], Gh[:, :, :], gidx[:, :].unsqueeze(1).to_broadcast([128, 3, 4]), ALU.mult))
                link(TT_(m_w[:, :, :], Gh[:, :, :], mbase[:, :].unsqueeze(1).to_broadcast([128, 3, 4]), ALU.mult))
                link(V.tensor_reduce(first[:, :, 0], g_w[:, :, :], AX.X, ALU.add))
                link(V.tensor_reduce(tmp[:, :, 0], m_w[:, :, :], AX.X, ALU.add))
                link(STT(tmp[:, :, :], tmp[:, :, :], 3.0, k_w[:, :, :], ALU.add, ALU.add))
                link(TT_(tmp[:, :, :], tmp[:, :, :], first[:, :, :], ALU.subtract))
                link(TS_(k_w[:, :, :], k_w[:, :, :], 0.0, None, ALU.is_gt))
                link(TT_(tmp[:, :, :], tmp[:, :, :], k_w[:, :, :], ALU.mult))
                link(TT_(tmp[:, :, :], tmp[:, :, :], first[:, :, :], ALU.add))
                link(STT(slotno[:, :, :], tmp[:, :, :], float(W), pos[:, :, :], ALU.mult, ALU.add))
                link(STT(slotno[:, :, :], slotno[:, :, :], 1.0, valid[:, :, :], ALU.add, ALU.mult))
                link(TS_(slotno[:, :, :], slotno[:, :, :], -1.0, None, ALU.add))
                link(V.memset(route_f[:, :], 0.0))
                link(V.tensor_reduce(route_f[:, 0:1], more[:, :], AX.X, ALU.add))
                link(TS_(route_f[:, 0:1], route_f[:, 0:1], float(NG), None, ALU.add))
                link(TT_(more[:, :], more[:, :], mbase[:, :], ALU.add))
                for x in range(MORE):
                    link(TS_(t4[:, :], mbase[:, :], float(x), None, ALU.is_le))
                    link(TT_(t4[:, :], t4[:, :], gidx[:, :], ALU.mult))
                    link(STT(t4[:, :], more[:, :], float(x), t4[:, :], ALU.is_gt, ALU.mult))
                    link(V.tensor_reduce(route_f[:, 1 + x:2 + x], t4[:, :], AX.X, ALU.add))
                V.tensor_copy(route_i[0:1, l, :], route_f[0:1, :]).then_inc(route_ready[l], 1)
                for i in range(3):
                    for e in range(NE):
                        ins = TS_(grep[:, i, e, :], ones[:, :], gate4[:, i, e:e + 1], None, ALU.mult)
                ins.then_inc(grep_ready[l], 1)
                eng.wait_ge(ax_ready[2 * l], KD)
                eng.wait_ge(route_ready[l], 1)
                n_win = eng.value_load(route_i[0:1, l, 0:1], min_val=NG, max_val=NG + MORE)
                base = C_MOE0 if l == 0 else C_MOE1
                with eng.Fori(0, n_win) as w:
                    seq = w if l == 0 else w + dve_extra[0]
                    lk = SelfOrder(eng, vmoe[l])
                    lk.start(w, MOE_LINKS)
                    eng.wait_ge(chunks_done, seq * PER_WIN + (base - PER_WIN + 1))
                    for i in range(3):
                        ins = TS_(P[:, i, :], iota_f[:, 0:W], slotno[:, i, :], None, ALU.is_equal)
                    ins.then_inc(P_ready[l], 1)
                    eng.wait_ge(P_ready[l], w + 1)
                    lk(TS_(slotno[:, :, :], slotno[:, :, :], -float(W), None, ALU.add))
                    for e in range(NE):
                        eng.wait_ge(th_ready[l], w * 4 + (e + 1))
                        prev = DN_DONE[e - 2] if e >= 2 else DN_DONE[e + 2] - PER_WIN
                        eng.wait_ge(chunks_done, seq * PER_WIN + (base + prev))
                        a = act[e % 2]
                        af = a.rearrange("p f w -> p (f w)")
                        lk(STT(af, th[:, :], 1.0, ps[:, 0, 0:KF * W], ALU.add, ALU.mult))
                        TT_(af, af, ps[:, 1, 0:KF * W], ALU.mult).then_inc(gu_free[l], 1)
                        eng.wait_ge(gu_free[l], w * 4 + (e + 2))
                        if e == 0:
                            eng.wait_ge(aux_act[l], w * 6 + 2)
                        TT_(a, a,
                            gbc[:, e, :].unsqueeze(1).to_broadcast([128, KF, W]), ALU.mult).then_inc(act_ready[l], 1)
                    eng.wait_ge(chunks_done, seq * PER_WIN + (base + DN_DONE[3]))
                    for b in range(2, 4):
                        ins = V.tensor_copy(osb[0:W, b * 512:(b + 1) * 512], ps[0:W, 2 + b, :])
                    ins.then_inc(o_dve[l], 1)
                    for j in range(KD):
                        eng.wait_ge(aux_full[l], w * 22 + (7 + j))
                        TT_(z[:, j, :], z[:, j, :], ps[:, 6 + j % 2, 0:T], ALU.add).then_inc(aux_dve[l], 1)
                    lk.check()
                signal(zall[1 + 2 * l], 1)
                eng.wait_ge(zall[1 + 2 * l], 1)
                if l == 0:
                    dve_extra.append(eng.snap(n_win - NG))

            def pool_add(g, extra):
                if g == 0:
                    eng.wait_ge(ax_ready[1], KD)
                eng.wait_ge(chunks_done, extra * PER_WIN + (C_POOL + g + 1))
                for b in range(4):
                    k = 4 * g + b
                    c = V_SCALE * KD + k
                    STT(z[:, k, :], ps[:, b, 0:T], prmT[:, c:c + 1], z[:, k, :], ALU.mult, ALU.add)\
                        .then_inc(z_ready[2], 1)

            dve_extra = []
            layer_norm(0)
            link(V.memset(xtok[:, 2, :], 0.0))
            moe(0)
            layer_norm(1)

            eng.wait_ge(x_ready[1], KD)
            Ls = PW + TP
            for g in range(NG):
                win = 2 << g
                blk = slice(4 * g, 4 * g + 4)
                V.memset(pext[:, :, 0:PW], 0.0)
                V.tensor_copy(pext[:, :, PW:Ls], xT[:, blk, 0:TP])
                V.tensor_copy(pext[:, :, Ls:Ls + PW], poolpre[:, blk, :])
                link(V.tensor_copy(pext[:, :, Ls + PW:PX], xT[:, blk, TP:T]))
                src = pext
                for j in range(g + 1):
                    step = 1 << j
                    lo = 2 * step - 1
                    dst = (pa, pb)[j % 2]
                    link(TT_(dst[:, :, lo:PX], src[:, :, lo:PX], src[:, :, lo - step:PX - step], ALU.add))
                    src = dst
                if g >= 2:
                    eng.wait_ge(z_ready[2], 4 * (g - 1))
                pd = pdiff[g % 2]
                STT(pd[:, :, 0:TP], src[:, :, PW:Ls], 1.0 / win, xT[:, blk, 0:TP], ALU.mult, ALU.subtract)
                link(STT(pd[:, :, TP:T], src[:, :, Ls + PW:PX], 1.0 / win, xT[:, blk, TP:T], ALU.mult, ALU.subtract))
                rc = rcount[:, 0:win - 1].unsqueeze(1).to_broadcast([128, 4, win - 1])
                link(TT_(src[:, :, PW:PW + win - 1], src[:, :, PW:PW + win - 1], rc, ALU.mult))
                TT_(pd[:, :, 0:win - 1], src[:, :, PW:PW + win - 1], xT[:, blk, 0:win - 1], ALU.subtract)\
                    .then_inc(pool_diff, 1)
                eng.wait_ge(pool_diff, g + 1)
                if g >= 1:
                    pool_add(g - 1, dve_extra[0])
            pool_add(NG - 1, dve_extra[0])
            eng.wait_ge(z_ready[2], KD)
            layer_norm(2)
            link(V.memset(xtok[:, 2, :], 0.0))
            moe(1)
            layer_norm(3)
            evacuate_x(3, False)


_INS = ["x_prompt", "x_sample", "state_lru_h", "state_lru_conv", "state_pool", "lru_w_in", "lru_conv_w", "lru_conv_b",
        "lru_w_a", "lru_b_a", "lru_w_x", "lru_b_x", "lru_lambda", "lru_w_out", "pool_w", "pool_scale", "ln_g", "ln_b",
        "moe_router_g_w", "moe_router_g_b", "moe_router_e_w", "moe_router_e_b", "moe_w_gate_up", "moe_w_down"]
_OUTS = [("y_prompt", (1, TP, D)), ("y_sample", (1, TS, D)), ("lru_h_prompt", (1, 1, D)),
         ("lru_conv_prompt", (1, 1, CW - 1, D)), ("pool_prompt", (1, 1, PW, D)), ("lru_h_sample", (1, 1, D)),
         ("lru_conv_sample", (1, 1, CW - 1, D)), ("pool_sample", (1, 1, PW, D))]


def kernel(**inputs):
    import concourse.bacc as bacc
    from concourse.bass_utils import run_bass_kernel_spmd as run

    nc = bacc.Bacc("TRN2", target_bir_lowering=False, num_devices=1)
    arrays = {f"in_{name}": np.ascontiguousarray(inputs[name]) for name in _INS}
    A = {name: nc.dram_tensor(f"in_{name}", arrays[f"in_{name}"].shape, F32, kind="ExternalInput").ap() for name in _INS}
    O = {name: nc.dram_tensor(f"out_{name}", shape, F32, kind="ExternalOutput").ap() for name, shape in _OUTS}
    encoder_step(nc, A, O)
    r = run(nc, [arrays], core_ids=[0])
    return tuple(r.results[0][f"out_{name}"] for name, _ in _OUTS)
```

```python
import numpy as np
import concourse.bass as bass
from concourse import mybir
from contextlib import ExitStack

F32 = mybir.dt.float32
F32R = mybir.dt.float32r
I32 = mybir.dt.int32
ALU = mybir.AluOpType
ACT = mybir.ActivationFunctionType
AX = mybir.AxisListType

D = 2048
KD = D // 128
TP, TS = 256, 32
T = TP + TS
TILES = [(0, 128), (128, 128), (256, 32)]
HEADS = 8
CW = 4
TG = TP + TS + CW - 1
SEAM = TP + CW - 2
UX = TG + CW - 1
NG, NE = 4, 4
FE = 512
KF = FE // 128
W = 96
MORE = T // (W + 1)
PW = 15
PT = TS + PW
ALPHA = 4.0 ** 0.25
EPS = 1e-5
NSLOT, SLOT = 6, 4096
SLOT0 = 4
C_OUT = 3 * HEADS
N_OUT = 8
C_MOE0 = C_OUT + N_OUT
PER_WIN = 24
DN_WIN = 8
C_POOL = C_MOE0 + NG * PER_WIN
C_MOE1 = C_POOL + NG
DONE_MOE0 = C_MOE0
DONE_POOL = DONE_MOE0 + NG * DN_WIN
DONE_MOE1 = DONE_POOL + NG
NPART, PART = 4, 512
PARTS_CHUNK = SLOT // PART
PARTS_GU = 4 * PARTS_CHUNK
PARTS_WIN = NE * PARTS_GU
WINDOW_ORDER = [("gu", 0), ("gu", 1), ("dn", 0), ("gu", 2), ("dn", 1), ("gu", 3), ("dn", 2), ("dn", 3)]
KINDS = [kind for kind, e in WINDOW_ORDER for _ in range(4 if kind == "gu" else 2)]
WINDOW_POS = {we: sum(4 if k == "gu" else 2 for k, _ in WINDOW_ORDER[:i]) for i, we in enumerate(WINDOW_ORDER)}
V_CW, V_CB, V_BA, V_BX, V_LAM, V_LNG, V_LNB, V_SCALE, V_H0, V_CONV0 = 0, 4, 5, 6, 7, 8, 12, 16, 17, 18


def slot_of(n):
    return (n + SLOT0) % NSLOT


def dmas_of(n):
    return 2 if n < C_OUT and n % 3 == 2 else 1


def ready_at(n):
    return 16 * sum(dmas_of(m) for m in range(n % NSLOT, n + 1, NSLOT))


LRU_LINKS = 28
MOE_LINKS = 5
CREDIT = 16


class SelfOrder:

    def __init__(self, eng, sem):
        self.eng, self.sem, self.n, self.i, self.per = eng, sem, 0, None, 0

    def start(self, i, per):
        self.i, self.per, self.n = i, per, 0

    def __call__(self, ins):
        self.n += 1
        ins.then_inc(self.sem, 1)
        self.eng.wait_ge(self.sem, self.n if self.i is None else self.i * self.per + self.n)

    def check(self):
        assert self.n == self.per, (self.n, self.per)


def encoder_step(nc, A, O):
    ctx = ExitStack()
    with ctx:
        def sb(name, shape, dt=F32):
            return ctx.enter_context(nc.sbuf_tensor(name, shape, dt))

        def sem(name):
            return ctx.enter_context(nc.semaphore(name))

        ring = sb("ring", [128, NSLOT, SLOT])
        xT = sb("xT", [128, KD, T])
        z = xT
        xtok = sb("xtok", [128, 3, D])
        arena = sb("arena", [128, 4096])
        prmT = sb("prmT", [128, 24 * KD])
        wrT = sb("wrT", [128, 2, 20, KD])
        brow = sb("brow", [1, 2, 20])
        ident = sb("ident", [128, 128])
        ones = sb("ones", [128, 128])
        onesd = sb("onesd", [128, 128])
        before = sb("before", [128, 128])
        iota_i = sb("iota_i", [128, 128], I32)
        iota_f = sb("iota_f", [128, 128])
        valid = sb("valid", [128, 3, 1])
        rcount = sb("rcount", [128, 16])
        poolpre = sb("poolpre", [128, PW, KD])
        cst = sb("cst", [128, KD, 8])
        cstT = sb("cstT", [128, 128])
        half_ba = sb("half_ba", [128, KD])
        half_bx = sb("half_bx", [128, KD])
        c_lam = sb("c_lam", [128, KD])
        sp = [sb(f"sp{i}", [128, KD]) for i in range(4)]
        tiny = sb("tiny", [128, 1])
        mark = sb("mark", [1, 32])
        uext = sb("uext", [128, 2, UX])
        sq = sb("sq", [128, 2, T])
        mean = sb("mean", [128, T])
        rstd = sb("rstd", [128, T])
        nmr = sb("nmr", [128, T])
        zsum = sb("zsum", [128, T])
        logit = sb("logit", [128, 3, 20])
        r4 = [sb(f"r4_{i}", [128, 3, 4]) for i in range(4)]
        Gh = sb("Gh", [128, 3, 4])
        E1 = sb("E1", [128, 3, 4])
        gate4 = sb("gate4", [128, 3, 4])
        les = sb("les", [128, 3, 4])
        lprod = sb("lprod", [128, 3, 16])
        r1 = [sb(f"r1_{i}", [128, 3, 1]) for i in range(8)]
        gidx = sb("gidx", [128, 4])
        firstw = sb("firstw", [128, 4])
        n_g = sb("n_g", [128, 4])
        more = sb("more", [128, 4])
        mbase = sb("mbase", [128, 4])
        t4 = sb("t4", [128, 4])
        slotno = sb("slotno", [128, 3, 1])
        route_f = sb("route_f", [128, 8])
        route_i = sb("route_i", [1, 2, 8], I32)
        ps = ctx.enter_context(nc.psum_tensor("ps", [128, 8, 512], F32))

        def carve(tensor, at, *shape):
            n = int(np.prod(shape))
            v = tensor[:, at:at + n]
            names = " ".join("abc"[:len(shape)])
            kw = {"abc"[i]: s for i, s in enumerate(shape[1:], 1)}
            return v.rearrange(f"p ({names}) -> p {names}", **kw) if len(shape) > 1 else v

        whi = sb("whi", [128, NPART, PART], F32R)
        wlo = sb("wlo", [128, NPART, PART], F32R)
        xhi = sb("xhi", [128, KD, W], F32R)
        xlo = sb("xlo", [128, KD, W], F32R)
        osb = carve(arena, 0, D)
        act = [carve(arena, 2048 + 384 * i, KF, W) for i in range(2)]
        th = carve(arena, 2816, FE)
        P = carve(arena, 3328, 3, W)
        S = carve(arena, 3616, T)
        gslot = carve(arena, 3904, NE)
        prow = carve(sq[:, :, :].rearrange("p a t -> p (a t)"), 0, 3, 128)
        xTf = xT[:, :, :].rearrange("p k t -> p (k t)")
        wbase = [arena, xTf]
        wrow = [(b[0:16, 0:512].rearrange("k (p g) -> k p g", g=4),
                 b[0:16, 512:2560].rearrange("k (p g) -> k p g", g=16)) for b in wbase]
        pstrow = arena[0:120, 2560:2816].rearrange("r (a p) -> r a p", a=2)
        prow_out = arena[0:PT, 0:D]
        UC, GG, GS, TR, TX, AA, TL = [carve(arena, i * 2 * TG, 2, TG) for i in range(7)]
        xtf = xtok[:, :, :].rearrange("p i d -> p (i d)")
        yT = carve(xtf, 0, KD, T)
        PX = PW + TP + PW + TS
        pext, pa, pb = [carve(xtf, i * 4 * PX, 4, PX) for i in range(3)]
        pdiff = [carve(xtf, 12 * PX + i * 4 * T, 4, T) for i in range(2)]

        x_in = [sem(f"x_in{i}") for i in range(3)]
        prm_in, wr_in, pst_in, brow_in = sem("prm_in"), sem("wr_in"), sem("pst_in"), sem("brow_in")
        consts = sem("consts")
        ring_ready = [sem(f"ring_ready{i}") for i in range(NSLOT)]
        chunks_done = sem("chunks_done")
        hi_ready, lo_ready, parts_used = sem("hi_ready"), sem("lo_ready"), sem("parts_used")
        init_tr = sem("init_tr")
        init_cp = sem("init_cp")
        derived = sem("derived")
        lam_exp = sem("lam_exp")
        vself = sem("vself")
        tr_full = [sem(f"tr_full{i}") for i in range(4)]
        tr_act = [sem(f"tr_act{i}") for i in range(4)]
        tr_dve = [sem(f"tr_dve{i}") for i in range(4)]
        u_copied, uext_free, uc_ready = sem("u_copied"), sem("uext_free"), sem("uc_ready")
        gsq_ready, gin_ready, gtanh_ready, gelu_done = sem("gsq"), sem("gin"), sem("gtanh"), sem("gelu_done")
        ri_read, decay_ready, q_ready, mult_ready = sem("ri_read"), sem("decay_ready"), sem("q_ready"), sem("mult")
        head_done = sem("head_done")
        vlru = sem("vlru")
        z_ready = [sem(f"z_ready{i}") for i in range(4)]
        zall = [sem(f"zall{i}") for i in range(4)]
        sq_ready = [sem(f"sq_ready{i}") for i in range(4)]
        sq_used = [sem(f"sq_used{i}") for i in range(4)]
        zsum_ready = [sem(f"zsum_ready{i}") for i in range(4)]
        stat_done = [sem(f"stat_done{i}") for i in range(4)]
        var_ready = [sem(f"var_ready{i}") for i in range(4)]
        std_ready = [sem(f"std_ready{i}") for i in range(4)]
        norm_q = [sem(f"norm_q{i}") for i in range(4)]
        x_ready = [sem(f"x_ready{i}") for i in range(4)]
        ax_ready = [sem(f"ax_ready{i}") for i in range(2)]
        two = range(2)
        lg_done = [sem(f"lg_done{i}") for i in two]
        ex_in = [sem(f"ex_in{i}") for i in two]
        ex_out = [sem(f"ex_out{i}") for i in two]
        oh_ready = [sem(f"oh_ready{i}") for i in two]
        cnt_done = [sem(f"cnt_done{i}") for i in two]
        route_ready = [sem(f"route_ready{i}") for i in two]
        P_ready = [sem(f"P_ready{i}") for i in two]
        aux_full = [sem(f"aux_full{i}") for i in two]
        aux_act = [sem(f"aux_act{i}") for i in two]
        aux_dve = [sem(f"aux_dve{i}") for i in two]
        th_ready = [sem(f"th_ready{i}") for i in two]
        gated = [sem(f"gated{i}") for i in two]
        xhi_ready = [sem(f"xhi_ready{i}") for i in two]
        o_act = [sem(f"o_act{i}") for i in two]
        o_dve = [sem(f"o_dve{i}") for i in two]
        vmoe = [sem(f"vmoe{i}") for i in two]
        cst_done, cstT_full, cstT_ready = sem("cst_done"), sem("cstT_full"), sem("cstT_ready")
        pst_full, pst_copied = sem("pst_full"), sem("pst_copied")
        pext_ready, pool_diff = sem("pext_ready"), sem("pool_diff")
        out_st, out_y = sem("out_st"), sem("out_y")

        w_in = A["lru_w_in"][0].rearrange("(k p) e -> p k e", p=128)
        w_a = A["lru_w_a"].rearrange("l h i j -> (l h i j)")
        w_x = A["lru_w_x"].rearrange("l h i j -> (l h i j)")
        w_out = A["lru_w_out"][0].rearrange("(k p) e -> p k e", p=128)
        pool_w = A["pool_w"][0].rearrange("g (k p) j -> g p k j", p=128)
        gu_w = [A["moe_w_gate_up"][l].rearrange("e d f -> (e d f)") for l in two]
        dn_w = [A["moe_w_down"][l].rearrange("e f d -> (e f d)") for l in two]

        def ring_at(n):
            return ring[:, slot_of(n), :]

        block = ctx.enter_context(nc.Block())

        @block.sync
        def _(eng):
            xp, xs = A["x_prompt"][0], A["x_sample"][0]
            for i, (t0, m) in enumerate(TILES):
                src = xp[t0:t0 + m, :] if t0 < TP else xs
                eng.dma_start(xtok[0:m, i, :], src).then_inc(x_in[i], 16)

            def lru_head(h, hh, it):
                for j in range(3):
                    n = 3 * hh + j
                    dst = ring_at(n)
                    if j < 2:
                        col = h * 256 + (D if j == 0 else 0)
                        if it is not None:
                            need = eng.snap(it * 6 + (n - NSLOT + 1))
                            eng.wait_ge(chunks_done, need)
                            col = h * 256 + D if j == 0 else it * 512 + hh * 256
                        eng.dma_start(dst.rearrange("p (k c) -> p k c", c=256), w_in[:, :, bass.ds(col, 256)])\
                           .then_inc(ring_ready[slot_of(n)], 16)
                    else:
                        if it is not None:
                            need = eng.snap(it * 6 + (n - NSLOT + 1))
                            eng.wait_ge(chunks_done, need)
                        for a, w in enumerate((w_a, w_x)):
                            src = w[bass.ds(h * (256 * 256), 256 * 256)]\
                                .rearrange("(k p j) -> p k j", k=2, p=128)
                            eng.dma_start(dst[:, a * 512:(a + 1) * 512].rearrange("p (k j) -> p k j", k=2), src)\
                               .then_inc(ring_ready[slot_of(n)], 16)

            for hh in range(2):
                lru_head(hh, hh, None)
            with eng.Fori(2, HEADS // 2 + 1) as after:
                it = after - 1
                for hh in range(2):
                    lru_head(eng.snap(it * 2 + hh), hh, it)
            for i in range(N_OUT):
                n = C_OUT + i
                eng.wait_ge(chunks_done, n - NSLOT + 1)
                eng.dma_start(ring_at(n).rearrange("p (k c) -> p k c", c=256), w_out[:, :, i * 256:(i + 1) * 256])\
                   .then_inc(ring_ready[slot_of(n)], 16)

            def window_loads(l, group, seq, base, first=False):
                def snap(v):
                    return v if isinstance(v, int) else eng.snap(v)
                n = base
                done = DONE_MOE0 if l == 0 else DONE_MOE1
                for kind, e in WINDOW_ORDER:
                    for c in range(4 if kind == "gu" else 2):
                        w, per_expert, k = (gu_w[l], D * 2 * FE, 4) if kind == "gu" else (dn_w[l], FE * D, 2)
                        at = snap(group * (NE * per_expert) + (e * per_expert + c * 128 * SLOT))
                        p = n - base
                        last = (p - NSLOT) % PER_WIN
                        before_w = 0 if p >= NSLOT else 1
                        upto = KINDS[:last + 1]
                        dn_need = snap(seq * DN_WIN + (done + upto.count("dn") - before_w * DN_WIN))
                        lo_need = snap(seq * PARTS_WIN + (l * NG * PARTS_WIN + CREDIT + PARTS_CHUNK *
                                           (upto.count("gu") - before_w * KINDS.count("gu"))))
                        if first and before_w:
                            eng.wait_ge(chunks_done, snap(seq * DN_WIN + (done - NSLOT + 1 + p)))
                        elif KINDS[last] == "dn":
                            eng.wait_ge(chunks_done, dn_need)
                        else:
                            eng.wait_ge(lo_ready, lo_need)
                        src = w[bass.ds(at, 128 * SLOT)].rearrange("(k p f) -> p k f", k=k, p=128)
                        dst = ring_at(n).rearrange("p (k f) -> p k f", k=k)
                        eng.dma_start(dst, src).then_inc(ring_ready[slot_of(n)], 16)
                        n += 1

            extra = 0
            for l, base in enumerate((C_MOE0, C_MOE1)):
                if l == 1:
                    for g in range(NG):
                        n = C_POOL + g
                        if g < 2:
                            lo_need = eng.snap(extra * PARTS_WIN + (CREDIT + NG * PARTS_WIN - (1 - g) * PARTS_CHUNK))
                            eng.wait_ge(lo_ready, lo_need)
                        else:
                            need = eng.snap(extra * DN_WIN + (DONE_POOL - 4 + (g - 1)))
                            eng.wait_ge(chunks_done, need)
                        eng.dma_start(ring_at(n)[:, 0:2048].rearrange("p (k j) -> p k j", k=4), pool_w[g])\
                           .then_inc(ring_ready[slot_of(n)], 16)
                window_loads(l, 0, extra, base, first=True)
                with eng.Fori(1, NG) as w:
                    window_loads(l, eng.snap(w + 0), eng.snap(w + extra), base)
                eng.wait_ge(route_ready[l], 1)
                n_win = eng.value_load(route_i[0:1, l, 0:1], min_val=NG, max_val=NG + MORE)
                with eng.If(n_win > NG):
                    with eng.Fori(NG, n_win) as w:
                        g = eng.value_load(route_i[0:1, l, bass.ds(w - (NG - 1), 1)], min_val=0, max_val=NG - 1)
                        window_loads(l, g, eng.snap(w + extra), base)
                with eng.Else():
                    eng.nop()
                if l == 0:
                    extra = eng.snap(n_win - NG)
            eng.wait_ge(tr_act[3], 6)
            eng.wait_ge(tr_dve[3], 6)
            for i, (t0, m) in enumerate(TILES):
                dst = O["y_prompt"][0, t0:t0 + m, :] if t0 < TP else O["y_sample"][0]
                eng.dma_start(dst, xtok[0:m, i, :]).then_inc(out_y, 16)
            eng.wait_ge(out_y, 48)

        @block.gpsimd
        def _(eng):
            eng.memset(ident[:, :], 0.0).then_inc(consts, 1)
            eng.memset(before[:, :], 1.0).then_inc(consts, 1)
            eng.memset(ones[:, :], 1.0).then_inc(consts, 1)
            eng.memset(onesd[:, :], 1.0 / D).then_inc(consts, 1)
            eng.wait_ge(consts, 4)
            eng.affine_select(out=ident[:, :], in_=ident[:, :], compare_op=ALU.not_equal, fill=1.0, base=0,
                              pattern=[[-1, 128]], channel_multiplier=1).then_inc(consts, 1)
            eng.affine_select(out=before[:, :], in_=before[:, :], compare_op=ALU.is_gt, fill=0.0, base=0,
                              pattern=[[1, 128]], channel_multiplier=-1).then_inc(consts, 1)
            eng.iota(iota_i[:, :], pattern=[[1, 128]], base=0, channel_multiplier=0).then_inc(consts, 1)
            for l in two:
                eng.wait_ge(tr_full[1 + l], 12)
                for k in range(KD):
                    eng.tensor_scalar(xT[:, k, :], xT[:, k, :], ALPHA, None, ALU.mult).then_inc(ax_ready[l], 1)

        @block.scalar
        def _(eng):
            for l in two:
                eng.dma_start(wbase[l][0:16, 0:512],
                              A["moe_router_g_w"][l].rearrange("(k p) g -> k (p g)", p=128)).then_inc(wr_in, 16)
                eng.dma_start(wbase[l][0:16, 512:2560],
                              A["moe_router_e_w"][l].rearrange("(k p) g -> k (p g)", p=128)).then_inc(wr_in, 16)
            prows = A["state_pool"][0, 0].rearrange("r (k p) -> (r k) p", p=128)
            for a in range(2):
                eng.dma_start(pstrow[:, a, :], prows[a * 120:(a + 1) * 120, :]).then_inc(pst_in, 16)

            def rows(v, src):
                r0, q = (v % 8) * KD, v // 8
                eng.dma_start(prow[r0:r0 + src.shape[0], q, :], src).then_inc(prm_in, 16)
            rows(V_CW, A["lru_conv_w"].rearrange("l w (b p) -> (l w b) p", p=128))
            rows(V_CB, A["lru_conv_b"].rearrange("l (b p) -> (l b) p", p=128))
            rows(V_BA, A["lru_b_a"].rearrange("l h (b p) -> (l h b) p", p=128))
            rows(V_BX, A["lru_b_x"].rearrange("l h (b p) -> (l h b) p", p=128))
            rows(V_LAM, A["lru_lambda"].rearrange("l (b p) -> (l b) p", p=128))
            rows(V_LNG, A["ln_g"].rearrange("l j (b p) -> (l j b) p", p=128))
            rows(V_LNB, A["ln_b"].rearrange("l j (b p) -> (l j b) p", p=128))
            rows(V_SCALE, A["pool_scale"].rearrange("l (b p) -> (l b) p", p=128))
            rows(V_H0, A["state_lru_h"].rearrange("l n (b p) -> (l n b) p", p=128))
            rows(V_CONV0, A["state_lru_conv"].rearrange("l n w (b p) -> (l n w b) p", p=128))
            def evacuate_x(which, to_feature, part):
                for n in part:
                    if n % 2 and which in (0, 3):
                        continue
                    i, q = n // 4, n % 4
                    t0, m = TILES[i]
                    eng.wait_ge(tr_full[which], n + 1)
                    if to_feature:
                        o = xT[:, 4 * q:4 * q + 4, t0:t0 + m]
                        s = ps[:, 4 + n % 4, :].rearrange("p (k c) -> p k c", k=4)[:, :, 0:m]
                    else:
                        o = xtok[0:m, i, q * 512:(q + 1) * 512]
                        s = ps[0:m, 4 + n % 4, :]
                    eng.activation(o, s, ACT.Copy).then_inc(tr_act[which], 1)

            for l in two:
                eng.dma_start(brow[0:1, l, 0:4], A["moe_router_g_b"][l:l + 1, :]).then_inc(brow_in, 16)
                eng.dma_start(brow[0:1, l, 4:20], A["moe_router_e_b"][l:l + 1, :]).then_inc(brow_in, 16)

            for l in two:
                eng.wait_ge(init_tr, 1 + l)
                eng.activation(wrT[:, l, :, :].rearrange("p j k -> p (j k)"), ps[:, 1 + l, 0:320], ACT.Copy)\
                   .then_inc(init_cp, 1)
            eng.wait_ge(init_tr, 3)
            eng.activation(poolpre[:, :, :].rearrange("p r k -> p (r k)"), ps[:, 3, 0:KD * PW], ACT.Copy)\
               .then_inc(init_cp, 1)
            eng.wait_ge(init_tr, 4)
            eng.activation(prmT[:, 0:336], ps[:, 0, 0:336], ACT.Copy).then_inc(init_cp, 1)
            evacuate_x(0, True, range(12))
            eng.wait_ge(derived, 1)
            eng.activation(sp[1][:, :], sp[0][:, :], ACT.Exp, scale=-1.0).then_inc(lam_exp, 1)
            eng.activation(mark[0:1, 30:31], tiny[0:1, 0:1], ACT.Copy).then_inc(u_copied, 2)
            eng.activation(mark[0:1, 31:32], tiny[0:1, 0:1], ACT.Copy).then_inc(ri_read, 1)

            with eng.Fori(0, HEADS // 2) as it:
                for hh in range(2):
                    h = it * 2 + hh
                    eng.wait_ge(chunks_done, it * 6 + (3 * hh + 1))
                    eng.wait_ge(uext_free, it * 2 + (hh + 1))
                    for b in range(2):
                        eng.activation(uext[:, b, CW - 1:CW - 1 + TP], ps[:, b, 0:TP], ACT.Copy)
                        eng.activation(uext[:, b, TP + 2 * (CW - 1):UX], ps[:, b, TP:T], ACT.Copy)\
                           .then_inc(u_copied, 1)
                    eng.wait_ge(chunks_done, it * 6 + (3 * hh + 2))
                    eng.wait_ge(head_done, it * 2 + (hh + 1))
                    eng.activation(GS[:, :, 0:T], ps[:, 2:4, 0:T], ACT.Square).then_inc(gsq_ready, 1)
                    eng.wait_ge(gin_ready, it * 2 + (hh + 1))
                    eng.activation(GG[:, :, 0:T], GS[:, :, 0:T], ACT.Tanh, scale=0.7978845608028654)\
                       .then_inc(gtanh_ready, 1)
                    eng.wait_ge(chunks_done, it * 6 + (3 * hh + 3))
                    for b in range(2):
                        blk = h * 2 + b
                        eng.activation(TR[:, b, :], ps[:, 4 + b, 0:TG], ACT.Tanh, scale=0.5,
                                       bias=half_ba[:, bass.ds(blk, 1)])
                        last = eng.activation(TX[:, b, :], ps[:, 6 + b, 0:TG], ACT.Tanh, scale=0.5,
                                              bias=half_bx[:, bass.ds(blk, 1)])
                    last.then_inc(ri_read, 1)
                    eng.wait_ge(ri_read, it * 2 + (hh + 2))
                    for b in range(2):
                        blk = h * 2 + b
                        c = c_lam[:, bass.ds(blk, 1)]
                        eng.activation(AA[:, b, :], TR[:, b, :], ACT.Exp, scale=c, bias=c)
                        last = eng.activation(TL[:, b, :], TR[:, b, :], ACT.Tanh, scale=c, bias=c)
                    last.then_inc(decay_ready, 1)
                    eng.wait_ge(q_ready, it * 2 + (hh + 1))
                    eng.activation(TL[:, :, :], TL[:, :, :], ACT.Sqrt, scale=-1.0, bias=tiny[:, 0:1])\
                       .then_inc(mult_ready, 1)

            def layer_norm(n, vec):
                for k in range(KD):
                    if n in (0, 2):
                        eng.wait_ge(z_ready[n], k + 1)
                    elif k == 0:
                        eng.wait_ge(zall[n], 1)
                    if k >= 2:
                        eng.wait_ge(sq_used[n], k - 1)
                    eng.activation(sq[:, k % 2, :], z[:, k, :], ACT.Square).then_inc(sq_ready[n], 1)
                eng.wait_ge(var_ready[n], 1)
                eng.activation(rstd[:, :], rstd[:, :], ACT.Sqrt).then_inc(std_ready[n], 1)
                for k in range(KD):
                    if k % 4 == 0:
                        eng.wait_ge(norm_q[n], k // 4 + 1)
                    g, b = (V_LNG + vec) * KD + k, (V_LNB + vec) * KD + k
                    eng.activation(xT[:, k, :], z[:, k, :], ACT.Identity, scale=prmT[:, g:g + 1],
                                   bias=prmT[:, b:b + 1]).then_inc(x_ready[n], 1)

            def moe(l):
                evacuate_x(1 + l, False, range(0, 4))
                eng.wait_ge(ex_in[l], 1)
                eng.activation(r4[1][:, :, :], r4[0][:, :, :], ACT.Exp).then_inc(ex_out[l], 1)
                eng.wait_ge(ex_in[l], 2)
                eng.activation(r1[3][:, :, :], r1[2][:, :, :], ACT.Exp).then_inc(ex_out[l], 1)
                evacuate_x(1 + l, False, range(4, 12))
                if l == 0:
                    eng.wait_ge(cstT_full, 1)
                    eng.activation(cstT[:, :], ps[:, 2, 0:128], ACT.Copy).then_inc(cstT_ready, 1)
                    eng.wait_ge(cstT_ready, 1)
                    dst = [O["lru_conv_prompt"][0, 0, k] for k in range(3)] + [O["lru_conv_sample"][0, 0, k] for k in range(3)]
                    dst += [O["lru_h_prompt"][0, 0], O["lru_h_sample"][0, 0]]
                    for j, o in enumerate(dst):
                        eng.dma_start(o.rearrange("(b p) -> b p", p=128), cstT[j:128:8, :]).then_inc(out_st, 16)
                eng.wait_ge(route_ready[l], 1)
                n_win = eng.value_load(route_i[0:1, l, 0:1], min_val=NG, max_val=NG + MORE)
                base = C_MOE0 if l == 0 else C_MOE1
                done = DONE_MOE0 if l == 0 else DONE_MOE1
                with eng.Fori(0, n_win) as w:
                    seq = w if l == 0 else w + act_extra[0]

                    def high_parts(e, part):
                        n0 = base + WINDOW_POS["gu", e]
                        for q in part:
                            n, at = n0 + q // PARTS_CHUNK, q % PARTS_CHUNK
                            if at == 0:
                                eng.wait_ge(ring_ready[slot_of(n)], seq * 64 + ready_at(n))
                            eng.wait_ge(parts_used, seq * PARTS_WIN + ((l * NG + 0) * PARTS_WIN + e * PARTS_GU + q + 1))
                            eng.activation(whi[:, q % NPART, :], ring_at(n)[:, at * PART:(at + 1) * PART], ACT.Copy)\
                               .then_inc(hi_ready, 1)

                    def transposed(e):
                        eng.wait_ge(aux_full[l], w * 26 + (7 + e))
                        eng.activation(act[e % 2][:, :, :].rearrange("p f w -> p (f w)"), ps[:, 6 + e % 2, 0:KF * W],
                                       ACT.Copy).then_inc(aux_act[l], 1)

                    high_parts(0, range(NPART))
                    eng.wait_ge(aux_full[l], w * 26 + 1)
                    eng.activation(S[0:W, :], ps[0:W, 6, 0:T], ACT.Copy).then_inc(aux_act[l], 1)
                    eng.wait_ge(aux_full[l], w * 26 + 2)
                    eng.activation(gslot[0:W, :], ps[0:W, 7, 0:NE], ACT.Copy, scale=0.5).then_inc(aux_act[l], 1)
                    for q in range(4):
                        eng.wait_ge(aux_full[l], w * 26 + (3 + q))
                        eng.activation(xhi[:, 4 * q:4 * q + 4, :],
                                       ps[:, 6 + q % 2, 0:4 * W].rearrange("p (k w) -> p k w", k=4), ACT.Copy)\
                           .then_inc(xhi_ready[l], 1)
                    for e in range(NE):
                        high_parts(e, range(NPART if e == 0 else 0, PARTS_GU))
                        if e >= 1:
                            transposed(e - 1)
                        eng.wait_ge(parts_used, seq * PARTS_WIN + (l * NG * PARTS_WIN + NPART + (e + 1) * PARTS_GU))
                        eng.activation(th[0:W, :], ps[0:W, 0, :], ACT.Tanh, scale=0.5).then_inc(th_ready[l], 1)
                    transposed(3)
                    eng.wait_ge(chunks_done, seq * DN_WIN + (done + DN_WIN))
                    for b in range(2):
                        last = eng.activation(osb[0:W, b * 512:(b + 1) * 512], ps[0:W, 2 + b, :], ACT.Copy)
                    last.then_inc(o_act[l], 1)
                if l == 0:
                    act_extra.append(eng.snap(n_win - NG))

            act_extra = []
            layer_norm(0, 0)
            moe(0)
            layer_norm(1, 1)
            for q in range(4):
                eng.wait_ge(pst_full, q + 1)
                eng.activation(prow_out[:, q * 512:(q + 1) * 512], ps[0:PT, 4 + q, :], ACT.Copy)\
                   .then_inc(pst_copied, 1)
            eng.wait_ge(pst_copied, 4)
            eng.dma_start(O["pool_prompt"][0, 0], prow_out[0:PW, :]).then_inc(out_st, 16)
            eng.dma_start(O["pool_sample"][0, 0], prow_out[TS:PT, :]).then_inc(out_st, 16)
            layer_norm(2, 2)
            eng.wait_ge(out_st, 160)
            moe(1)
            layer_norm(3, 3)
            evacuate_x(3, False, range(12))
            eng.wait_ge(out_st, 160)

        @block.tensor
        def _(eng):
            mm = nc.tensor.matmul
            eng.wait_ge(consts, 7)
            def transpose_x(which, to_feature, part=range(12)):
                for n in part:
                    i, q = n // 4, n % 4
                    t0, m = TILES[i]
                    if to_feature and q == 0:
                        eng.wait_ge(x_in[i], 16)
                    if n >= 4 and which in (0, 3):
                        eng.wait_ge((tr_act if n % 2 == 0 else tr_dve)[which], (n - 4) // 2 + 1)
                    elif n >= 4:
                        eng.wait_ge(tr_act[which], n - 3)
                    for b in range(4):
                        k = 4 * q + b
                        if to_feature:
                            last = nc.tensor.transpose(ps[:, 4 + n % 4, b * 128:b * 128 + m],
                                                       xtok[0:m, i, k * 128:(k + 1) * 128], ident[0:m, 0:m])
                        else:
                            last = nc.tensor.transpose(ps[0:m, 4 + n % 4, b * 128:(b + 1) * 128],
                                                       xT[:, k, t0:t0 + m], ident[:, :])
                    last.then_inc(tr_full[which], 1)

            eng.wait_ge(wr_in, 64)
            for l in two:
                for j in range(20):
                    src = wrow[l][0][:, :, j] if j < 4 else wrow[l][1][:, :, j - 4]
                    last = nc.tensor.transpose(ps[:, 1 + l, j * 16:(j + 1) * 16], src, ident[0:16, 0:16])
                last.then_inc(init_tr, 1)
            eng.wait_ge(pst_in, 32)
            for a in range(2):
                last = nc.tensor.transpose(ps[:, 3, a * 120:(a + 1) * 120], pstrow[:, a, :], ident[0:120, 0:120])
            last.then_inc(init_tr, 1)
            eng.wait_ge(prm_in, 160)
            for q in range(3):
                r = 128 if q < 2 else 80
                last = nc.tensor.transpose(ps[:, 0, q * 128:q * 128 + r], prow[0:r, q, :], ident[0:r, 0:r])
            last.then_inc(init_tr, 1)

            transpose_x(0, True)

            eng.wait_ge(tr_act[0], 6)
            eng.wait_ge(tr_dve[0], 6)
            eng.wait_ge(init_cp, 4)
            with eng.Fori(0, HEADS // 2) as it:
                for hh in range(2):
                    for j in range(2):
                        n = 3 * hh + j
                        eng.wait_ge(ring_ready[slot_of(n)], it * (16 * dmas_of(n)) + ready_at(n))
                        if j == 1:
                            eng.wait_ge(gelu_done, it * 2 + (hh + 1))
                        wv = ring_at(n).rearrange("p (k c) -> p k c", c=256)
                        for b in range(2):
                            if j == 0:
                                eng.wait_ge(u_copied, it * 4 + (2 * hh + b + 1))
                            for k in range(KD):
                                last = mm(ps[:, 2 * j + b, 0:T], wv[:, k, b * 128:(b + 1) * 128], xT[:, k, :],
                                          start=(k == 0), stop=(k == KD - 1))
                        last.then_inc(chunks_done, 1)
                    n = 3 * hh + 2
                    eng.wait_ge(ring_ready[slot_of(n)], it * (16 * dmas_of(n)) + ready_at(n))
                    eng.wait_ge(uc_ready, it * 2 + (hh + 1))
                    eng.wait_ge(ri_read, it * 2 + (hh + 1))
                    wv = ring_at(n)[:, 0:1024].rearrange("p (a k j) -> p a k j", a=2, k=2)
                    for a in range(2):
                        for b in range(2):
                            for k in range(2):
                                last = mm(ps[:, 4 + 2 * a + b, 0:TG], wv[:, a, k, b * 128:(b + 1) * 128], UC[:, k, :],
                                          start=(k == 0), stop=(k == 1))
                    last.then_inc(chunks_done, 1)
            eng.wait_ge(head_done, HEADS + 1)
            for i in range(N_OUT):
                n = C_OUT + i
                eng.wait_ge(ring_ready[slot_of(n)], ready_at(n))
                if i >= 3:
                    eng.wait_ge(z_ready[0], 2 * (i - 2))
                wv = ring_at(n).rearrange("p (k c) -> p k c", c=256)
                for b in range(2):
                    for k in range(KD):
                        last = mm(ps[:, (2 * i + b) % 6, 0:T], wv[:, k, b * 128:(b + 1) * 128], yT[:, k, :],
                                  start=(k == 0), stop=(k == KD - 1))
                last.then_inc(chunks_done, 1)

            def layer_norm(n):
                for k in range(KD):
                    eng.wait_ge(sq_ready[n], k + 1)
                    mm(ps[:, 6, 0:T], onesd[:, :], sq[:, k % 2, :], start=(k == 0), stop=(k == KD - 1))\
                        .then_inc(sq_used[n], 1)
                eng.wait_ge(zsum_ready[n], 1)
                mm(ps[:, 7, 0:T], onesd[:, :], zsum[:, :], start=True, stop=True).then_inc(stat_done[n], 1)

            def moe(l):
                if l == 0:
                    eng.wait_ge(brow_in, 64)
                for i, (t0, m) in enumerate(TILES):
                    o = ps[0:m, 0, i * 32:i * 32 + 20]
                    mm(o, ones[0:1, 0:m], brow[0:1, l, :], start=True, stop=False)
                    for k in range(KD):
                        if i == 0:
                            eng.wait_ge(x_ready[2 * l], k + 1)
                        last = mm(o, xT[:, k, t0:t0 + m], wrT[:, l, :, k], start=False, stop=(k == KD - 1))
                last.then_inc(lg_done[l], 1)
                transpose_x(1 + l, False, range(4))
                eng.wait_ge(oh_ready[l], 1)
                for i in range(3):
                    for j in range(i + 1):
                        mm(ps[:, 1, i * 4:i * 4 + 4], (before if j == i else ones)[:, :], Gh[:, j, :],
                           start=(j == 0), stop=(j == i))
                for j in range(3):
                    last = mm(ps[:, 1, 16:20], ones[:, :], Gh[:, j, :], start=(j == 0), stop=(j == 2))
                last.then_inc(cnt_done[l], 1)
                transpose_x(1 + l, False, range(4, 12))
                if l == 0:
                    eng.wait_ge(cst_done, 1)
                    nc.tensor.transpose(ps[:, 2, 0:128], cst[:, :, :].rearrange("p b j -> p (b j)"), ident[:, :])\
                        .then_inc(cstT_full, 1)

                base = C_MOE0 if l == 0 else C_MOE1
                eng.wait_ge(tr_act[1 + l], 12)
                eng.wait_ge(route_ready[l], 1)
                n_win = eng.value_load(route_i[0:1, l, 0:1], min_val=NG, max_val=NG + MORE)
                with eng.Fori(0, n_win) as w:
                    seq = w if l == 0 else w + pe_extra[0]

                    def gate_up(e, chunks):
                        if chunks[0] == 0:
                            eng.wait_ge(gated[l], w * 4 + (e + 1))
                        for c in chunks:
                            if e == 0:
                                eng.wait_ge(aux_dve[l], w * 20 + (3 + c))
                            for q in range(c * PARTS_CHUNK, (c + 1) * PARTS_CHUNK):
                                k, half, buf = q // 2, q % 2, q % NPART
                                eng.wait_ge(lo_ready, seq * PARTS_WIN + (l * NG * PARTS_WIN + CREDIT + e * PARTS_GU + q + 1))
                                o = ps[0:W, half, :]
                                mm(o, xhi[:, k, :], whi[:, buf, :], start=(k == 0), stop=False)
                                mm(o, xlo[:, k, :], whi[:, buf, :], start=False, stop=False)
                                mm(o, xhi[:, k, :], wlo[:, buf, :], start=False, stop=(k == KD - 1))\
                                    .then_inc(parts_used, 1)

                    def transpose_act(e):
                        eng.wait_ge(gated[l], w * 4 + (e + 2))
                        if e < 2:
                            eng.wait_ge(aux_dve[l], w * 20 + (5 + e))
                        else:
                            eng.wait_ge(aux_act[l], w * 6 + (1 + e))
                        for f in range(KF):
                            last = nc.tensor.transpose(ps[:, 6 + e % 2, f * W:(f + 1) * W],
                                                       th[0:W, f * 128:(f + 1) * 128], ident[0:W, 0:W])
                        last.then_inc(aux_full[l], 1)

                    def down(e, chunks):
                        if chunks[0] == 0:
                            eng.wait_ge(aux_act[l], w * 6 + (3 + e))
                            if e == 0:
                                eng.wait_ge(o_act[l], w + 1)
                                eng.wait_ge(o_dve[l], w + 1)
                        for c in chunks:
                            n = base + WINDOW_POS["dn", e] + c
                            eng.wait_ge(ring_ready[slot_of(n)], seq * 64 + ready_at(n))
                            wv = ring_at(n).rearrange("p (k f) -> p k f", k=2)
                            for kk in range(2):
                                for j in range(4):
                                    last = mm(ps[0:W, 2 + j, :], act[e % 2][:, 2 * c + kk, :],
                                              wv[:, kk, j * 512:(j + 1) * 512],
                                              start=(e == 0 and c == 0 and kk == 0),
                                              stop=(e == 3 and c == 1 and kk == 1))
                            last.then_inc(chunks_done, 1)

                    eng.wait_ge(P_ready[l], w + 1)
                    eng.wait_ge(aux_dve[l], w * 20 + 1)
                    for i, (t0, m) in enumerate(TILES):
                        last = nc.tensor.transpose(ps[0:W, 6, t0:t0 + m], P[0:m, i, :], ident[0:m, 0:m])
                    last.then_inc(aux_full[l], 1)
                    eng.wait_ge(aux_dve[l], w * 20 + 2)
                    for i in range(3):
                        last = mm(ps[0:W, 7, 0:NE], P[:, i, :], gate4[:, i, :], start=(i == 0), stop=(i == 2))
                    last.then_inc(aux_full[l], 1)
                    for q in range(4):
                        if q < 2:
                            eng.wait_ge(aux_act[l], w * 6 + (1 + q))
                        else:
                            eng.wait_ge(aux_dve[l], w * 20 + (1 + q))
                        for b in range(4):
                            k = 4 * q + b
                            for i in range(3):
                                last = mm(ps[:, 6 + q % 2, b * W:(b + 1) * W], xtok[:, i, k * 128:(k + 1) * 128],
                                          P[:, i, :], start=(i == 0), stop=(i == 2))
                        last.then_inc(aux_full[l], 1)
                    gate_up(0, range(4))
                    for e in range(3):
                        gate_up(e + 1, range(3))
                        transpose_act(e)
                        gate_up(e + 1, range(3, 4))
                        if e < 2:
                            down(e, range(2))
                    down(2, range(1))
                    transpose_act(3)
                    down(2, range(1, 2))
                    down(3, range(2))
                    eng.wait_ge(o_act[l], w + 2)
                    eng.wait_ge(o_dve[l], w + 2)
                    for j in range(KD):
                        if j < 2:
                            eng.wait_ge(aux_act[l], w * 6 + (5 + j))
                        else:
                            eng.wait_ge(aux_dve[l], w * 20 + (5 + j))
                        mm(ps[:, 6 + j % 2, 0:T], osb[0:W, j * 128:(j + 1) * 128], S[0:W, :], start=True, stop=True)\
                            .then_inc(aux_full[l], 1)
                if l == 0:
                    pe_extra.append(eng.snap(n_win - NG))

            pe_extra = []
            layer_norm(0)
            moe(0)
            layer_norm(1)
            eng.wait_ge(x_ready[1], KD)
            for q in range(4):
                for b in range(4):
                    last = nc.tensor.transpose(ps[0:PT, 4 + q, b * 128:(b + 1) * 128], xT[:, 4 * q + b, T - PT:T],
                                               ident[:, :])
                last.then_inc(pst_full, 1)
            for g in range(NG):
                n = C_POOL + g
                eng.wait_ge(pool_diff, g + 1)
                eng.wait_ge(ring_ready[slot_of(n)], pe_extra[0] * 64 + ready_at(n))
                wv = ring_at(n)[:, 0:2048].rearrange("p (k j) -> p k j", k=4)
                if g >= 1:
                    eng.wait_ge(z_ready[2], 4 * g)
                for b in range(4):
                    for k in range(4):
                        last = mm(ps[:, b, 0:T], wv[:, k, b * 128:(b + 1) * 128], pdiff[g % 2][:, k, :],
                                  start=(k == 0), stop=(k == 3))
                last.then_inc(chunks_done, 1)
            eng.wait_ge(pst_copied, 4)
            layer_norm(2)
            moe(1)
            layer_norm(3)
            eng.wait_ge(x_ready[3], KD)
            transpose_x(3, False)

        @block.vector
        def _(eng):
            V = nc.vector
            link = SelfOrder(eng, vself)
            TS_, TT_, STT = V.tensor_scalar, V.tensor_tensor, V.scalar_tensor_tensor

            def evacuate_x(which, to_feature, part=range(12)):
                for n in part:
                    if n % 2 == 0:
                        continue
                    i, q = n // 4, n % 4
                    t0, m = TILES[i]
                    eng.wait_ge(tr_full[which], n + 1)
                    if to_feature:
                        o = xT[:, 4 * q:4 * q + 4, t0:t0 + m]
                        s = ps[:, 4 + n % 4, :].rearrange("p (k c) -> p k c", k=4)[:, :, 0:m]
                    else:
                        o = xtok[0:m, i, q * 512:(q + 1) * 512]
                        s = ps[0:m, 4 + n % 4, :]
                    V.tensor_copy(o, s).then_inc(tr_dve[which], 1)

            marks = []

            def signal(s, n=1):
                marks.append(0)
                c = len(marks)
                V.memset(mark[0:1, c:c + 1], 0.0).then_inc(s, n)

            V.memset(tiny[:, :], 1e-30)
            V.memset(uext[:, :, :], 0.0)
            V.memset(valid[:, 0:2, :], 1.0)
            link(V.memset(valid[:, 2, :], 0.0))
            link(V.memset(valid[0:32, 2, :], 1.0))
            eng.wait_ge(consts, 7)
            link(V.tensor_copy(iota_f[:, :], iota_i[:, :]))
            V.tensor_copy(gidx[:, :], iota_f[:, 0:4])
            TS_(firstw[:, :], iota_f[:, 0:4], -1.0, 4.0, ALU.mult, ALU.add)
            link(TS_(rcount[:, :], iota_f[:, 0:16], 1.0, None, ALU.add))
            link(V.reciprocal(rcount[:, :], rcount[:, :]))
            signal(uext_free, 1)
            signal(gelu_done, 1)
            signal(head_done, 1)
            for l in two:
                signal(aux_dve[l], 2)
                signal(gated[l], 1)
                signal(o_act[l], 1)
                signal(o_dve[l], 1)
            signal(lo_ready, CREDIT)
            signal(parts_used, NPART)
            eng.wait_ge(init_cp, 4)
            lam = prmT[:, V_LAM * KD:(V_LAM + 1) * KD]
            STT(sp[0][:, :], lam, -1.0, lam, ALU.mult, ALU.max).then_inc(derived, 1)
            TS_(half_ba[:, :], prmT[:, V_BA * KD:(V_BA + 1) * KD], 0.5, None, ALU.mult)
            TS_(half_bx[:, :], prmT[:, V_BX * KD:(V_BX + 1) * KD], 0.5, None, ALU.mult)
            evacuate_x(0, True)
            eng.wait_ge(lam_exp, 1)
            link(TS_(sp[2][:, :], sp[1][:, :], 2.0, None, ALU.add))
            link(V.reciprocal(sp[2][:, :], sp[2][:, :]))
            link(TT_(sp[1][:, :], sp[1][:, :], sp[2][:, :], ALU.mult))
            link(TT_(sp[2][:, :], sp[1][:, :], sp[1][:, :], ALU.mult))
            link(TS_(sp[3][:, :], sp[2][:, :], 1.0 / 15, None, ALU.mult))
            for q in (13, 11, 9, 7, 5, 3):
                link(STT(sp[3][:, :], sp[3][:, :], 1.0 / q, sp[2][:, :], ALU.add, ALU.mult))
            link(STT(sp[3][:, :], sp[3][:, :], 1.0, sp[1][:, :], ALU.add, ALU.mult))
            link(TS_(sp[2][:, :], lam, -1.0, 0.0, ALU.mult, ALU.max))
            link(STT(sp[3][:, :], sp[3][:, :], 2.0, sp[2][:, :], ALU.mult, ALU.add))
            TS_(c_lam[:, :], sp[3][:, :], -4.0, None, ALU.mult).then_inc(derived, 1)
            eng.wait_ge(derived, 2)

            with eng.Fori(0, HEADS // 2) as it:
                lk = SelfOrder(eng, vlru)
                lk.start(it, LRU_LINKS)
                for hh in range(2):
                    h = it * 2 + hh

                    def prm(v, b):
                        return prmT[:, bass.ds(h * 2 + (b + v * KD), 1)]
                    eng.wait_ge(u_copied, it * 4 + (2 * hh + 4))
                    pre = prmT[:, V_CONV0 * KD:(V_CONV0 + 3) * KD].rearrange("p (w k) -> p k w", w=3)
                    lk(V.tensor_copy(uext[:, :, TP + CW - 1:TP + 2 * (CW - 1)], pre[:, bass.ds(h * 2, 2), :]))
                    for b in range(2):
                        lk(TS_(UC[:, b, :], uext[:, b, 0:TG], prm(V_CW, b), prm(V_CB, b), ALU.mult, ALU.add))
                        for k in range(1, CW):
                            i = STT(UC[:, b, :], uext[:, b, k:k + TG], prm(V_CW + k, b), UC[:, b, :], ALU.mult, ALU.add)
                            if k == CW - 1 and b == 1:
                                i.then_inc(uc_ready, 1)
                            else:
                                lk(i)
                    eng.wait_ge(uc_ready, it * 2 + (hh + 1))
                    V.tensor_copy(cst[:, bass.ds(h * 2, 2), 0:3], uext[:, :, TP:TP + 3])
                    V.tensor_copy(cst[:, bass.ds(h * 2, 2), 3:6], uext[:, :, UX - 3:UX]).then_inc(uext_free, 1)
                    eng.wait_ge(gsq_ready, it * 2 + (hh + 1))
                    lk(TS_(GS[:, :, 0:T], GS[:, :, 0:T], 0.044715, 1.0, ALU.mult, ALU.add))
                    TT_(GS[:, :, 0:T], GS[:, :, 0:T], ps[:, 2:4, 0:T], ALU.mult).then_inc(gin_ready, 1)
                    eng.wait_ge(gtanh_ready, it * 2 + (hh + 1))
                    STT(GG[:, :, 0:T], GG[:, :, 0:T], 1.0, ps[:, 2:4, 0:T], ALU.add, ALU.mult).then_inc(gelu_done, 1)
                    eng.wait_ge(decay_ready, it * 2 + (hh + 1))
                    lk(TT_(GS[:, :, :], AA[:, :, :], AA[:, :, :], ALU.mult))
                    STT(TL[:, :, :], GS[:, :, :], 1.0, TL[:, :, :], ALU.add, ALU.mult).then_inc(q_ready, 1)
                    lk(STT(TX[:, :, :], TX[:, :, :], 1.0, UC[:, :, :], ALU.add, ALU.mult))
                    eng.wait_ge(mult_ready, it * 2 + (hh + 1))
                    lk(STT(TX[:, :, :], TX[:, :, :], 0.5, TL[:, :, :], ALU.mult, ALU.mult))
                    V.memset(AA[:, :, SEAM:SEAM + 1], 0.0)
                    lk(V.tensor_copy(TX[:, :, SEAM:SEAM + 1],
                                     prmT[:, bass.ds(h * 2 + V_H0 * KD, 2)].rearrange("p (b o) -> p b o", o=1)))
                    for b in range(2):
                        i = V.tensor_tensor_scan(TR[:, b, :], AA[:, b, :], TX[:, b, :], 0.0, ALU.mult, ALU.add)
                    lk(i)
                    V.tensor_copy(cst[:, bass.ds(h * 2, 2), 6:7], TR[:, :, TP - 1:TP])
                    V.tensor_copy(cst[:, bass.ds(h * 2, 2), 7:8], TR[:, :, TG - 1:TG])
                    STT(yT[:, bass.ds(h * 2, 2), 0:TP], GG[:, :, 0:TP], 0.5, TR[:, :, 0:TP], ALU.mult, ALU.mult)
                    STT(yT[:, bass.ds(h * 2, 2), TP:T], GG[:, :, TP:T], 0.5, TR[:, :, TG - TS:TG], ALU.mult, ALU.mult)\
                        .then_inc(head_done, 1)
                lk.check()
            signal(cst_done, 1)
            for i in range(N_OUT):
                eng.wait_ge(chunks_done, C_OUT + i + 1)
                for b in range(2):
                    k = 2 * i + b
                    STT(z[:, k, :], xT[:, k, :], ALPHA, ps[:, k % 6, 0:T], ALU.mult, ALU.add).then_inc(z_ready[0], 1)
            eng.wait_ge(z_ready[0], KD)
            eng.wait_ge(chunks_done, C_MOE0)

            def layer_norm(n):
                V.tensor_reduce(zsum[:, :], z[:, :, :].rearrange("p k t -> p t k"), AX.X, ALU.add)\
                    .then_inc(zsum_ready[n], 1)
                eng.wait_ge(stat_done[n], 1)
                link(V.tensor_copy(mean[:, :], ps[:, 7, 0:T]))
                link(TT_(nmr[:, :], mean[:, :], mean[:, :], ALU.mult))
                link(STT(nmr[:, :], ps[:, 6, 0:T], EPS, nmr[:, :], ALU.add, ALU.subtract))
                TS_(rstd[:, :], nmr[:, :], EPS * 0.5, None, ALU.max).then_inc(var_ready[n], 1)
                eng.wait_ge(std_ready[n], 1)
                link(V.reciprocal(rstd[:, :], rstd[:, :]))
                link(STT(nmr[:, :], mean[:, :], -1.0, rstd[:, :], ALU.mult, ALU.mult))
                for q in range(4):
                    zq = z[:, 4 * q:4 * q + 4, :]
                    link(TT_(zq, zq, rstd[:, :].unsqueeze(1).to_broadcast([128, 4, T]), ALU.mult))
                    TT_(zq, zq, nmr[:, :].unsqueeze(1).to_broadcast([128, 4, T]), ALU.add).then_inc(norm_q[n], 1)

            def bc(v, n):
                return v.to_broadcast([128, 3, n])

            def first_max(out, v, m, tmp, tmp1):
                link(V.tensor_reduce(m[:, :, 0], v[:, :, :], AX.X, ALU.max))
                link(TT_(tmp[:, :, :], v[:, :, :], bc(m[:, :, :], 4), ALU.is_equal))
                fw = firstw[:, :].unsqueeze(1).to_broadcast([128, 3, 4])
                link(TT_(tmp[:, :, :], tmp[:, :, :], fw, ALU.mult))
                link(V.tensor_reduce(tmp1[:, :, 0], tmp[:, :, :], AX.X, ALU.max))
                link(TT_(out[:, :, :], tmp[:, :, :], bc(tmp1[:, :, :], 4), ALU.is_equal))

            def moe(l):
                link(V.memset(logit[:, :, :], 0.0))
                eng.wait_ge(lg_done[l], 1)
                V.tensor_copy(logit[:, 0:2, :], ps[:, 0, 0:64].rearrange("p (i j) -> p i j", i=2)[:, :, 0:20])
                link(V.tensor_copy(logit[0:32, 2, :], ps[0:32, 0, 64:84]))
                lg = logit[:, :, 0:4]
                link(V.tensor_reduce(r1[0][:, :, 0], lg, AX.X, ALU.max))
                TT_(r4[0][:, :, :], lg, bc(r1[0][:, :, :], 4), ALU.subtract).then_inc(ex_in[l], 1)
                link(TT_(r4[2][:, :, :], lg, bc(r1[0][:, :, :], 4), ALU.is_equal))
                fw = firstw[:, :].unsqueeze(1).to_broadcast([128, 3, 4])
                link(TT_(r4[2][:, :, :], r4[2][:, :, :], fw, ALU.mult))
                link(V.tensor_reduce(r1[1][:, :, 0], r4[2][:, :, :], AX.X, ALU.max))
                link(TT_(Gh[:, :, :], r4[2][:, :, :], bc(r1[1][:, :, :], 4), ALU.is_equal))
                TT_(Gh[:, :, :], Gh[:, :, :], bc(valid[:, :, :], 4), ALU.mult).then_inc(oh_ready[l], 1)
                eng.wait_ge(oh_ready[l], 1)
                for i in range(3):
                    o = lprod[:, i, :].rearrange("p (g j) -> p g j", g=4)
                    ins = TT_(o, logit[:, i, 4:20].rearrange("p (g j) -> p g j", g=4),
                              Gh[:, i, :].unsqueeze(2).to_broadcast([128, 4, 4]), ALU.mult)
                link(ins)
                link(V.tensor_reduce(les[:, :, :], lprod[:, :, :].rearrange("p i (g j) -> p i j g", g=4), AX.X, ALU.add))
                first_max(E1, les, r1[0], r4[2], r1[1])
                link(STT(les[:, :, :], E1[:, :, :], -1e30, les[:, :, :], ALU.mult, ALU.add))
                first_max(gate4, les, r1[4], r4[2], r1[1])
                TT_(r1[2][:, :, :], r1[4][:, :, :], r1[0][:, :, :], ALU.subtract).then_inc(ex_in[l], 1)
                eng.wait_ge(ex_out[l], 1)
                link(V.tensor_reduce(r1[5][:, :, 0], r4[1][:, :, :], AX.X, ALU.add))
                eng.wait_ge(ex_out[l], 2)
                link(STT(r1[6][:, :, :], r1[3][:, :, :], 1.0, r1[5][:, :, :], ALU.add, ALU.mult))
                link(V.reciprocal(r1[6][:, :, :], r1[6][:, :, :]))
                link(TT_(r1[7][:, :, :], r1[6][:, :, :], r1[3][:, :, :], ALU.mult))
                link(TT_(gate4[:, :, :], gate4[:, :, :], bc(r1[7][:, :, :], 4), ALU.mult))
                link(TT_(E1[:, :, :], E1[:, :, :], bc(r1[6][:, :, :], 4), ALU.mult))
                link(TT_(gate4[:, :, :], gate4[:, :, :], E1[:, :, :], ALU.add))
                eng.wait_ge(cnt_done[l], 1)
                link(V.tensor_copy(n_g[:, :], ps[:, 1, 16:20]))
                link(TT_(r4[2][:, :, :], Gh[:, :, :], ps[:, 1, 0:12].rearrange("p (i g) -> p i g", i=3), ALU.mult))
                pos, k_w, first, tmp = r1[0], r1[1], r1[2], r1[4]
                link(V.tensor_reduce(pos[:, :, 0], r4[2][:, :, :], AX.X, ALU.add))
                link(TS_(k_w[:, :, :], pos[:, :, :], float(W), None, ALU.is_ge))
                link(TS_(more[:, :], n_g[:, :], float(W), None, ALU.is_gt))
                for m in range(2, -(-T // W)):
                    link(STT(k_w[:, :, :], pos[:, :, :], float(m * W), k_w[:, :, :], ALU.is_ge, ALU.add))
                    link(STT(more[:, :], n_g[:, :], float(m * W), more[:, :], ALU.is_gt, ALU.add))
                link(STT(pos[:, :, :], k_w[:, :, :], -float(W), pos[:, :, :], ALU.mult, ALU.add))
                link(V.memset(mbase[:, :], 0.0))
                for g in range(1, NG):
                    link(TT_(mbase[:, g:g + 1], mbase[:, g - 1:g], more[:, g - 1:g], ALU.add))
                g_w, m_w = r4[0], r4[3]
                link(TT_(g_w[:, :, :], Gh[:, :, :], gidx[:, :].unsqueeze(1).to_broadcast([128, 3, 4]), ALU.mult))
                link(TT_(m_w[:, :, :], Gh[:, :, :], mbase[:, :].unsqueeze(1).to_broadcast([128, 3, 4]), ALU.mult))
                link(V.tensor_reduce(first[:, :, 0], g_w[:, :, :], AX.X, ALU.add))
                link(V.tensor_reduce(tmp[:, :, 0], m_w[:, :, :], AX.X, ALU.add))
                link(STT(tmp[:, :, :], tmp[:, :, :], 3.0, k_w[:, :, :], ALU.add, ALU.add))
                link(TT_(tmp[:, :, :], tmp[:, :, :], first[:, :, :], ALU.subtract))
                link(TS_(k_w[:, :, :], k_w[:, :, :], 0.0, None, ALU.is_gt))
                link(TT_(tmp[:, :, :], tmp[:, :, :], k_w[:, :, :], ALU.mult))
                link(TT_(tmp[:, :, :], tmp[:, :, :], first[:, :, :], ALU.add))
                link(STT(slotno[:, :, :], tmp[:, :, :], float(W), pos[:, :, :], ALU.mult, ALU.add))
                link(STT(slotno[:, :, :], slotno[:, :, :], 1.0, valid[:, :, :], ALU.add, ALU.mult))
                link(TS_(slotno[:, :, :], slotno[:, :, :], -1.0, None, ALU.add))
                link(V.memset(route_f[:, :], 0.0))
                link(V.tensor_reduce(route_f[:, 0:1], more[:, :], AX.X, ALU.add))
                link(TS_(route_f[:, 0:1], route_f[:, 0:1], float(NG), None, ALU.add))
                link(TT_(more[:, :], more[:, :], mbase[:, :], ALU.add))
                for x in range(MORE):
                    link(TS_(t4[:, :], mbase[:, :], float(x), None, ALU.is_le))
                    link(TT_(t4[:, :], t4[:, :], gidx[:, :], ALU.mult))
                    link(STT(t4[:, :], more[:, :], float(x), t4[:, :], ALU.is_gt, ALU.mult))
                    link(V.tensor_reduce(route_f[:, 1 + x:2 + x], t4[:, :], AX.X, ALU.add))
                V.tensor_copy(route_i[0:1, l, :], route_f[0:1, :]).then_inc(route_ready[l], 1)
                def one_hot():
                    for i in range(3):
                        ins = TS_(P[:, i, :], iota_f[:, 0:W], slotno[:, i, :], None, ALU.is_equal)
                    return ins.then_inc(P_ready[l], 1)

                one_hot()
                eng.wait_ge(ax_ready[l], KD)
                eng.wait_ge(route_ready[l], 1)
                n_win = eng.value_load(route_i[0:1, l, 0:1], min_val=NG, max_val=NG + MORE)
                base = C_MOE0 if l == 0 else C_MOE1
                done = DONE_MOE0 if l == 0 else DONE_MOE1
                with eng.Fori(0, n_win) as w:
                    seq = w if l == 0 else w + dve_extra[0]
                    lk = SelfOrder(eng, vmoe[l])
                    lk.start(w, MOE_LINKS)

                    def low_parts(e, part):
                        n0 = base + WINDOW_POS["gu", e]
                        for q in part:
                            n, at = n0 + q // PARTS_CHUNK, q % PARTS_CHUNK
                            eng.wait_ge(hi_ready, seq * PARTS_WIN + (l * NG * PARTS_WIN + e * PARTS_GU + q + 1))
                            TT_(wlo[:, q % NPART, :], ring_at(n)[:, at * PART:(at + 1) * PART],
                                whi[:, q % NPART, :].bitcast(F32), ALU.subtract).then_inc(lo_ready, 1)

                    low_parts(0, range(NPART))
                    for q in range(4):
                        eng.wait_ge(xhi_ready[l], w * 4 + (q + 1))
                        TT_(xlo[:, 4 * q:4 * q + 4, :], ps[:, 6 + q % 2, 0:4 * W].rearrange("p (k w) -> p k w", k=4),
                            xhi[:, 4 * q:4 * q + 4, :].bitcast(F32), ALU.subtract).then_inc(aux_dve[l], 1)
                    for e in range(NE):
                        low_parts(e, range(NPART if e == 0 else 0, PARTS_GU))
                        eng.wait_ge(th_ready[l], w * 4 + (e + 1))
                        lk(STT(th[0:W, :], th[0:W, :], 1.0, ps[0:W, 0, :], ALU.add, ALU.mult))
                        if e == 0:
                            eng.wait_ge(aux_act[l], w * 6 + 2)
                        STT(th[0:W, :], th[0:W, :], gslot[0:W, e:e + 1], ps[0:W, 1, :], ALU.mult, ALU.mult)\
                            .then_inc(gated[l], 1)
                    lk(TS_(slotno[:, :, :], slotno[:, :, :], -float(W), None, ALU.add))
                    one_hot()
                    eng.wait_ge(P_ready[l], w + 2)
                    eng.wait_ge(chunks_done, seq * DN_WIN + (done + DN_WIN))
                    for b in range(2, 4):
                        ins = V.tensor_copy(osb[0:W, b * 512:(b + 1) * 512], ps[0:W, 2 + b, :])
                    ins.then_inc(o_dve[l], 1)
                    for j in range(KD):
                        eng.wait_ge(aux_full[l], w * 26 + (11 + j))
                        TT_(z[:, j, :], z[:, j, :], ps[:, 6 + j % 2, 0:T], ALU.add).then_inc(aux_dve[l], 1)
                    lk.check()
                signal(zall[1 + 2 * l], 1)
                eng.wait_ge(zall[1 + 2 * l], 1)
                if l == 0:
                    dve_extra.append(eng.snap(n_win - NG))

            def pool_add(g, extra):
                eng.wait_ge(pst_full, g + 1)
                link(TS_(z[:, 4 * g:4 * g + 4, :], xT[:, 4 * g:4 * g + 4, :], ALPHA, None, ALU.mult))
                eng.wait_ge(chunks_done, extra * DN_WIN + (DONE_POOL + g + 1))
                for b in range(4):
                    k = 4 * g + b
                    c = V_SCALE * KD + k
                    STT(z[:, k, :], ps[:, b, 0:T], prmT[:, c:c + 1], z[:, k, :], ALU.mult, ALU.add)\
                        .then_inc(z_ready[2], 1)

            dve_extra = []
            layer_norm(0)
            link(V.memset(xtok[:, 2, :], 0.0))
            moe(0)
            layer_norm(1)

            eng.wait_ge(x_ready[1], KD)
            Ls = PW + TP
            for g in range(NG):
                win = 2 << g
                blk = slice(4 * g, 4 * g + 4)
                V.memset(pext[:, :, 0:PW], 0.0)
                V.tensor_copy(pext[:, :, PW:Ls], xT[:, blk, 0:TP])
                V.tensor_copy(pext[:, :, Ls:Ls + PW], poolpre[:, :, blk].rearrange("p r k -> p k r"))
                link(V.tensor_copy(pext[:, :, Ls + PW:PX], xT[:, blk, TP:T]))
                src = pext
                for j in range(g + 1):
                    step = 1 << j
                    lo = 2 * step - 1
                    dst = (pa, pb)[j % 2]
                    link(TT_(dst[:, :, lo:PX], src[:, :, lo:PX], src[:, :, lo - step:PX - step], ALU.add))
                    src = dst
                if g >= 2:
                    eng.wait_ge(z_ready[2], 4 * (g - 1))
                pd = pdiff[g % 2]
                STT(pd[:, :, 0:TP], src[:, :, PW:Ls], 1.0 / win, xT[:, blk, 0:TP], ALU.mult, ALU.subtract)
                link(STT(pd[:, :, TP:T], src[:, :, Ls + PW:PX], 1.0 / win, xT[:, blk, TP:T], ALU.mult, ALU.subtract))
                rc = rcount[:, 0:win - 1].unsqueeze(1).to_broadcast([128, 4, win - 1])
                link(TT_(src[:, :, PW:PW + win - 1], src[:, :, PW:PW + win - 1], rc, ALU.mult))
                TT_(pd[:, :, 0:win - 1], src[:, :, PW:PW + win - 1], xT[:, blk, 0:win - 1], ALU.subtract)\
                    .then_inc(pool_diff, 1)
                eng.wait_ge(pool_diff, g + 1)
                if g >= 1:
                    pool_add(g - 1, dve_extra[0])
            pool_add(NG - 1, dve_extra[0])
            eng.wait_ge(z_ready[2], KD)
            layer_norm(2)
            link(V.memset(xtok[:, 2, :], 0.0))
            moe(1)
            layer_norm(3)
            evacuate_x(3, False)


_INS = ["x_prompt", "x_sample", "state_lru_h", "state_lru_conv", "state_pool", "lru_w_in", "lru_conv_w", "lru_conv_b",
        "lru_w_a", "lru_b_a", "lru_w_x", "lru_b_x", "lru_lambda", "lru_w_out", "pool_w", "pool_scale", "ln_g", "ln_b",
        "moe_router_g_w", "moe_router_g_b", "moe_router_e_w", "moe_router_e_b", "moe_w_gate_up", "moe_w_down"]
_OUTS = [("y_prompt", (1, TP, D)), ("y_sample", (1, TS, D)), ("lru_h_prompt", (1, 1, D)),
         ("lru_conv_prompt", (1, 1, CW - 1, D)), ("pool_prompt", (1, 1, PW, D)), ("lru_h_sample", (1, 1, D)),
         ("lru_conv_sample", (1, 1, CW - 1, D)), ("pool_sample", (1, 1, PW, D))]


def kernel(**inputs):
    import concourse.bacc as bacc
    from concourse.bass_utils import run_bass_kernel_spmd as run

    nc = bacc.Bacc("TRN2", target_bir_lowering=False, num_devices=1)
    arrays = {f"in_{name}": np.ascontiguousarray(inputs[name]) for name in _INS}
    A = {name: nc.dram_tensor(f"in_{name}", arrays[f"in_{name}"].shape, F32, kind="ExternalInput").ap() for name in _INS}
    O = {name: nc.dram_tensor(f"out_{name}", shape, F32, kind="ExternalOutput").ap() for name, shape in _OUTS}
    encoder_step(nc, A, O)
    r = run(nc, [arrays], core_ids=[0])
    return tuple(r.results[0][f"out_{name}"] for name, _ in _OUTS)
```

```python
import numpy as np
import concourse.bass as bass
from concourse import mybir
from contextlib import ExitStack

F32 = mybir.dt.float32
F32R = mybir.dt.float32r
I32 = mybir.dt.int32
ALU = mybir.AluOpType
ACT = mybir.ActivationFunctionType
AX = mybir.AxisListType

D = 2048
KD = D // 128
TP, TS = 256, 32
T = TP + TS
TILES = [(0, 128), (128, 128), (256, 32)]
HEADS = 8
CW = 4
TG = TP + TS + CW - 1
SEAM = TP + CW - 2
UX = TG + CW - 1
NG, NE = 4, 4
FE = 512
KF = FE // 128
W = 96
MORE = T // (W + 1)
PW = 15
PT = TS + PW
ALPHA = 4.0 ** 0.25
EPS = 1e-5
NSLOT, SLOT = 6, 4096
SLOT0 = 4
C_OUT = 3 * HEADS
N_OUT = 8
C_MOE0 = C_OUT + N_OUT
PER_WIN = 24
C_POOL = C_MOE0 + NG * PER_WIN
C_MOE1 = C_POOL + NG
NPART, PART = 4, 512
PARTS_CHUNK = SLOT // PART
PARTS_WIN = PER_WIN * PARTS_CHUNK
PARTS_OUT = N_OUT * PARTS_CHUNK
WINDOW_ORDER = [("gu", 0), ("gu", 1), ("dn", 0), ("gu", 2), ("dn", 1), ("gu", 3), ("dn", 2), ("dn", 3)]
CHUNKS_OF = {"gu": 4, "dn": 2}
WINDOW_POS = {we: sum(CHUNKS_OF[k] for k, _ in WINDOW_ORDER[:i]) for i, we in enumerate(WINDOW_ORDER)}
WINDOW_PARTS = [(kind, e, q) for kind, e in WINDOW_ORDER for q in range(CHUNKS_OF[kind] * PARTS_CHUNK)]
GU_END = [(WINDOW_POS["gu", e] + CHUNKS_OF["gu"]) * PARTS_CHUNK for e in range(NE)]
SILU_AT = {end + NPART - 1: e for e, end in enumerate(GU_END)}
TRANSPOSE_AT = {end + PARTS_CHUNK: e for e, end in enumerate(GU_END)}
ACT_AT = {end + PARTS_CHUNK + NPART - 1: e for e, end in enumerate(GU_END)}


def gate_bank(e):
    return 2 if e == 0 else 0
V_CW, V_CB, V_BA, V_BX, V_LAM, V_LNG, V_LNB, V_SCALE, V_H0, V_CONV0 = 0, 4, 5, 6, 7, 8, 12, 16, 17, 18


def parts_base(l):
    return PARTS_OUT + l * NG * PARTS_WIN


def slot_of(n):
    return (n + SLOT0) % NSLOT


def dmas_of(n):
    return 2 if n < C_OUT and n % 3 == 2 else 1


def ready_at(n):
    return 16 * sum(dmas_of(m) for m in range(n % NSLOT, n + 1, NSLOT))


LRU_LINKS = 28
MOE_LINKS = 5
CREDIT = NSLOT * PARTS_CHUNK


class SelfOrder:

    def __init__(self, eng, sem):
        self.eng, self.sem, self.n, self.i, self.per = eng, sem, 0, None, 0

    def start(self, i, per):
        self.i, self.per, self.n = i, per, 0

    def __call__(self, ins):
        self.n += 1
        ins.then_inc(self.sem, 1)
        self.eng.wait_ge(self.sem, self.n if self.i is None else self.i * self.per + self.n)

    def check(self):
        assert self.n == self.per, (self.n, self.per)


def encoder_step(nc, A, O):
    ctx = ExitStack()
    with ctx:
        def sb(name, shape, dt=F32):
            return ctx.enter_context(nc.sbuf_tensor(name, shape, dt))

        def sem(name):
            return ctx.enter_context(nc.semaphore(name))

        ring = sb("ring", [128, NSLOT, SLOT])
        xT = sb("xT", [128, KD, T])
        z = xT
        with nc.sbuf_tensor("ylo", [128, KD, T], F32R) as ylo:
            pass
        xtok = sb("xtok", [128, 3, D])
        arena = sb("arena", [128, 12 * TG])
        prmT = sb("prmT", [128, 24 * KD])
        wrT = sb("wrT", [128, 2, 20, KD])
        brow = sb("brow", [1, 2, 20])
        ident = sb("ident", [128, 128])
        ones = sb("ones", [128, 128])
        onesd = sb("onesd", [128, 128])
        before = sb("before", [128, 128])
        iota_i = sb("iota_i", [128, 128], I32)
        iota_f = sb("iota_f", [128, 128])
        valid = sb("valid", [128, 3, 1])
        rcount = sb("rcount", [128, 16])
        poolpre = sb("poolpre", [128, PW, KD])
        cst = sb("cst", [128, KD, 8])
        cstT = sb("cstT", [128, 128])
        half_ba = sb("half_ba", [128, KD])
        half_bx = sb("half_bx", [128, KD])
        c_lam = sb("c_lam", [128, KD])
        sp = [sb(f"sp{i}", [128, KD]) for i in range(4)]
        tiny = sb("tiny", [128, 1])
        mark = sb("mark", [1, 32])
        uext = sb("uext", [128, 2, UX])
        sqm = sb("sqm", [128, 2 * TG])
        sq = sqm[:, 0:2 * T].rearrange("p (a t) -> p a t", a=2)
        mean = sb("mean", [128, T])
        rstd = sb("rstd", [128, T])
        nmr = sb("nmr", [128, T])
        zsum = sb("zsum", [128, T])
        logit = sb("logit", [128, 3, 20])
        r4 = [sb(f"r4_{i}", [128, 3, 4]) for i in range(4)]
        Gh = sb("Gh", [128, 3, 4])
        E1 = sb("E1", [128, 3, 4])
        gate4 = sb("gate4", [128, 3, 4])
        les = sb("les", [128, 3, 4])
        lprod = sb("lprod", [128, 3, 16])
        r1 = [sb(f"r1_{i}", [128, 3, 1]) for i in range(8)]
        gidx = sb("gidx", [128, 4])
        firstw = sb("firstw", [128, 4])
        n_g = sb("n_g", [128, 4])
        more = sb("more", [128, 4])
        mbase = sb("mbase", [128, 4])
        t4 = sb("t4", [128, 4])
        slotno = sb("slotno", [128, 3, 1])
        route_f = sb("route_f", [128, 8])
        route_i = sb("route_i", [1, 2, 8], I32)
        ps = ctx.enter_context(nc.psum_tensor("ps", [128, 8, 512], F32))

        def carve(tensor, at, *shape):
            n = int(np.prod(shape))
            v = tensor[:, at:at + n]
            names = " ".join("abc"[:len(shape)])
            kw = {"abc"[i]: s for i, s in enumerate(shape[1:], 1)}
            return v.rearrange(f"p ({names}) -> p {names}", **kw) if len(shape) > 1 else v

        whi = sb("whi", [128, NPART, PART], F32R)
        wlo = sb("wlo", [128, NPART, PART], F32R)
        operands = sb("operands", [128, max(KD * T, 2 * KD * W + 4 * KF * W)], F32R)
        yhi = carve(operands, 0, KD, T)
        xhi, xlo = [carve(operands, i * KD * W, KD, W) for i in range(2)]
        acthi, actlo = [carve(operands, 2 * KD * W + i * 2 * KF * W, 2, KF * W) for i in range(2)]
        osb = carve(arena, 0, D)
        th = carve(arena, 2048, FE)
        P = carve(arena, 2560, 3, W)
        S = carve(arena, 2848, T)
        gslot = carve(arena, 3136, NE)
        prow = carve(sqm, 0, 3, 128)
        xTf = xT[:, :, :].rearrange("p k t -> p (k t)")
        wbase = [arena, xTf]
        wrow = [(b[0:16, 0:512].rearrange("k (p g) -> k p g", g=4),
                 b[0:16, 512:2560].rearrange("k (p g) -> k p g", g=16)) for b in wbase]
        pstrow = arena[0:120, 2560:2816].rearrange("r (a p) -> r a p", a=2)
        prow_out = arena[0:PT, 0:D]
        UC, GG, GS, TR, TX, AA = [carve(arena, i * 2 * TG, 2, TG) for i in range(6)]
        TL = carve(sqm, 0, 2, TG)
        xtf = xtok[:, :, :].rearrange("p i d -> p (i d)")
        yT = carve(xtf, 0, KD, T)
        PX = PW + TP + PW + TS
        pext, pa, pb = [carve(xtf, i * 4 * PX, 4, PX) for i in range(3)]
        pdiff = [carve(xtf, 12 * PX + i * 4 * T, 4, T) for i in range(2)]

        x_in = [sem(f"x_in{i}") for i in range(3)]
        prm_in, wr_in, pst_in, brow_in = sem("prm_in"), sem("wr_in"), sem("pst_in"), sem("brow_in")
        consts = sem("consts")
        ring_ready = [sem(f"ring_ready{i}") for i in range(NSLOT)]
        chunks_done = sem("chunks_done")
        hi_ready, lo_ready, parts_used = sem("hi_ready"), sem("lo_ready"), sem("parts_used")
        init_tr = sem("init_tr")
        init_cp = sem("init_cp")
        derived = sem("derived")
        lam_exp = sem("lam_exp")
        vself = sem("vself")
        tr_full = [sem(f"tr_full{i}") for i in range(4)]
        tr_act = [sem(f"tr_act{i}") for i in range(4)]
        tr_dve = [sem(f"tr_dve{i}") for i in range(4)]
        u_copied, uext_free, uc_ready = sem("u_copied"), sem("uext_free"), sem("uc_ready")
        gsq_ready, gin_ready, gtanh_ready, gelu_done = sem("gsq"), sem("gin"), sem("gtanh"), sem("gelu_done")
        ri_read, decay_ready, q_ready, mult_ready = sem("ri_read"), sem("decay_ready"), sem("q_ready"), sem("mult")
        head_done = sem("head_done")
        yhi_ready, ylo_ready = sem("yhi_ready"), sem("ylo_ready")
        vlru = sem("vlru")
        z_ready = [sem(f"z_ready{i}") for i in range(4)]
        zall = [sem(f"zall{i}") for i in range(4)]
        sq_ready = [sem(f"sq_ready{i}") for i in range(4)]
        sq_used = [sem(f"sq_used{i}") for i in range(4)]
        zsum_ready = [sem(f"zsum_ready{i}") for i in range(4)]
        stat_done = [sem(f"stat_done{i}") for i in range(4)]
        var_ready = [sem(f"var_ready{i}") for i in range(4)]
        std_ready = [sem(f"std_ready{i}") for i in range(4)]
        norm_q = [sem(f"norm_q{i}") for i in range(4)]
        x_ready = [sem(f"x_ready{i}") for i in range(4)]
        ax_ready = [sem(f"ax_ready{i}") for i in range(2)]
        two = range(2)
        lg_done = [sem(f"lg_done{i}") for i in two]
        ex_in = [sem(f"ex_in{i}") for i in two]
        ex_out = [sem(f"ex_out{i}") for i in two]
        oh_ready = [sem(f"oh_ready{i}") for i in two]
        cnt_done = [sem(f"cnt_done{i}") for i in two]
        route_ready = [sem(f"route_ready{i}") for i in two]
        P_ready = [sem(f"P_ready{i}") for i in two]
        aux_full = [sem(f"aux_full{i}") for i in two]
        aux_act = [sem(f"aux_act{i}") for i in two]
        aux_dve = [sem(f"aux_dve{i}") for i in two]
        th_ready = [sem(f"th_ready{i}") for i in two]
        gated = [sem(f"gated{i}") for i in two]
        actlo_ready = [sem(f"actlo_ready{i}") for i in two]
        xhi_ready = [sem(f"xhi_ready{i}") for i in two]
        o_act = [sem(f"o_act{i}") for i in two]
        o_dve = [sem(f"o_dve{i}") for i in two]
        vmoe = [sem(f"vmoe{i}") for i in two]
        cst_done, cstT_full, cstT_ready = sem("cst_done"), sem("cstT_full"), sem("cstT_ready")
        pst_full, pst_copied = sem("pst_full"), sem("pst_copied")
        pool_diff = sem("pool_diff")
        out_st, out_y = sem("out_st"), sem("out_y")

        w_in = A["lru_w_in"][0].rearrange("(k p) e -> p k e", p=128)
        w_a = A["lru_w_a"].rearrange("l h i j -> (l h i j)")
        w_x = A["lru_w_x"].rearrange("l h i j -> (l h i j)")
        w_out = A["lru_w_out"][0].rearrange("(k p) e -> p k e", p=128)
        pool_w = A["pool_w"][0].rearrange("g (k p) j -> g p k j", p=128)
        gu_w = [A["moe_w_gate_up"][l].rearrange("e d f -> (e d f)") for l in two]
        dn_w = [A["moe_w_down"][l].rearrange("e f d -> (e f d)") for l in two]

        def ring_at(n):
            return ring[:, slot_of(n), :]

        block = ctx.enter_context(nc.Block())

        @block.sync
        def _(eng):
            xp, xs = A["x_prompt"][0], A["x_sample"][0]
            for i, (t0, m) in enumerate(TILES):
                src = xp[t0:t0 + m, :] if t0 < TP else xs
                eng.dma_start(xtok[0:m, i, :], src).then_inc(x_in[i], 16)

            def lru_head(h, hh, it):
                for j in range(3):
                    n = 3 * hh + j
                    dst = ring_at(n)
                    if j < 2:
                        col = h * 256 + (D if j == 0 else 0)
                        if it is not None:
                            need = eng.snap(it * 6 + (n - NSLOT + 1))
                            eng.wait_ge(chunks_done, need)
                            col = h * 256 + D if j == 0 else it * 512 + hh * 256
                        eng.dma_start(dst.rearrange("p (k c) -> p k c", c=256), w_in[:, :, bass.ds(col, 256)])\
                           .then_inc(ring_ready[slot_of(n)], 16)
                    else:
                        if it is not None:
                            need = eng.snap(it * 6 + (n - NSLOT + 1))
                            eng.wait_ge(chunks_done, need)
                        for a, w in enumerate((w_a, w_x)):
                            src = w[bass.ds(h * (256 * 256), 256 * 256)]\
                                .rearrange("(k p j) -> p k j", k=2, p=128)
                            eng.dma_start(dst[:, a * 512:(a + 1) * 512].rearrange("p (k j) -> p k j", k=2), src)\
                               .then_inc(ring_ready[slot_of(n)], 16)

            for hh in range(2):
                lru_head(hh, hh, None)
            with eng.Fori(2, HEADS // 2 + 1) as after:
                it = after - 1
                for hh in range(2):
                    lru_head(eng.snap(it * 2 + hh), hh, it)
            for i in range(N_OUT):
                n = C_OUT + i
                if i < NSLOT:
                    eng.wait_ge(chunks_done, n - NSLOT + 1)
                else:
                    eng.wait_ge(lo_ready, CREDIT + (i - NSLOT + 1) * PARTS_CHUNK)
                eng.dma_start(ring_at(n).rearrange("p (k c) -> p k c", c=256), w_out[:, :, i * 256:(i + 1) * 256])\
                   .then_inc(ring_ready[slot_of(n)], 16)

            def parts_before(l, p):
                return CREDIT + parts_base(l) + p * PARTS_CHUNK

            def window_loads(l, group, seq, base, first=False):
                def snap(v):
                    return v if isinstance(v, int) else eng.snap(v)
                n = base
                for kind, e in WINDOW_ORDER:
                    for c in range(CHUNKS_OF[kind]):
                        w, per_expert, k = (gu_w[l], D * 2 * FE, 4) if kind == "gu" else (dn_w[l], FE * D, 2)
                        at = snap(group * (NE * per_expert) + (e * per_expert + c * 128 * SLOT))
                        p = n - base
                        if p >= NSLOT:
                            eng.wait_ge(lo_ready, snap(seq * PARTS_WIN + parts_before(l, p - NSLOT + 1)))
                        elif first and l == 1 and p >= NSLOT - NG:
                            eng.wait_ge(chunks_done, C_OUT + (p - 1))
                        else:
                            last = p - NSLOT + (NG if first and l == 1 else 0)
                            eng.wait_ge(lo_ready, snap(seq * PARTS_WIN + parts_before(l, last + 1)))
                        src = w[bass.ds(at, 128 * SLOT)].rearrange("(k p f) -> p k f", k=k, p=128)
                        dst = ring_at(n).rearrange("p (k f) -> p k f", k=k)
                        eng.dma_start(dst, src).then_inc(ring_ready[slot_of(n)], 16)
                        n += 1

            extra = 0
            for l, base in enumerate((C_MOE0, C_MOE1)):
                if l == 1:
                    for g in range(NG):
                        n = C_POOL + g
                        need = eng.snap(extra * PARTS_WIN + parts_before(1, g - NSLOT + 1))
                        eng.wait_ge(lo_ready, need)
                        eng.dma_start(ring_at(n)[:, 0:2048].rearrange("p (k j) -> p k j", k=4), pool_w[g])\
                           .then_inc(ring_ready[slot_of(n)], 16)
                window_loads(l, 0, extra, base, first=True)
                with eng.Fori(1, NG) as w:
                    window_loads(l, eng.snap(w + 0), eng.snap(w + extra), base)
                eng.wait_ge(route_ready[l], 1)
                n_win = eng.value_load(route_i[0:1, l, 0:1], min_val=NG, max_val=NG + MORE)
                with eng.If(n_win > NG):
                    with eng.Fori(NG, n_win) as w:
                        g = eng.value_load(route_i[0:1, l, bass.ds(w - (NG - 1), 1)], min_val=0, max_val=NG - 1)
                        window_loads(l, g, eng.snap(w + extra), base)
                with eng.Else():
                    eng.nop()
                if l == 0:
                    extra = eng.snap(n_win - NG)
            eng.wait_ge(tr_act[3], 6)
            eng.wait_ge(tr_dve[3], 6)
            for i, (t0, m) in enumerate(TILES):
                dst = O["y_prompt"][0, t0:t0 + m, :] if t0 < TP else O["y_sample"][0]
                eng.dma_start(dst, xtok[0:m, i, :]).then_inc(out_y, 16)
            eng.wait_ge(out_y, 48)

        @block.gpsimd
        def _(eng):
            eng.memset(ident[:, :], 0.0).then_inc(consts, 1)
            eng.memset(before[:, :], 1.0).then_inc(consts, 1)
            eng.memset(ones[:, :], 1.0).then_inc(consts, 1)
            eng.memset(onesd[:, :], 1.0 / D).then_inc(consts, 1)
            eng.wait_ge(consts, 4)
            eng.affine_select(out=ident[:, :], in_=ident[:, :], compare_op=ALU.not_equal, fill=1.0, base=0,
                              pattern=[[-1, 128]], channel_multiplier=1).then_inc(consts, 1)
            eng.affine_select(out=before[:, :], in_=before[:, :], compare_op=ALU.is_gt, fill=0.0, base=0,
                              pattern=[[1, 128]], channel_multiplier=-1).then_inc(consts, 1)
            eng.iota(iota_i[:, :], pattern=[[1, 128]], base=0, channel_multiplier=0).then_inc(consts, 1)
            for l in two:
                eng.wait_ge(tr_full[1 + l], 12)
                for k in range(KD):
                    eng.tensor_scalar(xT[:, k, :], xT[:, k, :], ALPHA, None, ALU.mult).then_inc(ax_ready[l], 1)

        @block.scalar
        def _(eng):
            for l in two:
                eng.dma_start(wbase[l][0:16, 0:512],
                              A["moe_router_g_w"][l].rearrange("(k p) g -> k (p g)", p=128)).then_inc(wr_in, 16)
                eng.dma_start(wbase[l][0:16, 512:2560],
                              A["moe_router_e_w"][l].rearrange("(k p) g -> k (p g)", p=128)).then_inc(wr_in, 16)
            prows = A["state_pool"][0, 0].rearrange("r (k p) -> (r k) p", p=128)
            for a in range(2):
                eng.dma_start(pstrow[:, a, :], prows[a * 120:(a + 1) * 120, :]).then_inc(pst_in, 16)

            def rows(v, src):
                r0, q = (v % 8) * KD, v // 8
                eng.dma_start(prow[r0:r0 + src.shape[0], q, :], src).then_inc(prm_in, 16)
            rows(V_CW, A["lru_conv_w"].rearrange("l w (b p) -> (l w b) p", p=128))
            rows(V_CB, A["lru_conv_b"].rearrange("l (b p) -> (l b) p", p=128))
            rows(V_BA, A["lru_b_a"].rearrange("l h (b p) -> (l h b) p", p=128))
            rows(V_BX, A["lru_b_x"].rearrange("l h (b p) -> (l h b) p", p=128))
            rows(V_LAM, A["lru_lambda"].rearrange("l (b p) -> (l b) p", p=128))
            rows(V_LNG, A["ln_g"].rearrange("l j (b p) -> (l j b) p", p=128))
            rows(V_LNB, A["ln_b"].rearrange("l j (b p) -> (l j b) p", p=128))
            rows(V_SCALE, A["pool_scale"].rearrange("l (b p) -> (l b) p", p=128))
            rows(V_H0, A["state_lru_h"].rearrange("l n (b p) -> (l n b) p", p=128))
            rows(V_CONV0, A["state_lru_conv"].rearrange("l n w (b p) -> (l n w b) p", p=128))
            def evacuate_x(which, to_feature, part):
                for n in part:
                    if n % 2 and which in (0, 3):
                        continue
                    i, q = n // 4, n % 4
                    t0, m = TILES[i]
                    eng.wait_ge(tr_full[which], n + 1)
                    if to_feature:
                        o = xT[:, 4 * q:4 * q + 4, t0:t0 + m]
                        s = ps[:, 4 + n % 4, :].rearrange("p (k c) -> p k c", k=4)[:, :, 0:m]
                    else:
                        o = xtok[0:m, i, q * 512:(q + 1) * 512]
                        s = ps[0:m, 4 + n % 4, :]
                    eng.activation(o, s, ACT.Copy).then_inc(tr_act[which], 1)

            for l in two:
                eng.dma_start(brow[0:1, l, 0:4], A["moe_router_g_b"][l:l + 1, :]).then_inc(brow_in, 16)
                eng.dma_start(brow[0:1, l, 4:20], A["moe_router_e_b"][l:l + 1, :]).then_inc(brow_in, 16)

            for l in two:
                eng.wait_ge(init_tr, 1 + l)
                eng.activation(wrT[:, l, :, :].rearrange("p j k -> p (j k)"), ps[:, 1 + l, 0:320], ACT.Copy)\
                   .then_inc(init_cp, 1)
            eng.wait_ge(init_tr, 3)
            eng.activation(poolpre[:, :, :].rearrange("p r k -> p (r k)"), ps[:, 3, 0:KD * PW], ACT.Copy)\
               .then_inc(init_cp, 1)
            eng.wait_ge(init_tr, 4)
            eng.activation(prmT[:, 0:336], ps[:, 0, 0:336], ACT.Copy).then_inc(init_cp, 1)
            evacuate_x(0, True, range(12))
            eng.wait_ge(derived, 1)
            eng.activation(sp[1][:, :], sp[0][:, :], ACT.Exp, scale=-1.0).then_inc(lam_exp, 1)
            eng.activation(mark[0:1, 30:31], tiny[0:1, 0:1], ACT.Copy).then_inc(u_copied, 2)
            eng.activation(mark[0:1, 31:32], tiny[0:1, 0:1], ACT.Copy).then_inc(ri_read, 1)

            with eng.Fori(0, HEADS // 2) as it:
                for hh in range(2):
                    h = it * 2 + hh
                    eng.wait_ge(chunks_done, it * 6 + (3 * hh + 1))
                    eng.wait_ge(uext_free, it * 2 + (hh + 1))
                    for b in range(2):
                        eng.activation(uext[:, b, CW - 1:CW - 1 + TP], ps[:, b, 0:TP], ACT.Copy)
                        eng.activation(uext[:, b, TP + 2 * (CW - 1):UX], ps[:, b, TP:T], ACT.Copy)\
                           .then_inc(u_copied, 1)
                    eng.wait_ge(chunks_done, it * 6 + (3 * hh + 2))
                    eng.wait_ge(head_done, it * 2 + (hh + 1))
                    eng.activation(GS[:, :, 0:T], ps[:, 2:4, 0:T], ACT.Square).then_inc(gsq_ready, 1)
                    eng.wait_ge(gin_ready, it * 2 + (hh + 1))
                    eng.activation(GG[:, :, 0:T], GS[:, :, 0:T], ACT.Tanh, scale=0.7978845608028654)\
                       .then_inc(gtanh_ready, 1)
                    eng.wait_ge(chunks_done, it * 6 + (3 * hh + 3))
                    for b in range(2):
                        blk = h * 2 + b
                        eng.activation(TR[:, b, :], ps[:, 4 + b, 0:TG], ACT.Tanh, scale=0.5,
                                       bias=half_ba[:, bass.ds(blk, 1)])
                        last = eng.activation(TX[:, b, :], ps[:, 6 + b, 0:TG], ACT.Tanh, scale=0.5,
                                              bias=half_bx[:, bass.ds(blk, 1)])
                    last.then_inc(ri_read, 1)
                    eng.wait_ge(ri_read, it * 2 + (hh + 2))
                    for b in range(2):
                        blk = h * 2 + b
                        c = c_lam[:, bass.ds(blk, 1)]
                        eng.activation(AA[:, b, :], TR[:, b, :], ACT.Exp, scale=c, bias=c)
                        last = eng.activation(TL[:, b, :], TR[:, b, :], ACT.Tanh, scale=c, bias=c)
                    last.then_inc(decay_ready, 1)
                    eng.wait_ge(q_ready, it * 2 + (hh + 1))
                    eng.activation(TL[:, :, :], TL[:, :, :], ACT.Sqrt, scale=-1.0, bias=tiny[:, 0:1])\
                       .then_inc(mult_ready, 1)

            for part in range(PARTS_OUT):
                n, at = C_OUT + part // PARTS_CHUNK, part % PARTS_CHUNK
                if part == NPART:
                    eng.wait_ge(head_done, HEADS + 1)
                    for k in range(KD):
                        eng.activation(yhi[:, k, :], yT[:, k, :], ACT.Copy).then_inc(yhi_ready, 1)
                if at == 0:
                    eng.wait_ge(ring_ready[slot_of(n)], ready_at(n))
                eng.wait_ge(parts_used, part + 1)
                eng.activation(whi[:, part % NPART, :], ring_at(n)[:, at * PART:(at + 1) * PART], ACT.Copy)\
                   .then_inc(hi_ready, 1)

            def layer_norm(n, vec):
                for k in range(KD):
                    if n in (0, 2):
                        eng.wait_ge(z_ready[n], k + 1)
                    elif k == 0:
                        eng.wait_ge(zall[n], 1)
                    if k >= 2:
                        eng.wait_ge(sq_used[n], k - 1)
                    eng.activation(sq[:, k % 2, :], z[:, k, :], ACT.Square).then_inc(sq_ready[n], 1)
                eng.wait_ge(var_ready[n], 1)
                eng.activation(rstd[:, :], rstd[:, :], ACT.Sqrt).then_inc(std_ready[n], 1)
                for k in range(KD):
                    if k % 4 == 0:
                        eng.wait_ge(norm_q[n], k // 4 + 1)
                    g, b = (V_LNG + vec) * KD + k, (V_LNB + vec) * KD + k
                    eng.activation(xT[:, k, :], z[:, k, :], ACT.Identity, scale=prmT[:, g:g + 1],
                                   bias=prmT[:, b:b + 1]).then_inc(x_ready[n], 1)

            def moe(l):
                evacuate_x(1 + l, False, range(0, 4))
                eng.wait_ge(ex_in[l], 1)
                eng.activation(r4[1][:, :, :], r4[0][:, :, :], ACT.Exp).then_inc(ex_out[l], 1)
                eng.wait_ge(ex_in[l], 2)
                eng.activation(r1[3][:, :, :], r1[2][:, :, :], ACT.Exp).then_inc(ex_out[l], 1)
                evacuate_x(1 + l, False, range(4, 12))
                if l == 0:
                    eng.wait_ge(cstT_full, 1)
                    eng.activation(cstT[:, :], ps[:, 2, 0:128], ACT.Copy).then_inc(cstT_ready, 1)
                    eng.wait_ge(cstT_ready, 1)
                    dst = [O["lru_conv_prompt"][0, 0, k] for k in range(3)] + [O["lru_conv_sample"][0, 0, k] for k in range(3)]
                    dst += [O["lru_h_prompt"][0, 0], O["lru_h_sample"][0, 0]]
                    for j, o in enumerate(dst):
                        eng.dma_start(o.rearrange("(b p) -> b p", p=128), cstT[j:128:8, :]).then_inc(out_st, 16)
                eng.wait_ge(route_ready[l], 1)
                n_win = eng.value_load(route_i[0:1, l, 0:1], min_val=NG, max_val=NG + MORE)
                base = C_MOE0 if l == 0 else C_MOE1
                with eng.Fori(0, n_win) as w:
                    seq = w if l == 0 else w + act_extra[0]

                    parts0 = parts_base(l) + NPART

                    def high_part(i):
                        n, at = base + i // PARTS_CHUNK, i % PARTS_CHUNK
                        if at == 0:
                            eng.wait_ge(ring_ready[slot_of(n)], seq * 64 + ready_at(n))
                        eng.wait_ge(parts_used, seq * PARTS_WIN + (parts0 - NPART + i + 1))
                        eng.activation(whi[:, i % NPART, :], ring_at(n)[:, at * PART:(at + 1) * PART], ACT.Copy)\
                           .then_inc(hi_ready, 1)

                    for i in range(NPART):
                        high_part(i)
                    eng.wait_ge(aux_full[l], w * 26 + 1)
                    eng.activation(S[0:W, :], ps[0:W, 6, 0:T], ACT.Copy).then_inc(aux_act[l], 1)
                    eng.wait_ge(aux_full[l], w * 26 + 2)
                    eng.activation(gslot[0:W, :], ps[0:W, 7, 0:NE], ACT.Copy, scale=0.5).then_inc(aux_act[l], 1)
                    for q in range(4):
                        eng.wait_ge(aux_full[l], w * 26 + (3 + q))
                        eng.activation(xhi[:, 4 * q:4 * q + 4, :],
                                       ps[:, 6 + q % 2, 0:4 * W].rearrange("p (k w) -> p k w", k=4), ACT.Copy)\
                           .then_inc(xhi_ready[l], 1)
                    for i in range(NPART, PARTS_WIN):
                        if i in SILU_AT:
                            e = SILU_AT[i]
                            eng.wait_ge(parts_used, seq * PARTS_WIN + (parts0 + GU_END[e]))
                            eng.activation(th[0:W, :], ps[0:W, gate_bank(e), :], ACT.Tanh, scale=0.5)\
                               .then_inc(th_ready[l], 1)
                        if i in ACT_AT:
                            e = ACT_AT[i]
                            eng.wait_ge(aux_full[l], w * 26 + (7 + e))
                            eng.activation(acthi[:, e % 2, :], ps[:, 6 + e % 2, 0:KF * W], ACT.Copy)\
                               .then_inc(aux_act[l], 1)
                        high_part(i)
                    eng.wait_ge(parts_used, seq * PARTS_WIN + (parts0 + PARTS_WIN))
                    for b in range(2):
                        last = eng.activation(osb[0:W, b * 512:(b + 1) * 512], ps[0:W, 2 + b, :], ACT.Copy)
                    last.then_inc(o_act[l], 1)
                if l == 0:
                    act_extra.append(eng.snap(n_win - NG))

            act_extra = []
            layer_norm(0, 0)
            moe(0)
            layer_norm(1, 1)
            for q in range(4):
                eng.wait_ge(pst_full, q + 1)
                eng.activation(prow_out[:, q * 512:(q + 1) * 512], ps[0:PT, 4 + q, :], ACT.Copy)\
                   .then_inc(pst_copied, 1)
            eng.wait_ge(pst_copied, 4)
            eng.dma_start(O["pool_prompt"][0, 0], prow_out[0:PW, :]).then_inc(out_st, 16)
            eng.dma_start(O["pool_sample"][0, 0], prow_out[TS:PT, :]).then_inc(out_st, 16)
            layer_norm(2, 2)
            eng.wait_ge(out_st, 160)
            moe(1)
            layer_norm(3, 3)
            evacuate_x(3, False, range(12))
            eng.wait_ge(out_st, 160)

        @block.tensor
        def _(eng):
            mm = nc.tensor.matmul
            eng.wait_ge(consts, 7)
            def transpose_x(which, to_feature, part=range(12)):
                for n in part:
                    i, q = n // 4, n % 4
                    t0, m = TILES[i]
                    if to_feature and q == 0:
                        eng.wait_ge(x_in[i], 16)
                    if n >= 4 and which in (0, 3):
                        eng.wait_ge((tr_act if n % 2 == 0 else tr_dve)[which], (n - 4) // 2 + 1)
                    elif n >= 4:
                        eng.wait_ge(tr_act[which], n - 3)
                    for b in range(4):
                        k = 4 * q + b
                        if to_feature:
                            last = nc.tensor.transpose(ps[:, 4 + n % 4, b * 128:b * 128 + m],
                                                       xtok[0:m, i, k * 128:(k + 1) * 128], ident[0:m, 0:m])
                        else:
                            last = nc.tensor.transpose(ps[0:m, 4 + n % 4, b * 128:(b + 1) * 128],
                                                       xT[:, k, t0:t0 + m], ident[:, :])
                    last.then_inc(tr_full[which], 1)

            eng.wait_ge(wr_in, 64)
            for l in two:
                for j in range(20):
                    src = wrow[l][0][:, :, j] if j < 4 else wrow[l][1][:, :, j - 4]
                    last = nc.tensor.transpose(ps[:, 1 + l, j * 16:(j + 1) * 16], src, ident[0:16, 0:16])
                last.then_inc(init_tr, 1)
            eng.wait_ge(pst_in, 32)
            for a in range(2):
                last = nc.tensor.transpose(ps[:, 3, a * 120:(a + 1) * 120], pstrow[:, a, :], ident[0:120, 0:120])
            last.then_inc(init_tr, 1)
            eng.wait_ge(prm_in, 160)
            for q in range(3):
                r = 128 if q < 2 else 80
                last = nc.tensor.transpose(ps[:, 0, q * 128:q * 128 + r], prow[0:r, q, :], ident[0:r, 0:r])
            last.then_inc(init_tr, 1)

            transpose_x(0, True)

            eng.wait_ge(tr_act[0], 6)
            eng.wait_ge(tr_dve[0], 6)
            eng.wait_ge(init_cp, 4)
            with eng.Fori(0, HEADS // 2) as it:
                for hh in range(2):
                    for j in range(2):
                        n = 3 * hh + j
                        eng.wait_ge(ring_ready[slot_of(n)], it * (16 * dmas_of(n)) + ready_at(n))
                        if j == 1:
                            eng.wait_ge(gelu_done, it * 2 + (hh + 1))
                        wv = ring_at(n).rearrange("p (k c) -> p k c", c=256)
                        for b in range(2):
                            if j == 0:
                                eng.wait_ge(u_copied, it * 4 + (2 * hh + b + 1))
                            for k in range(KD):
                                last = mm(ps[:, 2 * j + b, 0:T], wv[:, k, b * 128:(b + 1) * 128], xT[:, k, :],
                                          start=(k == 0), stop=(k == KD - 1))
                        last.then_inc(chunks_done, 1)
                    n = 3 * hh + 2
                    eng.wait_ge(ring_ready[slot_of(n)], it * (16 * dmas_of(n)) + ready_at(n))
                    eng.wait_ge(uc_ready, it * 2 + (hh + 1))
                    eng.wait_ge(ri_read, it * 2 + (hh + 1))
                    wv = ring_at(n)[:, 0:1024].rearrange("p (a k j) -> p a k j", a=2, k=2)
                    for a in range(2):
                        for b in range(2):
                            for k in range(2):
                                last = mm(ps[:, 4 + 2 * a + b, 0:TG], wv[:, a, k, b * 128:(b + 1) * 128], UC[:, k, :],
                                          start=(k == 0), stop=(k == 1))
                    last.then_inc(chunks_done, 1)
            for i in range(N_OUT):
                if i >= 3:
                    eng.wait_ge(z_ready[0], 2 * (i - 2))
                for q in range(PARTS_CHUNK):
                    part = i * PARTS_CHUNK + q
                    if i == 0:
                        eng.wait_ge(ylo_ready, 2 * q + 2)
                    eng.wait_ge(lo_ready, CREDIT + part + 1)
                    for k in (2 * q, 2 * q + 1):
                        for b in range(2):
                            at = (k % 2) * 256 + b * 128
                            hi, lo = (a[:, part % NPART, at:at + 128] for a in (whi, wlo))
                            o = ps[:, (2 * i + b) % 6, 0:T]
                            mm(o, hi, yhi[:, k, :], start=(k == 0), stop=False)
                            mm(o, hi, ylo[:, k, :], start=False, stop=False)
                            last = mm(o, lo, yhi[:, k, :], start=False, stop=(k == KD - 1))
                    last.then_inc(parts_used, 1)

            def layer_norm(n):
                for k in range(KD):
                    eng.wait_ge(sq_ready[n], k + 1)
                    mm(ps[:, 6, 0:T], onesd[:, :], sq[:, k % 2, :], start=(k == 0), stop=(k == KD - 1))\
                        .then_inc(sq_used[n], 1)
                eng.wait_ge(zsum_ready[n], 1)
                mm(ps[:, 7, 0:T], onesd[:, :], zsum[:, :], start=True, stop=True).then_inc(stat_done[n], 1)

            def moe(l):
                if l == 0:
                    eng.wait_ge(brow_in, 64)
                for i, (t0, m) in enumerate(TILES):
                    o = ps[0:m, 0, i * 32:i * 32 + 20]
                    mm(o, ones[0:1, 0:m], brow[0:1, l, :], start=True, stop=False)
                    for k in range(KD):
                        if i == 0:
                            eng.wait_ge(x_ready[2 * l], k + 1)
                        last = mm(o, xT[:, k, t0:t0 + m], wrT[:, l, :, k], start=False, stop=(k == KD - 1))
                last.then_inc(lg_done[l], 1)
                transpose_x(1 + l, False, range(4))
                eng.wait_ge(oh_ready[l], 1)
                for i in range(3):
                    for j in range(i + 1):
                        mm(ps[:, 1, i * 4:i * 4 + 4], (before if j == i else ones)[:, :], Gh[:, j, :],
                           start=(j == 0), stop=(j == i))
                for j in range(3):
                    last = mm(ps[:, 1, 16:20], ones[:, :], Gh[:, j, :], start=(j == 0), stop=(j == 2))
                last.then_inc(cnt_done[l], 1)
                transpose_x(1 + l, False, range(4, 12))
                if l == 0:
                    eng.wait_ge(cst_done, 1)
                    nc.tensor.transpose(ps[:, 2, 0:128], cst[:, :, :].rearrange("p b j -> p (b j)"), ident[:, :])\
                        .then_inc(cstT_full, 1)

                base = C_MOE0 if l == 0 else C_MOE1
                eng.wait_ge(tr_act[1 + l], 12)
                eng.wait_ge(route_ready[l], 1)
                n_win = eng.value_load(route_i[0:1, l, 0:1], min_val=NG, max_val=NG + MORE)
                with eng.Fori(0, n_win) as w:
                    seq = w if l == 0 else w + pe_extra[0]

                    def transpose_act(e):
                        eng.wait_ge(gated[l], w * 4 + (e + 2))
                        if e < 2:
                            eng.wait_ge(aux_dve[l], w * 20 + (5 + e))
                        else:
                            eng.wait_ge(actlo_ready[l], w * 4 + (e - 1))
                        for f in range(KF):
                            last = nc.tensor.transpose(ps[:, 6 + e % 2, f * W:(f + 1) * W],
                                                       th[0:W, f * 128:(f + 1) * 128], ident[0:W, 0:W])
                        last.then_inc(aux_full[l], 1)

                    eng.wait_ge(P_ready[l], w + 1)
                    eng.wait_ge(aux_dve[l], w * 20 + 1)
                    for i, (t0, m) in enumerate(TILES):
                        last = nc.tensor.transpose(ps[0:W, 6, t0:t0 + m], P[0:m, i, :], ident[0:m, 0:m])
                    last.then_inc(aux_full[l], 1)
                    eng.wait_ge(aux_dve[l], w * 20 + 2)
                    for i in range(3):
                        last = mm(ps[0:W, 7, 0:NE], P[:, i, :], gate4[:, i, :], start=(i == 0), stop=(i == 2))
                    last.then_inc(aux_full[l], 1)
                    for q in range(4):
                        if q < 2:
                            eng.wait_ge(aux_act[l], w * 6 + (1 + q))
                        else:
                            eng.wait_ge(aux_dve[l], w * 20 + (1 + q))
                        for b in range(4):
                            k = 4 * q + b
                            for i in range(3):
                                last = mm(ps[:, 6 + q % 2, b * W:(b + 1) * W], xtok[:, i, k * 128:(k + 1) * 128],
                                          P[:, i, :], start=(i == 0), stop=(i == 2))
                        last.then_inc(aux_full[l], 1)
                    for i, (kind, e, q) in enumerate(WINDOW_PARTS):
                        if i in TRANSPOSE_AT:
                            transpose_act(TRANSPOSE_AT[i])
                        if kind == "gu":
                            k, half = q // 2, q % 2
                            o = ps[0:W, gate_bank(e) + half, :]
                            hi, lo = xhi[:, k, :], xlo[:, k, :]
                            start, stop = k == 0, k == KD - 1
                            if e == 0 and q == 0:
                                eng.wait_ge(o_act[l], w + 1)
                                eng.wait_ge(o_dve[l], w + 1)
                            elif q == 0:
                                eng.wait_ge(gated[l], w * 4 + (1 if e == 1 else e + 1))
                            if e == 0 and q % 8 == 0:
                                eng.wait_ge(aux_dve[l], w * 20 + (3 + q // 8))
                        else:
                            f, j = q // 4, q % 4
                            o = ps[0:W, 2 + j, :]
                            hi, lo = (a[:, e % 2, f * W:(f + 1) * W] for a in (acthi, actlo))
                            start, stop = e == 0 and f == 0, e == NE - 1 and f == KF - 1
                            if q == 0:
                                eng.wait_ge(actlo_ready[l], w * 4 + (e + 1))
                        eng.wait_ge(lo_ready, seq * PARTS_WIN + (parts_base(l) + CREDIT + i + 1))
                        mm(o, hi, whi[:, i % NPART, :], start=start, stop=False)
                        mm(o, lo, whi[:, i % NPART, :], start=False, stop=False)
                        mm(o, hi, wlo[:, i % NPART, :], start=False, stop=stop).then_inc(parts_used, 1)
                    eng.wait_ge(o_act[l], w + 2)
                    eng.wait_ge(o_dve[l], w + 2)
                    for j in range(KD):
                        if j < 2:
                            eng.wait_ge(actlo_ready[l], w * 4 + (3 + j))
                        else:
                            eng.wait_ge(aux_dve[l], w * 20 + (5 + j))
                        mm(ps[:, 6 + j % 2, 0:T], osb[0:W, j * 128:(j + 1) * 128], S[0:W, :], start=True, stop=True)\
                            .then_inc(aux_full[l], 1)
                if l == 0:
                    pe_extra.append(eng.snap(n_win - NG))

            pe_extra = []
            layer_norm(0)
            moe(0)
            layer_norm(1)
            eng.wait_ge(x_ready[1], KD)
            for q in range(4):
                for b in range(4):
                    last = nc.tensor.transpose(ps[0:PT, 4 + q, b * 128:(b + 1) * 128], xT[:, 4 * q + b, T - PT:T],
                                               ident[:, :])
                last.then_inc(pst_full, 1)
            for g in range(NG):
                n = C_POOL + g
                eng.wait_ge(pool_diff, g + 1)
                eng.wait_ge(ring_ready[slot_of(n)], pe_extra[0] * 64 + ready_at(n))
                wv = ring_at(n)[:, 0:2048].rearrange("p (k j) -> p k j", k=4)
                if g >= 1:
                    eng.wait_ge(z_ready[2], 4 * g)
                for b in range(4):
                    for k in range(4):
                        last = mm(ps[:, b, 0:T], wv[:, k, b * 128:(b + 1) * 128], pdiff[g % 2][:, k, :],
                                  start=(k == 0), stop=(k == 3))
                last.then_inc(chunks_done, 1)
            eng.wait_ge(pst_copied, 4)
            layer_norm(2)
            moe(1)
            layer_norm(3)
            eng.wait_ge(x_ready[3], KD)
            transpose_x(3, False)

        @block.vector
        def _(eng):
            V = nc.vector
            link = SelfOrder(eng, vself)
            TS_, TT_, STT = V.tensor_scalar, V.tensor_tensor, V.scalar_tensor_tensor

            def evacuate_x(which, to_feature, part=range(12)):
                for n in part:
                    if n % 2 == 0:
                        continue
                    i, q = n // 4, n % 4
                    t0, m = TILES[i]
                    eng.wait_ge(tr_full[which], n + 1)
                    if to_feature:
                        o = xT[:, 4 * q:4 * q + 4, t0:t0 + m]
                        s = ps[:, 4 + n % 4, :].rearrange("p (k c) -> p k c", k=4)[:, :, 0:m]
                    else:
                        o = xtok[0:m, i, q * 512:(q + 1) * 512]
                        s = ps[0:m, 4 + n % 4, :]
                    V.tensor_copy(o, s).then_inc(tr_dve[which], 1)

            marks = []

            def signal(s, n=1):
                marks.append(0)
                c = len(marks)
                V.memset(mark[0:1, c:c + 1], 0.0).then_inc(s, n)

            V.memset(tiny[:, :], 1e-30)
            V.memset(uext[:, :, :], 0.0)
            V.memset(valid[:, 0:2, :], 1.0)
            link(V.memset(valid[:, 2, :], 0.0))
            link(V.memset(valid[0:32, 2, :], 1.0))
            eng.wait_ge(consts, 7)
            link(V.tensor_copy(iota_f[:, :], iota_i[:, :]))
            V.tensor_copy(gidx[:, :], iota_f[:, 0:4])
            TS_(firstw[:, :], iota_f[:, 0:4], -1.0, 4.0, ALU.mult, ALU.add)
            link(TS_(rcount[:, :], iota_f[:, 0:16], 1.0, None, ALU.add))
            link(V.reciprocal(rcount[:, :], rcount[:, :]))
            signal(uext_free, 1)
            signal(gelu_done, 1)
            signal(head_done, 1)
            for l in two:
                signal(aux_dve[l], 2)
                signal(gated[l], 1)
                signal(o_act[l], 1)
                signal(o_dve[l], 1)
            signal(lo_ready, CREDIT)
            signal(parts_used, NPART)
            eng.wait_ge(init_cp, 4)
            lam = prmT[:, V_LAM * KD:(V_LAM + 1) * KD]
            STT(sp[0][:, :], lam, -1.0, lam, ALU.mult, ALU.max).then_inc(derived, 1)
            TS_(half_ba[:, :], prmT[:, V_BA * KD:(V_BA + 1) * KD], 0.5, None, ALU.mult)
            TS_(half_bx[:, :], prmT[:, V_BX * KD:(V_BX + 1) * KD], 0.5, None, ALU.mult)
            evacuate_x(0, True)
            eng.wait_ge(lam_exp, 1)
            link(TS_(sp[2][:, :], sp[1][:, :], 2.0, None, ALU.add))
            link(V.reciprocal(sp[2][:, :], sp[2][:, :]))
            link(TT_(sp[1][:, :], sp[1][:, :], sp[2][:, :], ALU.mult))
            link(TT_(sp[2][:, :], sp[1][:, :], sp[1][:, :], ALU.mult))
            link(TS_(sp[3][:, :], sp[2][:, :], 1.0 / 15, None, ALU.mult))
            for q in (13, 11, 9, 7, 5, 3):
                link(STT(sp[3][:, :], sp[3][:, :], 1.0 / q, sp[2][:, :], ALU.add, ALU.mult))
            link(STT(sp[3][:, :], sp[3][:, :], 1.0, sp[1][:, :], ALU.add, ALU.mult))
            link(TS_(sp[2][:, :], lam, -1.0, 0.0, ALU.mult, ALU.max))
            link(STT(sp[3][:, :], sp[3][:, :], 2.0, sp[2][:, :], ALU.mult, ALU.add))
            TS_(c_lam[:, :], sp[3][:, :], -4.0, None, ALU.mult).then_inc(derived, 1)
            eng.wait_ge(derived, 2)

            with eng.Fori(0, HEADS // 2) as it:
                lk = SelfOrder(eng, vlru)
                lk.start(it, LRU_LINKS)
                for hh in range(2):
                    h = it * 2 + hh

                    def prm(v, b):
                        return prmT[:, bass.ds(h * 2 + (b + v * KD), 1)]
                    eng.wait_ge(u_copied, it * 4 + (2 * hh + 4))
                    pre = prmT[:, V_CONV0 * KD:(V_CONV0 + 3) * KD].rearrange("p (w k) -> p k w", w=3)
                    lk(V.tensor_copy(uext[:, :, TP + CW - 1:TP + 2 * (CW - 1)], pre[:, bass.ds(h * 2, 2), :]))
                    for b in range(2):
                        lk(TS_(UC[:, b, :], uext[:, b, 0:TG], prm(V_CW, b), prm(V_CB, b), ALU.mult, ALU.add))
                        for k in range(1, CW):
                            i = STT(UC[:, b, :], uext[:, b, k:k + TG], prm(V_CW + k, b), UC[:, b, :], ALU.mult, ALU.add)
                            if k == CW - 1 and b == 1:
                                i.then_inc(uc_ready, 1)
                            else:
                                lk(i)
                    eng.wait_ge(uc_ready, it * 2 + (hh + 1))
                    V.tensor_copy(cst[:, bass.ds(h * 2, 2), 0:3], uext[:, :, TP:TP + 3])
                    V.tensor_copy(cst[:, bass.ds(h * 2, 2), 3:6], uext[:, :, UX - 3:UX]).then_inc(uext_free, 1)
                    eng.wait_ge(gsq_ready, it * 2 + (hh + 1))
                    lk(TS_(GS[:, :, 0:T], GS[:, :, 0:T], 0.044715, 1.0, ALU.mult, ALU.add))
                    TT_(GS[:, :, 0:T], GS[:, :, 0:T], ps[:, 2:4, 0:T], ALU.mult).then_inc(gin_ready, 1)
                    eng.wait_ge(gtanh_ready, it * 2 + (hh + 1))
                    STT(GG[:, :, 0:T], GG[:, :, 0:T], 1.0, ps[:, 2:4, 0:T], ALU.add, ALU.mult).then_inc(gelu_done, 1)
                    eng.wait_ge(decay_ready, it * 2 + (hh + 1))
                    lk(TT_(GS[:, :, :], AA[:, :, :], AA[:, :, :], ALU.mult))
                    STT(TL[:, :, :], GS[:, :, :], 1.0, TL[:, :, :], ALU.add, ALU.mult).then_inc(q_ready, 1)
                    lk(STT(TX[:, :, :], TX[:, :, :], 1.0, UC[:, :, :], ALU.add, ALU.mult))
                    eng.wait_ge(mult_ready, it * 2 + (hh + 1))
                    lk(STT(TX[:, :, :], TX[:, :, :], 0.5, TL[:, :, :], ALU.mult, ALU.mult))
                    V.memset(AA[:, :, SEAM:SEAM + 1], 0.0)
                    lk(V.tensor_copy(TX[:, :, SEAM:SEAM + 1],
                                     prmT[:, bass.ds(h * 2 + V_H0 * KD, 2)].rearrange("p (b o) -> p b o", o=1)))
                    for b in range(2):
                        i = V.tensor_tensor_scan(TR[:, b, :], AA[:, b, :], TX[:, b, :], 0.0, ALU.mult, ALU.add)
                    lk(i)
                    V.tensor_copy(cst[:, bass.ds(h * 2, 2), 6:7], TR[:, :, TP - 1:TP])
                    V.tensor_copy(cst[:, bass.ds(h * 2, 2), 7:8], TR[:, :, TG - 1:TG])
                    STT(yT[:, bass.ds(h * 2, 2), 0:TP], GG[:, :, 0:TP], 0.5, TR[:, :, 0:TP], ALU.mult, ALU.mult)
                    STT(yT[:, bass.ds(h * 2, 2), TP:T], GG[:, :, TP:T], 0.5, TR[:, :, TG - TS:TG], ALU.mult, ALU.mult)\
                        .then_inc(head_done, 1)
                lk.check()
            signal(cst_done, 1)
            def out_add(i):
                eng.wait_ge(parts_used, NPART + (i + 1) * PARTS_CHUNK)
                for b in range(2):
                    k = 2 * i + b
                    STT(z[:, k, :], xT[:, k, :], ALPHA, ps[:, k % 6, 0:T], ALU.mult, ALU.add).then_inc(z_ready[0], 1)

            for part in range(PARTS_OUT):
                n, at = C_OUT + part // PARTS_CHUNK, part % PARTS_CHUNK
                if part == NPART:
                    eng.wait_ge(head_done, HEADS + 1)
                    for k in range(KD):
                        eng.wait_ge(yhi_ready, k + 1)
                        TT_(ylo[:, k, :], yT[:, k, :], yhi[:, k, :].bitcast(F32), ALU.subtract).then_inc(ylo_ready, 1)
                if part >= PARTS_CHUNK + NPART and (part - NPART) % PARTS_CHUNK == 0:
                    out_add((part - NPART) // PARTS_CHUNK - 1)
                eng.wait_ge(hi_ready, part + 1)
                TT_(wlo[:, part % NPART, :], ring_at(n)[:, at * PART:(at + 1) * PART],
                    whi[:, part % NPART, :].bitcast(F32), ALU.subtract).then_inc(lo_ready, 1)
            out_add(N_OUT - 1)
            eng.wait_ge(z_ready[0], KD)
            eng.wait_ge(parts_used, NPART + PARTS_OUT)

            def layer_norm(n):
                V.tensor_reduce(zsum[:, :], z[:, :, :].rearrange("p k t -> p t k"), AX.X, ALU.add)\
                    .then_inc(zsum_ready[n], 1)
                eng.wait_ge(stat_done[n], 1)
                link(V.tensor_copy(mean[:, :], ps[:, 7, 0:T]))
                link(TT_(nmr[:, :], mean[:, :], mean[:, :], ALU.mult))
                link(STT(nmr[:, :], ps[:, 6, 0:T], EPS, nmr[:, :], ALU.add, ALU.subtract))
                TS_(rstd[:, :], nmr[:, :], EPS * 0.5, None, ALU.max).then_inc(var_ready[n], 1)
                eng.wait_ge(std_ready[n], 1)
                link(V.reciprocal(rstd[:, :], rstd[:, :]))
                link(STT(nmr[:, :], mean[:, :], -1.0, rstd[:, :], ALU.mult, ALU.mult))
                for q in range(4):
                    zq = z[:, 4 * q:4 * q + 4, :]
                    link(TT_(zq, zq, rstd[:, :].unsqueeze(1).to_broadcast([128, 4, T]), ALU.mult))
                    TT_(zq, zq, nmr[:, :].unsqueeze(1).to_broadcast([128, 4, T]), ALU.add).then_inc(norm_q[n], 1)

            def bc(v, n):
                return v.to_broadcast([128, 3, n])

            def first_max(out, v, m, tmp, tmp1):
                link(V.tensor_reduce(m[:, :, 0], v[:, :, :], AX.X, ALU.max))
                link(TT_(tmp[:, :, :], v[:, :, :], bc(m[:, :, :], 4), ALU.is_equal))
                fw = firstw[:, :].unsqueeze(1).to_broadcast([128, 3, 4])
                link(TT_(tmp[:, :, :], tmp[:, :, :], fw, ALU.mult))
                link(V.tensor_reduce(tmp1[:, :, 0], tmp[:, :, :], AX.X, ALU.max))
                link(TT_(out[:, :, :], tmp[:, :, :], bc(tmp1[:, :, :], 4), ALU.is_equal))

            def moe(l):
                link(V.memset(logit[:, :, :], 0.0))
                eng.wait_ge(lg_done[l], 1)
                V.tensor_copy(logit[:, 0:2, :], ps[:, 0, 0:64].rearrange("p (i j) -> p i j", i=2)[:, :, 0:20])
                link(V.tensor_copy(logit[0:32, 2, :], ps[0:32, 0, 64:84]))
                lg = logit[:, :, 0:4]
                link(V.tensor_reduce(r1[0][:, :, 0], lg, AX.X, ALU.max))
                TT_(r4[0][:, :, :], lg, bc(r1[0][:, :, :], 4), ALU.subtract).then_inc(ex_in[l], 1)
                link(TT_(r4[2][:, :, :], lg, bc(r1[0][:, :, :], 4), ALU.is_equal))
                fw = firstw[:, :].unsqueeze(1).to_broadcast([128, 3, 4])
                link(TT_(r4[2][:, :, :], r4[2][:, :, :], fw, ALU.mult))
                link(V.tensor_reduce(r1[1][:, :, 0], r4[2][:, :, :], AX.X, ALU.max))
                link(TT_(Gh[:, :, :], r4[2][:, :, :], bc(r1[1][:, :, :], 4), ALU.is_equal))
                TT_(Gh[:, :, :], Gh[:, :, :], bc(valid[:, :, :], 4), ALU.mult).then_inc(oh_ready[l], 1)
                eng.wait_ge(oh_ready[l], 1)
                for i in range(3):
                    o = lprod[:, i, :].rearrange("p (g j) -> p g j", g=4)
                    ins = TT_(o, logit[:, i, 4:20].rearrange("p (g j) -> p g j", g=4),
                              Gh[:, i, :].unsqueeze(2).to_broadcast([128, 4, 4]), ALU.mult)
                link(ins)
                link(V.tensor_reduce(les[:, :, :], lprod[:, :, :].rearrange("p i (g j) -> p i j g", g=4), AX.X, ALU.add))
                first_max(E1, les, r1[0], r4[2], r1[1])
                link(STT(les[:, :, :], E1[:, :, :], -1e30, les[:, :, :], ALU.mult, ALU.add))
                first_max(gate4, les, r1[4], r4[2], r1[1])
                TT_(r1[2][:, :, :], r1[4][:, :, :], r1[0][:, :, :], ALU.subtract).then_inc(ex_in[l], 1)
                eng.wait_ge(ex_out[l], 1)
                link(V.tensor_reduce(r1[5][:, :, 0], r4[1][:, :, :], AX.X, ALU.add))
                eng.wait_ge(ex_out[l], 2)
                link(STT(r1[6][:, :, :], r1[3][:, :, :], 1.0, r1[5][:, :, :], ALU.add, ALU.mult))
                link(V.reciprocal(r1[6][:, :, :], r1[6][:, :, :]))
                link(TT_(r1[7][:, :, :], r1[6][:, :, :], r1[3][:, :, :], ALU.mult))
                link(TT_(gate4[:, :, :], gate4[:, :, :], bc(r1[7][:, :, :], 4), ALU.mult))
                link(TT_(E1[:, :, :], E1[:, :, :], bc(r1[6][:, :, :], 4), ALU.mult))
                link(TT_(gate4[:, :, :], gate4[:, :, :], E1[:, :, :], ALU.add))
                eng.wait_ge(cnt_done[l], 1)
                link(V.tensor_copy(n_g[:, :], ps[:, 1, 16:20]))
                link(TT_(r4[2][:, :, :], Gh[:, :, :], ps[:, 1, 0:12].rearrange("p (i g) -> p i g", i=3), ALU.mult))
                pos, k_w, first, tmp = r1[0], r1[1], r1[2], r1[4]
                link(V.tensor_reduce(pos[:, :, 0], r4[2][:, :, :], AX.X, ALU.add))
                link(TS_(k_w[:, :, :], pos[:, :, :], float(W), None, ALU.is_ge))
                link(TS_(more[:, :], n_g[:, :], float(W), None, ALU.is_gt))
                for m in range(2, -(-T // W)):
                    link(STT(k_w[:, :, :], pos[:, :, :], float(m * W), k_w[:, :, :], ALU.is_ge, ALU.add))
                    link(STT(more[:, :], n_g[:, :], float(m * W), more[:, :], ALU.is_gt, ALU.add))
                link(STT(pos[:, :, :], k_w[:, :, :], -float(W), pos[:, :, :], ALU.mult, ALU.add))
                link(V.memset(mbase[:, :], 0.0))
                for g in range(1, NG):
                    link(TT_(mbase[:, g:g + 1], mbase[:, g - 1:g], more[:, g - 1:g], ALU.add))
                g_w, m_w = r4[0], r4[3]
                link(TT_(g_w[:, :, :], Gh[:, :, :], gidx[:, :].unsqueeze(1).to_broadcast([128, 3, 4]), ALU.mult))
                link(TT_(m_w[:, :, :], Gh[:, :, :], mbase[:, :].unsqueeze(1).to_broadcast([128, 3, 4]), ALU.mult))
                link(V.tensor_reduce(first[:, :, 0], g_w[:, :, :], AX.X, ALU.add))
                link(V.tensor_reduce(tmp[:, :, 0], m_w[:, :, :], AX.X, ALU.add))
                link(STT(tmp[:, :, :], tmp[:, :, :], 3.0, k_w[:, :, :], ALU.add, ALU.add))
                link(TT_(tmp[:, :, :], tmp[:, :, :], first[:, :, :], ALU.subtract))
                link(TS_(k_w[:, :, :], k_w[:, :, :], 0.0, None, ALU.is_gt))
                link(TT_(tmp[:, :, :], tmp[:, :, :], k_w[:, :, :], ALU.mult))
                link(TT_(tmp[:, :, :], tmp[:, :, :], first[:, :, :], ALU.add))
                link(STT(slotno[:, :, :], tmp[:, :, :], float(W), pos[:, :, :], ALU.mult, ALU.add))
                link(STT(slotno[:, :, :], slotno[:, :, :], 1.0, valid[:, :, :], ALU.add, ALU.mult))
                link(TS_(slotno[:, :, :], slotno[:, :, :], -1.0, None, ALU.add))
                link(V.memset(route_f[:, :], 0.0))
                link(V.tensor_reduce(route_f[:, 0:1], more[:, :], AX.X, ALU.add))
                link(TS_(route_f[:, 0:1], route_f[:, 0:1], float(NG), None, ALU.add))
                link(TT_(more[:, :], more[:, :], mbase[:, :], ALU.add))
                for x in range(MORE):
                    link(TS_(t4[:, :], mbase[:, :], float(x), None, ALU.is_le))
                    link(TT_(t4[:, :], t4[:, :], gidx[:, :], ALU.mult))
                    link(STT(t4[:, :], more[:, :], float(x), t4[:, :], ALU.is_gt, ALU.mult))
                    link(V.tensor_reduce(route_f[:, 1 + x:2 + x], t4[:, :], AX.X, ALU.add))
                V.tensor_copy(route_i[0:1, l, :], route_f[0:1, :]).then_inc(route_ready[l], 1)
                def one_hot():
                    for i in range(3):
                        ins = TS_(P[:, i, :], iota_f[:, 0:W], slotno[:, i, :], None, ALU.is_equal)
                    return ins.then_inc(P_ready[l], 1)

                one_hot()
                eng.wait_ge(ax_ready[l], KD)
                eng.wait_ge(route_ready[l], 1)
                n_win = eng.value_load(route_i[0:1, l, 0:1], min_val=NG, max_val=NG + MORE)
                base = C_MOE0 if l == 0 else C_MOE1
                with eng.Fori(0, n_win) as w:
                    seq = w if l == 0 else w + dve_extra[0]
                    lk = SelfOrder(eng, vmoe[l])
                    lk.start(w, MOE_LINKS)

                    def low_part(i):
                        n, at = base + i // PARTS_CHUNK, i % PARTS_CHUNK
                        eng.wait_ge(hi_ready, seq * PARTS_WIN + (parts_base(l) + i + 1))
                        TT_(wlo[:, i % NPART, :], ring_at(n)[:, at * PART:(at + 1) * PART],
                            whi[:, i % NPART, :].bitcast(F32), ALU.subtract).then_inc(lo_ready, 1)

                    for i in range(NPART):
                        low_part(i)
                    for q in range(4):
                        eng.wait_ge(xhi_ready[l], w * 4 + (q + 1))
                        TT_(xlo[:, 4 * q:4 * q + 4, :], ps[:, 6 + q % 2, 0:4 * W].rearrange("p (k w) -> p k w", k=4),
                            xhi[:, 4 * q:4 * q + 4, :].bitcast(F32), ALU.subtract).then_inc(aux_dve[l], 1)
                    for i in range(NPART, PARTS_WIN):
                        if i in SILU_AT:
                            e = SILU_AT[i]
                            hg, hv = ps[0:W, gate_bank(e), :], ps[0:W, gate_bank(e) + 1, :]
                            eng.wait_ge(th_ready[l], w * 4 + (e + 1))
                            lk(STT(th[0:W, :], th[0:W, :], 1.0, hg, ALU.add, ALU.mult))
                            if e == 0:
                                eng.wait_ge(aux_act[l], w * 6 + 2)
                            STT(th[0:W, :], th[0:W, :], gslot[0:W, e:e + 1], hv, ALU.mult, ALU.mult)\
                                .then_inc(gated[l], 1)
                        if i in ACT_AT:
                            e = ACT_AT[i]
                            eng.wait_ge(aux_act[l], w * 6 + (3 + e))
                            TT_(actlo[:, e % 2, :], ps[:, 6 + e % 2, 0:KF * W], acthi[:, e % 2, :].bitcast(F32),
                                ALU.subtract).then_inc(actlo_ready[l], 1)
                        low_part(i)
                    lk(TS_(slotno[:, :, :], slotno[:, :, :], -float(W), None, ALU.add))
                    one_hot()
                    eng.wait_ge(P_ready[l], w + 2)
                    eng.wait_ge(parts_used, seq * PARTS_WIN + (parts_base(l) + NPART + PARTS_WIN))
                    for b in range(2, 4):
                        ins = V.tensor_copy(osb[0:W, b * 512:(b + 1) * 512], ps[0:W, 2 + b, :])
                    ins.then_inc(o_dve[l], 1)
                    for j in range(KD):
                        eng.wait_ge(aux_full[l], w * 26 + (11 + j))
                        TT_(z[:, j, :], z[:, j, :], ps[:, 6 + j % 2, 0:T], ALU.add).then_inc(aux_dve[l], 1)
                    lk.check()
                signal(zall[1 + 2 * l], 1)
                eng.wait_ge(zall[1 + 2 * l], 1)
                if l == 0:
                    dve_extra.append(eng.snap(n_win - NG))

            def pool_add(g):
                eng.wait_ge(pst_full, g + 1)
                link(TS_(z[:, 4 * g:4 * g + 4, :], xT[:, 4 * g:4 * g + 4, :], ALPHA, None, ALU.mult))
                eng.wait_ge(chunks_done, C_OUT + g + 1)
                for b in range(4):
                    k = 4 * g + b
                    c = V_SCALE * KD + k
                    STT(z[:, k, :], ps[:, b, 0:T], prmT[:, c:c + 1], z[:, k, :], ALU.mult, ALU.add)\
                        .then_inc(z_ready[2], 1)

            dve_extra = []
            layer_norm(0)
            link(V.memset(xtok[:, 2, :], 0.0))
            moe(0)
            layer_norm(1)

            eng.wait_ge(x_ready[1], KD)
            Ls = PW + TP
            for g in range(NG):
                win = 2 << g
                blk = slice(4 * g, 4 * g + 4)
                V.memset(pext[:, :, 0:PW], 0.0)
                V.tensor_copy(pext[:, :, PW:Ls], xT[:, blk, 0:TP])
                V.tensor_copy(pext[:, :, Ls:Ls + PW], poolpre[:, :, blk].rearrange("p r k -> p k r"))
                link(V.tensor_copy(pext[:, :, Ls + PW:PX], xT[:, blk, TP:T]))
                src = pext
                for j in range(g + 1):
                    step = 1 << j
                    lo = 2 * step - 1
                    dst = (pa, pb)[j % 2]
                    link(TT_(dst[:, :, lo:PX], src[:, :, lo:PX], src[:, :, lo - step:PX - step], ALU.add))
                    src = dst
                if g >= 2:
                    eng.wait_ge(z_ready[2], 4 * (g - 1))
                pd = pdiff[g % 2]
                STT(pd[:, :, 0:TP], src[:, :, PW:Ls], 1.0 / win, xT[:, blk, 0:TP], ALU.mult, ALU.subtract)
                link(STT(pd[:, :, TP:T], src[:, :, Ls + PW:PX], 1.0 / win, xT[:, blk, TP:T], ALU.mult, ALU.subtract))
                rc = rcount[:, 0:win - 1].unsqueeze(1).to_broadcast([128, 4, win - 1])
                link(TT_(src[:, :, PW:PW + win - 1], src[:, :, PW:PW + win - 1], rc, ALU.mult))
                TT_(pd[:, :, 0:win - 1], src[:, :, PW:PW + win - 1], xT[:, blk, 0:win - 1], ALU.subtract)\
                    .then_inc(pool_diff, 1)
                eng.wait_ge(pool_diff, g + 1)
                if g >= 1:
                    pool_add(g - 1)
            pool_add(NG - 1)
            eng.wait_ge(z_ready[2], KD)
            layer_norm(2)
            link(V.memset(xtok[:, 2, :], 0.0))
            moe(1)
            layer_norm(3)
            evacuate_x(3, False)


_INS = ["x_prompt", "x_sample", "state_lru_h", "state_lru_conv", "state_pool", "lru_w_in", "lru_conv_w", "lru_conv_b",
        "lru_w_a", "lru_b_a", "lru_w_x", "lru_b_x", "lru_lambda", "lru_w_out", "pool_w", "pool_scale", "ln_g", "ln_b",
        "moe_router_g_w", "moe_router_g_b", "moe_router_e_w", "moe_router_e_b", "moe_w_gate_up", "moe_w_down"]
_OUTS = [("y_prompt", (1, TP, D)), ("y_sample", (1, TS, D)), ("lru_h_prompt", (1, 1, D)),
         ("lru_conv_prompt", (1, 1, CW - 1, D)), ("pool_prompt", (1, 1, PW, D)), ("lru_h_sample", (1, 1, D)),
         ("lru_conv_sample", (1, 1, CW - 1, D)), ("pool_sample", (1, 1, PW, D))]


def kernel(**inputs):
    import concourse.bacc as bacc
    from concourse.bass_utils import run_bass_kernel_spmd as run

    nc = bacc.Bacc("TRN2", target_bir_lowering=False, num_devices=1)
    arrays = {f"in_{name}": np.ascontiguousarray(inputs[name]) for name in _INS}
    A = {name: nc.dram_tensor(f"in_{name}", arrays[f"in_{name}"].shape, F32, kind="ExternalInput").ap() for name in _INS}
    O = {name: nc.dram_tensor(f"out_{name}", shape, F32, kind="ExternalOutput").ap() for name, shape in _OUTS}
    encoder_step(nc, A, O)
    r = run(nc, [arrays], core_ids=[0])
    return tuple(r.results[0][f"out_{name}"] for name, _ in _OUTS)
```
